# Optimizing a Trainium2 kernel written in Bass

```python
import jax, jax.numpy as jnp
from jax import lax
import numpy as np

D_MODEL = 1024
BATCH = 1
SEQ = 512
DEPTH = 1
DEC_BATCH = 8
DEC_SEQ = 1
PAST_LEN = 2048
PAGE_SIZE = 128

HEAD_DIM = 64
MIX_WIDTH = D_MODEL
SGU_GROUPS = (MIX_WIDTH // 2) // HEAD_DIM
ATT_HEADS = (MIX_WIDTH // 2) // HEAD_DIM
SGU_WIDTH = SGU_GROUPS * HEAD_DIM
ATT_WIDTH = ATT_HEADS * HEAD_DIM
PROJ_COLS = 2 * SGU_WIDTH + 3 * ATT_WIDTH
CHUNK = 128
BLOCK = 128
DILATED_PATTERNS = ((128, 1), (512, 4), (2048, 16))
MAX_WINDOW = 2048
ROPE_THETA = 10000.0
N_EXPERT_GROUPS = 4
EXPERTS_PER_GROUP = 8
N_EXPERTS = N_EXPERT_GROUPS * EXPERTS_PER_GROUP
EXPERT_TOP_K = 2
D_EXPERT = 128
EPS = 1e-6

kernel_name = "hybrid_sgu_dilated_attn_hmoe_step"

def rmsnorm(x, g):
    xf = x.astype(jnp.float32)
    y = xf * lax.rsqrt(jnp.mean(xf * xf, axis=-1, keepdims=True) + EPS)
    return (y * g.astype(jnp.float32)).astype(x.dtype)

def rope(x, pos):
    half = HEAD_DIM // 2
    inv = ROPE_THETA ** (-jnp.arange(half, dtype=jnp.float32) * 2.0 / HEAD_DIM)
    ang = pos.astype(jnp.float32)[:, None] * inv[None, :]
    cos = jnp.cos(ang)[:, None, :]
    sin = jnp.sin(ang)[:, None, :]
    xf = x.astype(jnp.float32)
    x1, x2 = xf[..., :half], xf[..., half:]
    return jnp.concatenate([x1 * cos - x2 * sin, x2 * cos + x1 * sin], axis=-1).astype(x.dtype)

def project(h, w_in, pos):
    z = jnp.einsum('btd,dc->btc', h, w_in)
    B, T = z.shape[:2]
    cuts = [SGU_WIDTH, 2 * SGU_WIDTH, 2 * SGU_WIDTH + ATT_WIDTH, 2 * SGU_WIDTH + 2 * ATT_WIDTH]
    u, va, q, k, v = jnp.split(z, cuts, axis=-1)
    heads = lambda t: t.reshape(B, T, -1, HEAD_DIM)
    return heads(u), heads(va), rope(heads(q), pos), rope(heads(k), pos), heads(v)

def causal_spatial_weight(w_s):
    mask = jnp.tril(jnp.ones((CHUNK, CHUNK), dtype=bool))
    return jnp.where(mask[None], w_s, 0)

def sgu_prompt(u, va, g_v, w_s, b_s):
    B, S = u.shape[:2]
    vn = rmsnorm(va, g_v)
    vc = vn.reshape(B, S // CHUNK, CHUNK, SGU_GROUPS, HEAD_DIM)
    mix = jnp.einsum('gts,bcsgd->bctgd', causal_spatial_weight(w_s), vc) + b_s.T[:, :, None]
    return u * mix.reshape(u.shape)

def sgu_sample(u, va, g_v, w_s, b_s):
    T = u.shape[1]
    vn = rmsnorm(va, g_v)
    w = causal_spatial_weight(w_s)[:, :T, :T]
    mix = jnp.einsum('gts,bsgd->btgd', w, vn) + b_s[:, :T].T[None, :, :, None]
    return u * mix, vn

def dilated_attn_prompt(q, k, v, dilation, n_keys):
    B, S, H, Dh = q.shape
    span = dilation * BLOCK
    s_pad = -(-S // span) * span
    nb = s_pad // span

    def to_blocks(t):
        t = jnp.pad(t, ((0, 0), (0, s_pad - S), (0, 0), (0, 0)))
        return t.reshape(B, nb, BLOCK, dilation, H, Dh)

    def with_prev(t):
        prev = jnp.pad(t, ((0, 0), (1, 0), (0, 0), (0, 0), (0, 0), (0, 0)))[:, :-1]
        return jnp.concatenate([prev, t], axis=2)

    qb = to_blocks(q)
    kk = with_prev(to_blocks(k))
    vv = with_prev(to_blocks(v))
    s = jnp.einsum('bnqrhd,bnkrhd->bnrhqk', qb, kk,
                   preferred_element_type=jnp.float32) * (HEAD_DIM ** -0.5)
    qi = jnp.arange(BLOCK)[:, None]
    kj = jnp.arange(2 * BLOCK)[None, :]
    dist = BLOCK + qi - kj
    band = (dist >= 0) & (dist <= n_keys)
    exists = (jnp.arange(nb)[:, None, None] > 0) | (kj[None] >= BLOCK)
    mask = band[None] & exists
    s = jnp.where(mask[None, :, None, None], s, -jnp.inf)
    m = jnp.max(s, axis=-1, keepdims=True)
    e = jnp.exp(s - m)
    den = jnp.sum(e, axis=-1, keepdims=True)
    p = e / den
    lse = (m + jnp.log(den))[..., 0]
    o = jnp.einsum('bnrhqk,bnkrhd->bnqrhd', p.astype(v.dtype), vv)
    o = o.reshape(B, s_pad, H, Dh)[:, :S]
    lse = jnp.transpose(lse, (0, 1, 4, 2, 3)).reshape(B, s_pad, H)[:, :S]
    return o, lse

def dilated_attn_sample(q, k_all, v_all, buf_len, dilation, n_keys):
    T = q.shape[1]
    j = np.arange(n_keys + 1)
    idx = buf_len + np.arange(T)[:, None] - j[None, :] * dilation
    valid = jnp.asarray(idx >= 0)
    idx_c = jnp.asarray(np.maximum(idx, 0))
    kg = k_all[:, idx_c]
    vg = v_all[:, idx_c]
    s = jnp.einsum('bthd,btjhd->bhtj', q, kg,
                   preferred_element_type=jnp.float32) * (HEAD_DIM ** -0.5)
    s = jnp.where(valid[None, None], s, -jnp.inf)
    m = jnp.max(s, axis=-1, keepdims=True)
    e = jnp.exp(s - m)
    den = jnp.sum(e, axis=-1, keepdims=True)
    p = e / den
    lse = jnp.transpose((m + jnp.log(den))[..., 0], (0, 2, 1))
    o = jnp.einsum('bhtj,btjhd->bthd', p.astype(v_all.dtype), vg)
    return o, lse

def merge_by_denominator(outs, lses):
    w = jax.nn.softmax(jnp.stack(lses), axis=0)
    o = jnp.einsum('pbth,pbthd->bthd', w, jnp.stack(outs).astype(jnp.float32))
    return o.astype(outs[0].dtype)

def mix_out(a_out, b_out, w_out):
    B, T = a_out.shape[:2]
    cat = jnp.concatenate([a_out.reshape(B, T, -1), b_out.reshape(B, T, -1)], axis=-1)
    return jnp.einsum('btc,cd->btd', cat, w_out)

def hier_moe(h, w_rg, b_rg, w_re, b_re, w_gate, w_up, w_down):
    N = h.shape[0]
    hf = h.astype(jnp.float32)
    pg = jax.nn.softmax(hf @ w_rg.astype(jnp.float32) + b_rg.astype(jnp.float32), axis=-1)
    gi = jnp.argmax(pg, axis=-1)
    gp = jnp.take_along_axis(pg, gi[:, None], axis=-1)[:, 0]
    le = (hf @ w_re.astype(jnp.float32) + b_re.astype(jnp.float32)).reshape(N, N_EXPERT_GROUPS, EXPERTS_PER_GROUP)
    le_sel = jnp.take_along_axis(le, gi[:, None, None], axis=1)[:, 0]
    pe = jax.nn.softmax(le_sel, axis=-1)
    top_p, top_i = lax.top_k(pe, EXPERT_TOP_K)
    top_p = top_p / jnp.sum(top_p, axis=-1, keepdims=True)
    within = jnp.einsum('nk,nke->ne', top_p, jax.nn.one_hot(top_i, EXPERTS_PER_GROUP, dtype=jnp.float32))
    gates = (gp[:, None, None] * jax.nn.one_hot(gi, N_EXPERT_GROUPS, dtype=jnp.float32)[:, :, None]
             * within[:, None, :]).reshape(N, N_EXPERTS)
    a = jnp.einsum('nd,edf->nef', h, w_gate)
    b = jnp.einsum('nd,edf->nef', h, w_up)
    hid = jax.nn.silu(a) * b * gates[:, :, None].astype(h.dtype)
    return jnp.einsum('nef,efd->nd', hid, w_down)

def setup_inputs(seed: int = 0) -> dict:
    key = jax.random.key(seed)
    ks = jax.random.split(key, 20)
    f32 = jnp.float32
    nrm = lambda k, shape, scale: jax.random.normal(k, shape, f32) * scale
    buf = min(MAX_WINDOW, PAST_LEN)
    return {
        "x_prompt": nrm(ks[0], (BATCH, SEQ, D_MODEL), 1.0),
        "x_sample": nrm(ks[1], (DEC_BATCH, DEC_SEQ, D_MODEL), 1.0),
        "cache_win_k": nrm(ks[2], (DEPTH, DEC_BATCH, buf, ATT_HEADS, HEAD_DIM), 1.0),
        "cache_win_v": nrm(ks[3], (DEPTH, DEC_BATCH, buf, ATT_HEADS, HEAD_DIM), 1.0),
        "ln1_g": 1.0 + nrm(ks[4], (DEPTH, D_MODEL), 0.02),
        "w_in": nrm(ks[5], (DEPTH, D_MODEL, PROJ_COLS), D_MODEL ** -0.5),
        "sgu_norm_g": 1.0 + nrm(ks[6], (DEPTH, SGU_GROUPS, HEAD_DIM), 0.02),
        "sgu_w": nrm(ks[7], (DEPTH, SGU_GROUPS, CHUNK, CHUNK), CHUNK ** -0.5),
        "sgu_b": 1.0 + nrm(ks[8], (DEPTH, SGU_GROUPS, CHUNK), 0.02),
        "w_out": nrm(ks[9], (DEPTH, MIX_WIDTH, D_MODEL), MIX_WIDTH ** -0.5),
        "ln2_g": 1.0 + nrm(ks[10], (DEPTH, D_MODEL), 0.02),
        "w_router_group": nrm(ks[11], (DEPTH, D_MODEL, N_EXPERT_GROUPS), D_MODEL ** -0.5),
        "b_router_group": nrm(ks[12], (DEPTH, N_EXPERT_GROUPS), 0.01),
        "w_router_expert": nrm(ks[13], (DEPTH, D_MODEL, N_EXPERTS), D_MODEL ** -0.5),
        "b_router_expert": nrm(ks[14], (DEPTH, N_EXPERTS), 0.01),
        "w_gate": nrm(ks[15], (DEPTH, N_EXPERTS, D_MODEL, D_EXPERT), D_MODEL ** -0.5),
        "w_up": nrm(ks[16], (DEPTH, N_EXPERTS, D_MODEL, D_EXPERT), D_MODEL ** -0.5),
        "w_down": nrm(ks[17], (DEPTH, N_EXPERTS, D_EXPERT, D_MODEL), D_EXPERT ** -0.5),
        "lnf_g": 1.0 + nrm(ks[18], (D_MODEL,), 0.02),
    }

def reference(x_prompt, x_sample, cache_win_k, cache_win_v, ln1_g, w_in, sgu_norm_g, sgu_w, sgu_b,
              w_out, ln2_g, w_router_group, b_router_group, w_router_expert, b_router_expert,
              w_gate, w_up, w_down, lnf_g):
    S = x_prompt.shape[1]
    T = x_sample.shape[1]
    buf_p = min(MAX_WINDOW, S)
    buf_s = cache_win_k.shape[2]
    pos_p = jnp.arange(S)
    pos_s = PAST_LEN + jnp.arange(T)
    xp, xs = x_prompt, x_sample
    kp_l, vp_l, ks_l, vs_l, sv_l = [], [], [], [], []
    for l in range(DEPTH):
        moe = lambda t: hier_moe(t.reshape(-1, D_MODEL), w_router_group[l], b_router_group[l],
                                 w_router_expert[l], b_router_expert[l], w_gate[l], w_up[l],
                                 w_down[l]).reshape(t.shape)
        h = rmsnorm(xp, ln1_g[l])
        u, va, q, k, v = project(h, w_in[l], pos_p)
        a_out = sgu_prompt(u, va, sgu_norm_g[l], sgu_w[l], sgu_b[l])
        outs, lses = [], []
        for window, dil in DILATED_PATTERNS:
            o, lse = dilated_attn_prompt(q, k, v, dil, window // dil)
            outs.append(o)
            lses.append(lse)
        b_out = merge_by_denominator(outs, lses)
        xp = xp + mix_out(a_out, b_out, w_out[l])
        xp = xp + moe(rmsnorm(xp, ln2_g[l]))
        kp_l.append(k[:, S - buf_p:])
        vp_l.append(v[:, S - buf_p:])
        h = rmsnorm(xs, ln1_g[l])
        u, va, q, k, v = project(h, w_in[l], pos_s)
        a_out, vn = sgu_sample(u, va, sgu_norm_g[l], sgu_w[l], sgu_b[l])
        k_all = jnp.concatenate([cache_win_k[l].astype(k.dtype), k], axis=1)
        v_all = jnp.concatenate([cache_win_v[l].astype(v.dtype), v], axis=1)
        outs, lses = [], []
        for window, dil in DILATED_PATTERNS:
            o, lse = dilated_attn_sample(q, k_all, v_all, buf_s, dil, window // dil)
            outs.append(o)
            lses.append(lse)
        b_out = merge_by_denominator(outs, lses)
        xs = xs + mix_out(a_out, b_out, w_out[l])
        xs = xs + moe(rmsnorm(xs, ln2_g[l]))
        ks_l.append(k)
        vs_l.append(v)
        sv_l.append(vn)
    y_prompt = rmsnorm(xp, lnf_g)
    y_sample = rmsnorm(xs, lnf_g)
    return (y_prompt, y_sample, jnp.stack(kp_l), jnp.stack(vp_l), jnp.stack(ks_l), jnp.stack(vs_l), jnp.stack(sv_l))


_drawn_inputs = setup_inputs


def setup_inputs(seed=0):
    import zlib

    import numpy as np

    out = dict(_drawn_inputs(seed))
    spreads = {}
    factors = {'sgu_norm_g': 2.786, 'ln2_g': 2.704, 'b_router_expert': 5.683, 'lnf_g': 2.908}
    for name, (base, spread) in spreads.items():
        noise = np.random.default_rng([zlib.crc32(name.encode()), seed]).standard_normal(out[name].shape)
        drawn = base * np.exp(spread * noise) if base else spread * noise
        out[name] = __import__('jax').numpy.asarray(drawn.astype(out[name].dtype))
    for name, factor in factors.items():
        out[name] = (out[name] * factor).astype(out[name].dtype)
    return out
```

```python
from contextlib import ExitStack

import numpy as np

import concourse.bass as bass
from concourse import mybir

F32 = mybir.dt.float32
I32 = mybir.dt.int32
ALU = mybir.AluOpType
ACT = mybir.ActivationFunctionType
AX = mybir.AxisListType.X

P = 128
D = 1024
KD = D // P
SEQ = 512
NS = 8
NT = SEQ // P + 1
HEADS, HD = 8, 64
W = HEADS * HD
PAST = 2048
DILATIONS = (1, 4, 16)
NPAT = len(DILATIONS)
NG, EPG = 4, 8
NE = NG * EPG
FE = 128
CAP = 64
PAIRS = NE // 2
ROUNDS = -(-(SEQ + NS) // CAP)
TOTAL = ROUNDS * PAIRS
ROWS = SEQ + NS
EPS = 1e-6
SCALE = HD ** -0.5
NEG = -1e30
FAR = 1.0e6

C_IDENT = 0
C_MASK = C_IDENT + P
C_ROPE = C_MASK + 4 * P
C_LTRI = C_ROPE + 2 * NT * HD
C_IOTA = C_LTRI + P
C_M100 = C_IOTA + TOTAL
C_ECODE = C_M100 + EPG
C_VAL = C_ECODE + NE
C_HM = C_VAL + 4 * NT
C_BIND = C_HM + HEADS
C_BINDT = C_BIND + NS
C_SELB = C_BINDT + NS * HEADS
C_END = C_SELB + NS * P


def rows_of(t):
    return P if t < NT - 1 else NS


def constants():
    c = np.zeros((P, C_END), np.float32)
    r = np.arange(P)
    c[:, C_IDENT:C_IDENT + P] = np.eye(P)
    for j in range(4):
        delta = (3 - j) * P + r[:, None] - r[None, :]
        count = ((delta >= 0) & (delta <= P)).astype(int)
        for dil in DILATIONS[1:]:
            count += (delta >= 0) & (delta % dil == 0)
        c[:, C_MASK + j * P:C_MASK + (j + 1) * P] = np.where(
            count > 0, np.log(np.maximum(count, 1)) / SCALE, NEG)
    inv = (np.float32(10000.0) ** (-np.arange(HD // 2, dtype=np.float32) * np.float32(2.0) / np.float32(HD))).astype(np.float32)
    for t in range(NT):
        pos = (t * P + r if t < NT - 1 else np.full(P, PAST)).astype(np.float32)
        ang = (pos[:, None] * inv[None, :]).astype(np.float32).astype(np.float64)
        at = C_ROPE + t * HD
        c[:, at:at + HD] = np.concatenate([np.cos(ang), np.cos(ang)], 1)
        at += NT * HD
        c[:, at:at + HD] = np.concatenate([-np.sin(ang), np.sin(ang)], 1)
    c[:, C_LTRI:C_LTRI + P] = r[:, None] < r[None, :]
    c[:, C_IOTA:C_IOTA + TOTAL] = np.arange(TOTAL)
    c[:, C_M100:C_M100 + EPG] = np.arange(EPG) - 100
    c[:, C_ECODE:C_ECODE + NE] = 1024 * np.arange(NE)
    for k in range(2):
        for t in range(NT):
            at = C_VAL + 2 * (k * NT + t)
            c[:, at] = t * P + r + 1
            c[:, at + 1] = k * ROWS + t * P + r + 1
    bh = np.arange(NS * HEADS)
    c[bh, C_HM + bh % HEADS] = 1
    c[bh, C_BIND + bh // HEADS] = 1
    c[bh // HEADS, C_BINDT + bh] = 1
    for b in range(NS):
        c[b, C_SELB + b * P:C_SELB + (b + 1) * P] = 1
    return c


SLOTS = [("va", t) for t in range(NT)] + [("u", t) for t in range(NT)]
UNITS = [("q", t) for t in range(NT)] + [("k", t) for t in range(NT)] + [("v", t) for t in range(NT)]
for _s, _u in enumerate(SLOTS):
    UNITS.append(_u)
    if _s < NS:
        UNITS.append(("bq", _s))
UNITS += [("mix", j) for j in range(4)]
UNITS += [("pv", b) for b in range(NS)]
UNITS += [("out", 2 * t + h) for t in range(NT) for h in range(2)]
UNIT = {u: n for n, u in enumerate(UNITS)}
BY_SCALAR = ("v", "u", "bq")
GROUP_AT = {"u": 0, "va": W, "q": 2 * W, "k": 3 * W, "v": 4 * W}
W_ORDER = ["q", "k", "v", "va", "u"]


def evacuated(n):
    scalar = UNITS[n][0] in BY_SCALAR
    return scalar, sum((u[0] in BY_SCALAR) == scalar for u in UNITS[:n + 1])


TURNS = [("h", 2 * t + c) for t in range(NT) for c in range(2)]
TURNS += [("q", t) for t in range(NT - 1)] + [("k", t) for t in range(NT - 1)]
TURNS += [("sgu", t) for t in range(NT - 1)] + [("att", t) for t in range(NT - 1)] + [("sgu", NT - 1)]
TURNS += [("h2", 2 * t + c) for t in range(NT) for c in range(2)]
TURN = {u: n for n, u in enumerate(TURNS)}

TASKS = [(i, h) for i in range(4) for h in range(HEADS)]
PER_SLOT = [4, 4, 3, 3, 3, 3, 3, 3, 3, 3]


def build(nc, x_prompt, x_sample, cache_k, cache_v, ln1_g, w_in, sgu_g, sgu_wt, sgu_w, sgu_bt, sgu_b,
          w_out, ln2_g, w_router, b_router, w_gate, w_up, w_down, lnf_g, const,
          y_prompt, y_sample, k_prompt, v_prompt, k_sample, v_sample, sgu_v_sample):
    h2_dram = nc.dram_tensor("h2_rows", (ROWS, D), F32, kind="Internal").ap()
    y2_dram = nc.dram_tensor("expert_rows", (2 * ROWS, D), F32, kind="Internal").ap()

    with ExitStack() as ctx:
        def sb(name, shape, dt=F32):
            return ctx.enter_context(nc.sbuf_tensor(name, shape, dt))

        def sem(name):
            return ctx.enter_context(nc.semaphore(name))

        x = sb("x", [P, NT, D])
        hT = sb("hT", [P, KD, SEQ + NS])
        wring = sb("wring", [P, 2, KD * W])
        att = sb("att", [P, 4096])
        vring = sb("vring", [P, 3072])
        h2T = sb("h2T", [P, KD, P])
        gain = sb("gain", [P, D])
        gv = sb("gv", [P, 592])
        big = sb("big", [P, 4 * 6144])
        ident = sb("ident", [P, P])
        ones = sb("ones", [P, P])
        ltri = sb("ltri", [P, P])
        iota = sb("iota", [P, TOTAL])
        small = sb("small", [P, EPG + NE + 4 * NT + HEADS + NS + NS * HEADS])
        sT = sb("sT", [P, NPAT, NS * HEADS])
        wr = sb("wr", [P, KD, NG + NE])
        rbias = sb("rbias", [P, NG + NE])
        negm = sb("negm", [P, 32])
        den = sb("den", [P, 32])
        stat = sb("stat", [P, 72])
        epsc = sb("epsc", [P, 1])
        flag = sb("flag", [P, 1], I32)

        def cut(base, at, *shape):
            n = int(np.prod(shape))
            v = base[:, at:at + n]
            if len(shape) == 2:
                return v.rearrange("p (a b) -> p a b", a=shape[0])
            if len(shape) == 3:
                return v.rearrange("p (a b c) -> p a b c", a=shape[0], b=shape[1])
            return v

        m100 = small[:, 0:EPG]
        ecode = small[:, EPG:EPG + NE]
        o = EPG + NE
        val = small[:, o:o + 4 * NT].rearrange("p (a v) -> p a v", v=2)
        o += 4 * NT
        hm, bind = small[0:NS * HEADS, o:o + HEADS], small[0:NS * HEADS, o + HEADS:o + HEADS + NS]
        bindT = small[0:NS, o + HEADS + NS:o + HEADS + NS + NS * HEADS]

        qT = cut(big, 0, 4, SEQ)
        kT = cut(big, 2048, 4, SEQ)
        mask = cut(big, 4096, 512)
        qn = cut(big, 4608, 2, W)
        qs = cut(big, 5632, W)
        kn = cut(big, 6144, NT, W)
        vn = cut(big, 8704, NT, W)
        kring = cut(big, 11264, 2, NPAT, W)
        prod = cut(big, 14336, NPAT, W)
        rtmp = cut(big, 14336, W)
        attn = cut(big, 15872, 4, W)
        sqt = cut(big, 17920, W)
        hbuf = cut(big, 15872, 2, D)
        vv = cut(big, 18432, NT, W)
        uu = cut(big, 20992, NT, W)
        cos = cut(big, 23552, NT, HD)
        sin = cut(big, 23552 + NT * HD, NT, HD)
        bcol = cut(big, 24192, HEADS)
        w00 = cut(big, 24200, HEADS)[0:NS]
        b0 = cut(big, 24208, HEADS)[0:NS]
        ew = big[:, :].rearrange("p (s m e n) -> p s m e n", s=4, m=3, e=2)

        wg = wring[:, :, :].rearrange("p s (k n) -> p s k n", k=KD)
        xg = cut(wring[:, 0, :], 0, 2, D)
        xgT = cut(wring[:, 0, :], 2048, 2, KD * P)
        yrow = cut(wring[:, 1, :], 0, 2, D)
        sg = cut(wring[:, 1, :], 2048, 2, 2 * CAP)
        hid = cut(wring[:, 1, :], 2048 + 256, 2, 2 * CAP)
        idxg = wring[:, 1, 2560:2562].bitcast(I32)
        idxs = wring[:, 1, 2562:2564].bitcast(I32)

        s_sb = cut(att, 0, 2, 512)
        p_sb = cut(att, 1024, 2, 512)
        pt_sb = cut(att, 2048, 2, 512)
        qb = cut(att, 3072, 2, 512)
        masked = cut(att, 0, NS, W)
        vr = cut(vring, 0, 2, NPAT, W)
        selb = cut(vring, 0, NS, P)
        h2n = cut(vring, 0, 2, D)
        wt = h2T
        gvb = gv[:, 0:W]
        sall = gv[0:NS * HEADS, 0:NPAT * P + 1]
        ptm = cut(gv, 400, NPAT, NS * HEADS)
        vw = cut(big, 14336, W)[0:NS, :]

        at = [0]

        def route(*shape):
            n = int(np.prod(shape))
            v = cut(att, at[0], *shape)
            at[0] += n
            return v

        onehot_p = route(2 * NT, P)
        L = route(NT, NG + NE)
        gmax, gsum, gp = route(NT), route(NT), route(NT)
        ge = route(NT, NG)
        gpick = route(NT, NG)
        gidx = route(NT)
        lmul = route(NT, NE)
        sel = route(NT, EPG)
        sel2 = route(NT, EPG)
        pickt = route(NT, EPG)
        m12 = route(2, NT)
        i12 = route(2, NT)
        o12 = route(2 * NT, EPG)
        ex = route(NT)
        gates = route(2, NT)
        O = route(2, NT, NE)
        M = route(NT, NE)
        X = route(NT, NE)
        OX = route(2 * NT, NE)
        rk, rm, r1, r2, r3, r4, rk2, rk3 = [route(2 * NT) for _ in range(8)]
        over = route(NE)
        table = route(2 * TOTAL)
        tabtmp = route(2 * PAIRS * (ROUNDS - 1))
        assert at[0] <= 4096
        tab = table.bitcast(I32)
        val_q = cut(vring, 0, 2 * NT, 2, TOTAL)

        banks = [ctx.enter_context(nc.psum_tensor(f"bank{i}", [P, 512], F32)) for i in range(8)]
        acc, tp, sbk, ptb, ovb = banks[0:2], banks[2:4], banks[4:6], banks[6], banks[7]

        x_in = [sem(f"x_in{t}") for t in range(NT)]
        gain_in = sem("gain_in")
        ident_in, rope_in, mask_in, consts_in, selb_in, gv_in, wt_in, wt_mask = [
            sem(n) for n in ("ident_in", "rope_in", "mask_in", "consts_in", "selb_in", "gv_in", "wt_in", "wt_masked")]
        w_loaded = [sem(f"w_loaded{i}") for i in range(7)]
        k_in = [sem(f"k_in{i}") for i in range(2)]
        v_in = [sem(f"v_in{i}") for i in range(2)]
        squares, h_ready = sem("squares"), sem("h_ready")
        tp_ready, tp_free = sem("tp_ready"), sem("tp_free")
        acc_ready, free_d, free_a = sem("acc_ready"), sem("acc_free_vector"), sem("acc_free_scalar")
        q_ready, k_ready = sem("q_ready"), sem("k_ready")
        s_ready, masked_s, exp_done, p_turned, pt_copied, pv_done, o_done = [
            sem(n) for n in ("s_ready", "masked_s", "exp_done", "p_turned", "pt_copied", "pv_done", "o_done")]
        ones_set, eps_set, rooted = sem("ones_set"), sem("eps_set"), sem("rooted")
        prods, sums = sem("prods"), sem("sums")
        self_s, st_ready, sall_ready, sexp, sp_ready, stb_ready, ptm_ready, fin_ready, fin_copied = [
            sem(n) for n in ("self_s", "st_ready", "sall_ready", "sexp", "sp_ready", "stb_ready", "ptm_ready", "fin_ready", "fin_copied")]
        va_ready, sgu_s_ready = sem("va_ready"), sem("sgu_s_ready")
        sq2, h2_ready, r_done = sem("sq2"), sem("h2_ready"), sem("router_done")
        h2w = [sem(f"h2_written{t}") for t in range(NT)]
        dv = sem("vector_step")
        gexp_in, gexp, eexp_in, eexp = sem("gexp_in"), sem("gexp"), sem("eexp_in"), sem("eexp")
        picks, ranks, onehots, tabs, tab_ready, flag_ready, cnt_ready = [
            sem(n) for n in ("picks", "ranks", "onehots", "tabs", "tab_ready", "flag_ready", "cnt_ready")]
        zeroed = sem("zeroed")
        e_in = [sem(f"expert_in{i}") for i in range(4)]
        gidx_copied, sidx_copied = sem("gidx_copied"), sem("sidx_copied")
        x_landed = [sem(f"x_landed{i}") for i in range(2)]
        y_landed = [sem(f"y_landed{i}") for i in range(2)]
        turned, xt_copied, gu_done, silu_done, hid_done, down_done, y_half_d, y_half_a = [
            sem(n) for n in ("turned", "xt_copied", "gate_up_done", "silu_done", "hid_done", "down_done", "y_half_d", "y_half_a")]
        rows_ready, out_k, out_v, out_s, y_out = sem("rows_ready"), sem("out_k"), sem("out_v"), sem("out_s"), sem("y_out")
        rows_in = [sem(f"rows_in{t}") for t in range(NT)]
        mixed, sq3, y_ready = sem("mixed"), sem("sq3"), sem("y_ready")

        xp = x_prompt.rearrange("a (t p) d -> (a t) p d", p=P)
        xs = x_sample.rearrange("b a d -> (b a) d")
        w_in_v = w_in.rearrange("a (k p) n -> (a p) k n", p=P)
        w_out_v = w_out.rearrange("a (k p) n -> (a p) k n", p=P)
        gate_v = [w[0].rearrange("e (p k) f -> p e (k f)", k=KD) for w in (w_gate, w_up)]
        down_v = w_down[0].rearrange("e p n -> p e n")
        yp = y_prompt.rearrange("a (t p) d -> (a t) p d", p=P)
        ys = y_sample.rearrange("b a d -> (b a) d")

        def free_wait(eng, n):
            if n >= 2:
                scalar, count = evacuated(n - 2)
                eng.wait_ge(free_a if scalar else free_d, count)

        def left(eng, unit):
            scalar, count = evacuated(UNIT[unit])
            eng.wait_ge(free_a if scalar else free_d, count)

        def bcast_rows(src, rows=P):
            return src.partition_broadcast(rows)

        def expert_loads(sp, slot, pair):
            for m in range(2):
                sp.dma_start(ew[:, slot, m], gate_v[m][:, bass.ds(pair, 2), :]).then_inc(e_in[slot], 16)
            sp.dma_start(ew[:, slot, 2], down_v[:, bass.ds(pair, 2), :]).then_inc(e_in[slot], 16)

        block = ctx.enter_context(nc.Block())

        @block.sync
        def _(sp):
            sp.dma_start(x[:, 0, :], xp[0]).then_inc(x_in[0], 16)
            for t in range(1, NT - 1):
                sp.dma_start(x[:, t, :], xp[t]).then_inc(x_in[t], 16)
            sp.dma_start(x[0:NS, NT - 1, :], xs).then_inc(x_in[NT - 1], 16)

            def load_w(n):
                if 2 <= n:
                    sp.wait_ge(acc_ready, UNIT[(W_ORDER[n - 2], NT - 1)] + 1)
                dst = wg[:, n % 2]
                if n < 5:
                    at = GROUP_AT[W_ORDER[n]]
                    src = w_in_v[:, :, at:at + W]
                else:
                    src = w_out_v[:, :, (n - 5) * W:(n - 4) * W]
                sp.dma_start(dst, src).then_inc(w_loaded[n], 16)

            def load_k(b):
                if b >= 2:
                    sp.wait_ge(prods, b - 1)
                for p_, dil in enumerate(DILATIONS):
                    src = cache_k[0, b, PAST - P * dil:PAST:dil].rearrange("j h d -> j (h d)")
                    sp.dma_start(kring[:, b % 2, p_, :], src).then_inc(k_in[b % 2], 16)

            load_w(0)
            load_w(1)
            load_k(0)
            load_k(1)
            load_w(2)
            load_w(3)
            load_w(4)
            for b in range(2, 5):
                load_k(b)
            load_w(5)
            for b in range(5, NS):
                load_k(b)
            load_w(6)
            sp.wait_ge(masked_s, len(TASKS))
            sp.wait_ge(s_ready, len(TASKS))
            sp.wait_ge(self_s, 1)
            sp.wait_ge(prods, NS)
            expert_loads(sp, 0, 0)
            sp.wait_ge(sums, NS)
            sp.wait_ge(acc_ready, UNIT[("mix", 3)] + 1)
            sp.wait_ge(sgu_s_ready, 1)
            sp.wait_ge(tp_ready, TURN[("sgu", NT - 1)] + 1)
            sp.wait_ge(out_k, 32)
            sp.wait_ge(out_s, 16)
            sp.wait_ge(fin_ready, 1)
            expert_loads(sp, 1, 2)
            expert_loads(sp, 2, 4)
            sp.wait_ge(out_v, 32)
            expert_loads(sp, 3, 6)
            with sp.Fori(4, PAIRS - 3, 4) as i:
                for j in range(4):
                    sp.wait_ge(down_done, i + (j - 3))
                    expert_loads(sp, j, i * 2 + 2 * j)
            sp.wait_ge(flag_ready, 1)
            more = sp.value_load(flag[0:1, 0:1], min_val=0, max_val=1)
            with sp.If(more > 0):
                with sp.Fori(PAIRS, TOTAL - PAIRS + 1, PAIRS) as r:
                    with sp.Fori(0, PAIRS - 3, 4) as i:
                        for j in range(4):
                            sp.wait_ge(down_done, r + i + (j - 3))
                            expert_loads(sp, j, i * 2 + 2 * j)
            sp.wait_ge(rows_ready, 1)
            rows = big[:, 0:2 * NT * D].rearrange("p (t k n) -> p t k n", t=NT, k=2)
            for t in range(NT):
                n = rows_of(t)
                for k in range(2):
                    at = k * ROWS + t * P
                    sp.dma_start(rows[0:n, t, k], y2_dram[at:at + n, :]).then_inc(rows_in[t], 16)
            for t in range(NT):
                sp.wait_ge(y_ready, t + 1)
                sp.dma_start(yp[t] if t < NT - 1 else ys, x[0:rows_of(t), t, :]).then_inc(y_out, 16)
            sp.wait_ge(y_out, 16 * NT)

        @block.gpsimd
        def _(pool):
            nc.gpsimd.memset(epsc[:], EPS).then_inc(eps_set, 1)
            nc.gpsimd.memset(ones[:], 1.0).then_inc(ones_set, 1)
            pool.wait_ge(wt_in, 16)
            nc.gpsimd.affine_select(out=wt[:, :, :], in_=wt[:, :, :], compare_op=ALU.is_ge, fill=0.0, base=0,
                                    pattern=[[0, HEADS], [1, P]], channel_multiplier=-1).then_inc(wt_mask, 1)
            kp = k_prompt.rearrange("a b (t p) h d -> (a b p) t (h d)", p=P)
            vp = v_prompt.rearrange("a b (t p) h d -> (a b p) t (h d)", p=P)
            pool.wait_ge(k_ready, NT)
            pool.dma_start(kp, kn[:, 0:4, :]).then_inc(out_k, 16)
            pool.dma_start(k_sample.rearrange("a b t h d -> (a b t) (h d)"), kn[0:NS, 4, :]).then_inc(out_k, 16)
            left(pool, ("v", NT - 1))
            pool.dma_start(vp, vv[:, 0:4, :]).then_inc(out_v, 16)
            pool.dma_start(v_sample.rearrange("a b t h d -> (a b t) (h d)"), vv[0:NS, 4, :]).then_inc(out_v, 16)
            pool.wait_ge(self_s, 1)
            for b in range(NS):
                pool.wait_ge(k_in[b % 2], 48 * (b // 2 + 1))
                left(pool, ("bq", b))
                if b >= 1:
                    pool.wait_ge(sums, b)
                nc.gpsimd.tensor_tensor(
                    prod[:, :, :], kring[:, b % 2],
                    qb[:, b % 2, :].unsqueeze(1).to_broadcast([P, NPAT, W]), ALU.mult).then_inc(prods, 1)
            pool.wait_ge(va_ready, NT)
            pool.dma_start(sgu_v_sample.rearrange("a b t h d -> (a b t) (h d)"), vn[0:NS, 4, :]).then_inc(out_s, 16)
            for b in range(NS):
                if b >= 2:
                    pool.wait_ge(acc_ready, UNIT[("pv", b - 2)] + 1)
                for p_, dil in enumerate(DILATIONS):
                    src = cache_v[0, b, PAST - P * dil:PAST:dil].rearrange("j h d -> j (h d)")
                    pool.dma_start(vr[:, b % 2, p_, :], src).then_inc(v_in[b % 2], 16)
            for t in range(NT):
                pool.wait_ge(h2_ready, t + 1)
                pool.dma_start(h2_dram[t * P:t * P + rows_of(t), :], h2n[0:rows_of(t), t % 2, :]).then_inc(h2w[t], 16)
            pool.wait_ge(acc_ready, UNIT[("out", 2 * NT - 1)] + 1)
            nc.gpsimd.memset(xg[:, :, :], 0.0).then_inc(zeroed, 1)
            pool.wait_ge(zeroed, 1)
            for t in range(NT):
                pool.wait_ge(h2w[t], 16)
            pool.wait_ge(tab_ready, 1)

            def gather(n, b, first=False):
                if not first:
                    pool.wait_ge(turned, n - 1)
                nc.gpsimd.tensor_copy(idxg[:, b:b + 1], tab[:, bass.ds(n, 1)]).then_inc(gidx_copied, 1)
                pool.wait_ge(gidx_copied, n + 1)
                nc.gpsimd.indirect_dma_start(
                    out=xg[:, b, :], out_offset=None, in_=h2_dram,
                    in_offset=bass.IndirectOffsetOnAxis(ap=idxg[:, b:b + 1], axis=0),
                    bounds_check=n + (ROWS - 1), oob_is_err=False).then_inc(x_landed[b], 16)

            def scatter(n, b):
                pool.wait_ge(y_half_d, n + 1)
                pool.wait_ge(y_half_a, n + 1)
                nc.gpsimd.tensor_copy(idxs[:, b:b + 1], tab[:, bass.ds(n + TOTAL, 1)]).then_inc(sidx_copied, 1)
                pool.wait_ge(sidx_copied, n + 1)
                nc.gpsimd.indirect_dma_start(
                    out=y2_dram, out_offset=bass.IndirectOffsetOnAxis(ap=idxs[:, b:b + 1], axis=0),
                    in_=yrow[:, b, :], in_offset=None,
                    bounds_check=n + (2 * ROWS - 1), oob_is_err=False).then_inc(y_landed[b], 16)

            def work(first, last):
                gather(first, 0, first == 0)
                gather(first + 1, 1, first == 0)
                with pool.Fori(first, last - 7, 4) as i:
                    for j in range(4):
                        gather(i + (j + 2), j % 2)
                        scatter(i + j, j % 2)
                for n in range(last - 4, last):
                    if n + 2 < last:
                        gather(n + 2, n % 2)
                    scatter(n, n % 2)
                for b in range(2):
                    pool.wait_ge(y_landed[b], 8 * last)

            work(0, PAIRS)
            pool.wait_ge(flag_ready, 1)
            more = pool.value_load(flag[0:1, 0:1], min_val=0, max_val=1)
            with pool.If(more > 0):
                work(PAIRS, TOTAL)
            pool.drain().then_inc(rows_ready, 1)
            for s_, n_ in ((out_k, 32), (out_v, 32), (out_s, 16)):
                pool.wait_ge(s_, n_)

        @block.scalar
        def _(act):
            act.dma_start(gain[:, :], ln1_g.partition_broadcast(P)).then_inc(gain_in, 16)
            act.dma_start(ident[:, :], const[:, C_IDENT:C_IDENT + P]).then_inc(ident_in, 16)
            act.dma_start(cos[:, :, :], const[:, C_ROPE:C_ROPE + NT * HD].rearrange("p (t n) -> p t n", t=NT)).then_inc(rope_in, 16)
            act.dma_start(sin[:, :, :], const[:, C_ROPE + NT * HD:C_LTRI].rearrange("p (t n) -> p t n", t=NT)).then_inc(rope_in, 16)
            act.dma_start(selb[0:NS], const[0:NS, C_SELB:C_END].rearrange("p (b n) -> p b n", b=NS)).then_inc(selb_in, 16)
            act.dma_start(gvb, sgu_g.partition_broadcast(P)).then_inc(gv_in, 16)
            act.dma_start(mask, const[:, C_MASK:C_MASK + 4 * P]).then_inc(mask_in, 16)
            act.dma_start(wt[:, :, :], sgu_wt).then_inc(wt_in, 16)
            act.dma_start(ltri[:, :], const[:, C_LTRI:C_LTRI + P]).then_inc(consts_in, 16)
            act.dma_start(iota[:, :], const[:, C_IOTA:C_IOTA + TOTAL]).then_inc(consts_in, 16)
            act.dma_start(small[:, :], const[:, C_M100:C_SELB]).then_inc(consts_in, 16)
            act.dma_start(wr[:, :, :], w_router).then_inc(consts_in, 16)
            act.dma_start(rbias[:, :], b_router.partition_broadcast(P)).then_inc(consts_in, 16)
            act.dma_start(bcol[:, :], sgu_bt).then_inc(consts_in, 16)
            act.dma_start(w00[:, :], sgu_w.partition_broadcast(NS)).then_inc(consts_in, 16)
            act.dma_start(b0[:, :], sgu_b.partition_broadcast(NS)).then_inc(consts_in, 16)

            def turn(unit, dst):
                n = TURN[unit]
                m = dst.shape[-1]
                act.wait_ge(tp_ready, n + 1)
                src = tp[n % 2][:, 0:4 * m].rearrange("p (c m) -> p c m", c=4)
                nc.scalar.activation(dst, src, ACT.Copy).then_inc(tp_free, 1)

            def cols(t):
                return slice(t * P, t * P + rows_of(t))

            def root(sem_, count, v):
                act.wait_ge(sem_, count)
                nc.scalar.activation(v, v, ACT.Sqrt, bias=epsc[0:v.shape[0], :]).then_inc(rooted, 1)

            act.wait_ge(eps_set, 1)
            def square(t):
                act.wait_ge(x_in[t], 16)
                if t >= 2:
                    act.wait_ge(tp_ready, 2 * (t - 1))
                n = rows_of(t)
                nc.scalar.activation(hbuf[0:n, t % 2, :], x[0:n, t, :], ACT.Square, scale=D ** -0.5,
                                     accum_out=stat[0:n, t:t + 1]).then_inc(squares, 1)
                root(squares, t + 1, stat[0:n, t:t + 1])

            square(0)
            square(1)
            for t in range(NT):
                for c in range(2):
                    turn(("h", 2 * t + c), hT[:, 4 * c:4 * c + 4, cols(t)])
                if t + 2 < NT:
                    square(t + 2)
            for t in range(NT - 1):
                turn(("q", t), qT[:, :, cols(t)])
            for t in range(NT - 1):
                turn(("k", t), kT[:, :, cols(t)])

            def copy_unit(unit, dst):
                n = UNIT[unit]
                act.wait_ge(acc_ready, n + 1)
                nc.scalar.activation(dst, acc[n % 2][0:dst.shape[0], 0:W], ACT.Copy).then_inc(free_a, 1)

            for t in range(NT):
                copy_unit(("v", t), vv[0:rows_of(t), t, :])

            def exps(n):
                width = P * (TASKS[n][0] + 1)
                act.wait_ge(masked_s, n + 1)
                if n >= 2:
                    act.wait_ge(p_turned, n - 1)
                nc.scalar.activation(p_sb[:, n % 2, 0:width], s_sb[:, n % 2, 0:width], ACT.Exp, scale=-1.0,
                                     bias=negm[:, n:n + 1], accum_out=den[:, n:n + 1]).then_inc(exp_done, 1)

            def copy_pt(n):
                width = P * (TASKS[n][0] + 1)
                act.wait_ge(p_turned, n + 1)
                if n >= 2:
                    act.wait_ge(pv_done, n - 1)
                nc.scalar.activation(pt_sb[:, n % 2, 0:width], ptb[:, 0:width], ACT.Copy).then_inc(pt_copied, 1)

            exps(0)
            n = 0
            for s, (kind, t) in enumerate(SLOTS):
                if kind == "u":
                    copy_unit((kind, t), uu[0:rows_of(t), t, :])
                if s < NS:
                    if s >= 2:
                        act.wait_ge(prods, s - 1)
                    copy_unit(("bq", s), qb[:, s % 2, :])
                for _ in range(PER_SLOT[s]):
                    copy_pt(n)
                    if n + 1 < len(TASKS):
                        exps(n + 1)
                    n += 1
            act.wait_ge(sall_ready, 1)
            nc.scalar.activation(sall, sall, ACT.Exp, bias=stat[0:64, 11:12],
                                 accum_out=stat[0:64, 12:13]).then_inc(sexp, 1)
            for t in range(NT - 1):
                turn(("sgu", t), hT[:, 0:4, cols(t)])
            for t in range(NT - 1):
                turn(("att", t), hT[:, 4:8, cols(t)])
            turn(("sgu", NT - 1), hT[:, 0:4, cols(NT - 1)])
            act.wait_ge(fin_ready, 1)
            nc.scalar.activation(hT[:, 4:8, cols(NT - 1)], ovb[:, 0:4 * NS].rearrange("p (c b) -> p c b", c=4),
                                 ACT.Copy).then_inc(fin_copied, 1)
            act.wait_ge(h_ready, NT)
            act.dma_start(gain[:, :], ln2_g.partition_broadcast(P)).then_inc(gain_in, 16)

            def square2(t):
                n = rows_of(t)
                left(act, ("out", 2 * t + 1))
                act.wait_ge(acc_ready, UNIT[("pv", NS - 1)] + 1)
                if t >= 2:
                    act.wait_ge(h2w[t - 2], 16)
                    act.wait_ge(tp_ready, TURN[("h2", 2 * (t - 2) + 1)] + 1)
                nc.scalar.activation(h2n[0:n, t % 2, :], x[0:n, t, :], ACT.Square, scale=D ** -0.5,
                                     accum_out=stat[0:n, 16 + t:17 + t]).then_inc(sq2, 1)
                root(sq2, t + 1, stat[0:n, 16 + t:17 + t])

            def turn_h2(t):
                if t >= 1:
                    act.wait_ge(r_done, t)
                else:
                    act.wait_ge(acc_ready, UNIT[("mix", 3)] + 1)
                for c in range(2):
                    turn(("h2", 2 * t + c), h2T[:, 4 * c:4 * c + 4, 0:rows_of(t)])

            for t in range(NT):
                square2(t)
                turn_h2(t)
            act.wait_ge(gexp_in, 1)
            nc.scalar.activation(ge, ge, ACT.Exp).then_inc(gexp, 1)
            act.wait_ge(eexp_in, 1)
            nc.scalar.activation(ex, ex, ACT.Exp).then_inc(eexp, 1)
            act.wait_ge(h2_ready, NT)
            act.dma_start(gain[:, :], lnf_g.partition_broadcast(P)).then_inc(gain_in, 16)

            def copy_xt(n, b):
                act.wait_ge(turned, n + 1)
                for c in range(2):
                    last = nc.scalar.activation(xgT[:, b, c * 512:(c + 1) * 512], sbk[c][:, :], ACT.Copy)
                last.then_inc(xt_copied, 1)

            def silu(n, b):
                act.wait_ge(gu_done, n + 1)
                bank = (ptb, ovb)[b]
                src = bank[:, 0:4 * CAP].rearrange("p (e m c) -> p e m c", e=2, m=2)[:, :, 0, :]
                nc.scalar.activation(sg[:, b].rearrange("p (e c) -> p e c", e=2), src, ACT.Silu).then_inc(silu_done, 1)

            def copy_y(n, b, first=False):
                act.wait_ge(down_done, n + 1)
                if not first:
                    act.wait_ge(y_landed[b], scattered(n, b))
                bank = (acc, tp)[b]
                nc.scalar.activation(yrow[:, b, 512:1024], bank[1][:, :], ACT.Copy).then_inc(y_half_a, 1)

            def work(first, last):
                copy_xt(first, 0)
                if first == 0:
                    for n in range(4):
                        silu(n, n % 2)
                        copy_xt(n + 1, (n + 1) % 2)
                        copy_y(n, n % 2, n < 2)
                with act.Fori(4 if first == 0 else first, last - 7, 4) as i:
                    for j in range(4):
                        silu(i + j, j % 2)
                        copy_xt(i + (j + 1), (j + 1) % 2)
                        copy_y(i + j, j % 2)
                for n in range(last - 4, last):
                    silu(n, n % 2)
                    if n + 1 < last:
                        copy_xt(n + 1, (n + 1) % 2)
                    copy_y(n, n % 2)

            work(0, PAIRS)
            act.wait_ge(flag_ready, 1)
            more = act.value_load(flag[0:1, 0:1], min_val=0, max_val=1)
            with act.If(more > 0):
                work(PAIRS, TOTAL)
            for t in range(NT):
                n = rows_of(t)
                act.wait_ge(mixed, t + 1)
                nc.scalar.activation(hT[0:n, :, 0:P], x[0:n, t, :].rearrange("p (k n) -> p k n", k=KD), ACT.Square, scale=D ** -0.5,
                                     accum_out=stat[0:n, 24 + t:25 + t]).then_inc(sq3, 1)
                root(sq3, t + 1, stat[0:n, 24 + t:25 + t])

        @block.vector
        def _(dve):
            steps = [0]

            def step(ins):
                steps[0] += 1
                ins.then_inc(dv, 1)
                dve.wait_ge(dv, steps[0])

            V = nc.vector

            def rsqrt(y, v, w):
                step(V.tensor_scalar(w.bitcast(I32), v.bitcast(I32), 1, None, ALU.logical_shift_right))
                step(V.tensor_scalar(y.bitcast(I32), w.bitcast(I32), -1.0, float(0x5F3759DF), ALU.mult, ALU.add))
                for _ in range(4):
                    step(V.tensor_tensor(w, y, y, ALU.mult))
                    step(V.scalar_tensor_tensor(out=w, in0=w, scalar=-0.5, in1=v, op0=ALU.mult, op1=ALU.mult))
                    step(V.scalar_tensor_tensor(out=y, in0=w, scalar=1.5, in1=y, op0=ALU.add, op1=ALU.mult))

            dve.wait_ge(gain_in, 16)
            for t in range(NT):
                n = rows_of(t)
                dve.wait_ge(rooted, t + 1)
                step(V.reciprocal(stat[0:n, 5 + t:6 + t], stat[0:n, t:t + 1]))
                V.scalar_tensor_tensor(out=hbuf[0:n, t % 2, :], in0=x[0:n, t, :], scalar=stat[0:n, 5 + t:6 + t],
                                       in1=gain[0:n, :], op0=ALU.mult, op1=ALU.mult).then_inc(h_ready, 1)

            def rope(kind, t):
                u = UNIT[(kind, t)]
                n = rows_of(t)
                dst = kn[0:n, t] if kind == "k" else (qn[0:n, t % 2] if t < NT - 1 else qs[0:n])
                z = acc[u % 2][0:n, 0:W].rearrange("p (h n) -> p h n", h=HEADS)
                d3 = dst.rearrange("p (h n) -> p h n", h=HEADS)
                t3 = rtmp[0:n].rearrange("p (h n) -> p h n", h=HEADS)
                half = HD // 2

                def tb(table, a, b):
                    return table[0:n, t, a:b].unsqueeze(1).to_broadcast([n, HEADS, b - a])
                dve.wait_ge(acc_ready, u + 1)
                if kind == "q" and 2 <= t < NT - 1:
                    dve.wait_ge(tp_ready, TURN[("q", t - 2)] + 1)
                V.tensor_tensor(d3, z, tb(cos, 0, HD), ALU.mult)
                V.tensor_tensor(t3[:, :, 0:half], z[:, :, half:HD], tb(sin, 0, half), ALU.mult)
                V.tensor_tensor(t3[:, :, half:HD], z[:, :, 0:half], tb(sin, half, HD), ALU.mult).then_inc(free_d, 1)
                dve.wait_ge(free_d, evacuated(u)[1])
                V.tensor_tensor(dst, dst, rtmp[0:n], ALU.add).then_inc(q_ready if kind == "q" else k_ready, 1)
                dve.wait_ge(q_ready if kind == "q" else k_ready, t + 1)

            dve.wait_ge(rope_in, 32)
            for kind in ("q", "k"):
                for t in range(NT):
                    rope(kind, t)
            pr = rtmp[0:NS]
            step(V.tensor_tensor(pr, qs[0:NS], kn[0:NS, 4], ALU.mult))
            V.tensor_reduce(stat[0:NS, 32:40], pr.rearrange("p (h n) -> p h n", h=HEADS), AX, ALU.add).then_inc(self_s, 1)

            def add_mask(n):
                i, h = TASKS[n]
                width = P * (i + 1)
                dve.wait_ge(s_ready, n + 1)
                if n >= 2:
                    dve.wait_ge(exp_done, n - 1)
                V.tensor_tensor_reduce(out=s_sb[:, n % 2, 0:width], in0=sbk[n % 2][:, 0:width],
                                       in1=mask[:, (3 - i) * P:4 * P], scale=-SCALE, scalar=3.0e38,
                                       op0=ALU.add, op1=ALU.min, accum_out=negm[:, n:n + 1]).then_inc(masked_s, 1)

            def scale_o(n):
                i, h = TASKS[n]
                dve.wait_ge(exp_done, n + 1)
                step(V.reciprocal(den[:, n:n + 1], den[:, n:n + 1]))
                dve.wait_ge(pv_done, n + 1)
                V.tensor_scalar(attn[:, i, h * HD:(h + 1) * HD], ovb[:, 0:HD], den[:, n:n + 1], None,
                                ALU.mult).then_inc(o_done, 1)

            def va(t):
                u = UNIT[("va", t)]
                n = rows_of(t)
                z = acc[u % 2][0:n, 0:W]
                dst = vn[0:n, t]
                g3 = dst.rearrange("p (h n) -> p h n", h=HEADS)
                z3 = z.rearrange("p (h n) -> p h n", h=HEADS)
                r8 = stat[0:n, 48:56]
                dve.wait_ge(acc_ready, u + 1)
                step(V.tensor_copy(dst, z))
                step(V.scalar_tensor_tensor(out=sqt[0:n], in0=dst, scalar=1.0 / HD, in1=dst, op0=ALU.mult, op1=ALU.mult))
                step(V.tensor_reduce(r8, sqt[0:n].rearrange("p (h n) -> p h n", h=HEADS), AX, ALU.add))
                step(V.tensor_scalar(r8, r8, EPS, None, ALU.add))
                y8 = stat[0:n, 56:64]
                rsqrt(y8, r8, stat[0:n, 64:72])
                V.tensor_tensor(g3, z3, y8.unsqueeze(2).to_broadcast([n, HEADS, HD]), ALU.mult).then_inc(free_d, 1)
                dve.wait_ge(free_d, evacuated(u)[1])
                V.tensor_tensor(dst, dst, gvb[0:n], ALU.mult).then_inc(va_ready, 1)

            def sum_prod(b):
                dve.wait_ge(prods, b + 1)
                V.tensor_reduce(sT[:, :, b * HEADS:(b + 1) * HEADS],
                                prod[:, :, :].rearrange("p a (h n) -> p a h n", h=HEADS), AX, ALU.add).then_inc(sums, 1)

            dve.wait_ge(mask_in, 16)
            dve.wait_ge(gv_in, 16)
            add_mask(0)
            add_mask(1)
            n = 0
            for s, (kind, t) in enumerate(SLOTS):
                if kind == "va":
                    va(t)
                for j in range(PER_SLOT[s]):
                    if n + 2 < len(TASKS):
                        add_mask(n + 2)
                    scale_o(n)
                    n += 1
                    if s < NS and j == 1:
                        sum_prod(s)
            dve.wait_ge(consts_in, 128)
            us, vs_ = uu[0:NS, 4], vn[0:NS, 4]
            tmp8 = sqt[0:NS]

            def g8(v):
                return v.unsqueeze(2).to_broadcast([NS, HEADS, HD])

            def h8(v):
                return v.rearrange("p (h n) -> p h n", h=HEADS)
            dve.wait_ge(va_ready, NT)
            step(V.tensor_tensor(h8(tmp8), h8(vs_), g8(w00[:, :]), ALU.mult))
            step(V.tensor_tensor(h8(tmp8), h8(tmp8), g8(b0[:, :]), ALU.add))
            left(dve, ("u", NT - 1))
            V.tensor_tensor(us, us, tmp8, ALU.mult).then_inc(sgu_s_ready, 1)
            R = NS * HEADS
            dve.wait_ge(st_ready, 1)
            step(V.tensor_scalar(sall[:, 0:NPAT * P], sbk[0][0:R, 0:NPAT * P], SCALE, None, ALU.mult))
            step(V.tensor_tensor_reduce(out=stat[0:R, 40:48], in0=sbk[0][0:R, 384:392], in1=hm, scale=SCALE,
                                        scalar=0.0, op0=ALU.mult, op1=ALU.add, accum_out=stat[0:R, 10:11]))
            step(V.tensor_scalar(sall[:, NPAT * P:], stat[0:R, 10:11], float(np.log(NPAT)), None, ALU.add))
            step(V.tensor_reduce(stat[0:R, 13:14], sall, AX, ALU.max))
            V.tensor_scalar(stat[0:R, 11:12], stat[0:R, 13:14], -1.0, None, ALU.mult).then_inc(sall_ready, 1)

            def mix(j):
                u = UNIT[("mix", j)]
                dve.wait_ge(acc_ready, u + 1)
                for g in range(2):
                    cols_ = slice((2 * j + g) * HD, (2 * j + g + 1) * HD)
                    src = acc[u % 2][:, g * 256:(g + 1) * 256].rearrange("p (t n) -> p t n", t=4)
                    last = V.scalar_tensor_tensor(out=uu[:, 0:4, cols_], in0=src,
                                                  scalar=bcol[:, 2 * j + g:2 * j + g + 1], in1=uu[:, 0:4, cols_],
                                                  op0=ALU.add, op1=ALU.mult)
                last.then_inc(free_d, 1)

            mix(0)
            mix(1)
            dve.wait_ge(sexp, 1)
            step(V.reciprocal(stat[0:R, 14:15], stat[0:R, 12:13]))
            step(V.tensor_scalar(sall, sall, stat[0:R, 14:15], None, ALU.mult))
            V.tensor_scalar(stat[0:R, 40:48], hm, sall[:, NPAT * P:], None, ALU.mult).then_inc(sp_ready, 1)
            mix(2)
            mix(3)
            dve.wait_ge(stb_ready, 1)
            V.tensor_copy(ptm[:, :, :], sbk[1][:, 0:NPAT * R].rearrange("p (a r) -> p a r", a=NPAT)).then_inc(ptm_ready, 1)
            dve.wait_ge(sums, NS)
            V.tensor_tensor(h8(vw), h8(vv[0:NS, 4]), g8(sbk[1][0:NS, 192:200]), ALU.mult).then_inc(ptm_ready, 1)
            for b in range(NS):
                u = UNIT[("pv", b)]
                dve.wait_ge(acc_ready, u + 1)
                if b == 0:
                    dve.wait_ge(pv_done, len(TASKS))
                    dve.wait_ge(prods, NS)
                V.tensor_tensor(h8(masked[0:NS, b]), h8(acc[u % 2][0:NS, 0:W]), g8(ident[0:NS, 0:NS]),
                                ALU.mult).then_inc(free_d, 1)
            for t in range(NT):
                n = rows_of(t)
                for half in range(2):
                    u = UNIT[("out", 2 * t + half)]
                    dve.wait_ge(acc_ready, u + 1)
                    xh = x[0:n, t, half * 512:(half + 1) * 512]
                    ins = V.tensor_tensor(xh, xh, acc[u % 2][0:n, :], ALU.add)
                    ins.then_inc(free_d, 1)
                dve.wait_ge(free_d, evacuated(u)[1])
                if t == 0:
                    dve.wait_ge(gain_in, 32)
                dve.wait_ge(rooted, NT + t + 1)
                step(V.reciprocal(stat[0:n, 16 + t:17 + t], stat[0:n, 16 + t:17 + t]))
                V.scalar_tensor_tensor(
                    out=h2n[0:n, t % 2, :].rearrange("p (k q) -> p k q", k=KD),
                    in0=x[0:n, t, :].rearrange("p (q k) -> p k q", k=KD), scalar=stat[0:n, 16 + t:17 + t],
                    in1=gain[0:n, :].rearrange("p (q k) -> p k q", k=KD),
                    op0=ALU.mult, op1=ALU.mult).then_inc(h2_ready, 1)

            def over_t(v, m):
                return v.unsqueeze(2).to_broadcast([P, v.shape[1], m])

            def over_r(v, t=NT):
                return v.unsqueeze(1).to_broadcast([P, t, v.shape[1]])
            dve.wait_ge(fin_ready, 1)
            step(V.memset(L[:, NT - 1, :], 0.0))
            dve.wait_ge(r_done, NT)
            lg = ptb[:, 0:NT * (NG + NE)].rearrange("p (t n) -> p t n", t=NT)
            V.tensor_tensor(L[:, 0:NT - 1, :], lg[:, 0:NT - 1, :], over_r(rbias[:, :], NT - 1), ALU.add)
            step(V.tensor_tensor(L[0:NS, NT - 1, :], lg[0:NS, NT - 1, :], rbias[0:NS, :], ALU.add))
            L4 = L[:, :, 0:NG]
            step(V.tensor_reduce(gmax, L4, AX, ALU.max))
            V.tensor_tensor(ge, L4, over_t(gmax, NG), ALU.subtract).then_inc(gexp_in, 1)
            step(V.tensor_tensor(gpick, L4, over_t(gmax, NG), ALU.is_ge))
            step(V.tensor_tensor(gpick, gpick, over_r(m100[:, 0:NG]), ALU.mult))
            step(V.tensor_reduce(gidx, gpick, AX, ALU.min))
            step(V.tensor_tensor(gpick, over_r(m100[:, 0:NG]), over_t(gidx, NG), ALU.is_equal))
            og = gpick.unsqueeze(3).to_broadcast([P, NT, NG, EPG])
            le4 = L[:, :, NG:NG + NE].rearrange("p t (g e) -> p t g e", g=NG)
            lm4 = lmul.rearrange("p t (g e) -> p t g e", g=NG)
            step(V.tensor_tensor(lm4, le4, og, ALU.mult))
            step(V.tensor_reduce(sel, lmul.rearrange("p t (g e) -> p t e g", g=NG), AX, ALU.add))
            for k, s_ in enumerate((sel, sel2)):
                ok = o12[:, k * NT:(k + 1) * NT, :]
                step(V.tensor_reduce(m12[:, k, :], s_, AX, ALU.max))
                step(V.tensor_tensor(pickt, s_, over_t(m12[:, k, :], EPG), ALU.is_ge))
                step(V.tensor_tensor(pickt, pickt, over_r(m100), ALU.mult))
                step(V.tensor_reduce(i12[:, k, :], pickt, AX, ALU.min))
                step(V.tensor_tensor(ok, over_r(m100), over_t(i12[:, k, :], EPG), ALU.is_equal))
                if k == 0:
                    step(V.scalar_tensor_tensor(out=sel2, in0=ok, scalar=NEG, in1=sel, op0=ALU.mult, op1=ALU.add))
            V.tensor_tensor(ex, m12[:, 1, :], m12[:, 0, :], ALU.subtract).then_inc(eexp_in, 1)
            for k in range(2):
                ins = V.tensor_tensor(
                    O[:, k].rearrange("p t (g e) -> p t g e", g=NG), og,
                    o12[:, k * NT:(k + 1) * NT, :].unsqueeze(2).to_broadcast([P, NT, NG, EPG]), ALU.mult)
            step(ins)
            V.tensor_tensor(M, O[:, 0], O[:, 1], ALU.add).then_inc(picks, 1)
            dve.wait_ge(gexp, 1)
            step(V.tensor_reduce(gsum, ge, AX, ALU.add))
            dve.wait_ge(eexp, 1)
            step(V.tensor_scalar(gp, ex, 1.0, None, ALU.add))
            step(V.tensor_tensor(gp, gp, gsum, ALU.mult))
            step(V.reciprocal(gates[:, 0, :], gp))
            step(V.tensor_tensor(gates[:, 1, :], gates[:, 0, :], ex, ALU.mult))
            dve.wait_ge(ranks, 1)
            pre = acc[0][:, 0:NT * NE].rearrange("p (t n) -> p t n", t=NT)
            step(V.tensor_tensor(X, pre, over_r(ecode), ALU.add))
            for k in range(2):
                ins = V.tensor_tensor(OX[:, k * NT:(k + 1) * NT, :], O[:, k], X, ALU.mult)
            step(ins)
            step(V.tensor_reduce(rk, OX, AX, ALU.add))
            xi, lo, hi, rd, pr_ = [v.bitcast(I32) for v in (rm, r2, r3, rk2, rk3)]
            step(V.tensor_copy(xi, rk))
            V.tensor_scalar(lo, xi, CAP - 1, None, ALU.bitwise_and)
            V.tensor_scalar(hi, xi, 4, CAP, ALU.logical_shift_right, ALU.bitwise_and)
            V.tensor_scalar(rd, xi, 6, 15, ALU.logical_shift_right, ALU.bitwise_and)
            step(V.tensor_scalar(pr_, xi, 11, None, ALU.logical_shift_right))
            V.tensor_tensor(r1, lo, hi, ALU.add)
            step(V.scalar_tensor_tensor(out=r4, in0=rd, scalar=float(PAIRS), in1=pr_, op0=ALU.mult, op1=ALU.add))
            dve.wait_ge(h2w[NT - 1], 16)
            dve.wait_ge(h2w[NT - 2], 16)
            V.tensor_tensor(onehot_p, over_r(iota[:, 0:P], 2 * NT), over_t(r1, P), ALU.is_equal)
            last_tab = 0
            for part, (a, b) in enumerate(((0, PAIRS), (PAIRS, TOTAL))):
                m = b - a
                for v in range(2):
                    ins = V.tensor_tensor(val_q[:, :, v, a:b], over_r(iota[:, a:b], 2 * NT), over_t(r4, m), ALU.is_equal)
                step(ins)
                for v in range(2):
                    ins = V.tensor_tensor(val_q[:, :, v, a:b], val_q[:, :, v, a:b],
                                          val[:, :, v:v + 1].to_broadcast([P, 2 * NT, m]), ALU.mult)
                ins.then_inc(onehots, 1)
                dve.wait_ge(tabs, part + 1)
                src = tp[part][:, 0:2 * m].rearrange("p (v n) -> p v n", v=2)
                tt = tabtmp[:, 0:2 * m].rearrange("p (v n) -> p v n", v=2)
                step(V.tensor_scalar(tt, src, 0.0, FAR, ALU.is_equal, ALU.mult))
                dst = tab.rearrange("p (v n) -> p v n", v=2)[:, :, a:b]
                V.scalar_tensor_tensor(out=dst, in0=src, scalar=-1.0, in1=tt, op0=ALU.add, op1=ALU.add).then_inc(tab_ready, 1)
            dve.wait_ge(cnt_ready, 1)
            step(V.tensor_reduce(rk[:, 0:1], acc[1][:, 256:256 + NE], AX, ALU.max))
            V.tensor_scalar(flag[:, :], rk[:, 0:1], float(CAP), None, ALU.is_gt).then_inc(flag_ready, 1)

            def hidden(n, b):
                dve.wait_ge(silu_done, n + 1)
                bank = (ptb, ovb)[b]
                up = bank[:, 0:4 * CAP].rearrange("p (e m c) -> p e m c", e=2, m=2)[:, :, 1, :]
                V.tensor_tensor(hid[:, b].rearrange("p (e c) -> p e c", e=2),
                                sg[:, b].rearrange("p (e c) -> p e c", e=2), up, ALU.mult).then_inc(hid_done, 1)

            def copy_y(n, b, first=False):
                dve.wait_ge(down_done, n + 1)
                if not first:
                    dve.wait_ge(y_landed[b], scattered(n, b))
                V.tensor_copy(yrow[:, b, 0:512], (acc, tp)[b][0][:, :]).then_inc(y_half_d, 1)

            def work(first, last):
                if first == 0:
                    for n in range(4):
                        hidden(n, n % 2)
                        copy_y(n, n % 2, n < 2)
                with dve.Fori(4 if first == 0 else first, last - 3, 4) as i:
                    for j in range(4):
                        hidden(i + j, j % 2)
                        copy_y(i + j, j % 2)

            work(0, PAIRS)
            more = dve.value_load(flag[0:1, 0:1], min_val=0, max_val=1)
            with dve.If(more > 0):
                work(PAIRS, TOTAL)
            rows = big[:, 0:2 * NT * D].rearrange("p (t k n) -> p t k n", t=NT, k=2)
            dve.wait_ge(gain_in, 48)
            for t in range(NT):
                n = rows_of(t)
                xt = x[0:n, t, :]
                dve.wait_ge(rows_in[t], 32)
                step(V.scalar_tensor_tensor(out=xt, in0=rows[0:n, t, 0], scalar=gates[0:n, 0, t:t + 1], in1=xt,
                                            op0=ALU.mult, op1=ALU.add))
                V.scalar_tensor_tensor(out=xt, in0=rows[0:n, t, 1], scalar=gates[0:n, 1, t:t + 1], in1=xt,
                                       op0=ALU.mult, op1=ALU.add).then_inc(mixed, 1)
                dve.wait_ge(mixed, t + 1)
                dve.wait_ge(rooted, 2 * NT + t + 1)
                step(V.reciprocal(stat[0:n, 24 + t:25 + t], stat[0:n, 24 + t:25 + t]))
                V.scalar_tensor_tensor(out=xt, in0=xt, scalar=stat[0:n, 24 + t:25 + t], in1=gain[0:n, :],
                                       op0=ALU.mult, op1=ALU.mult).then_inc(y_ready, 1)

        @block.tensor
        def _(pe):
            T = nc.tensor

            def turns(unit, parts):
                n = TURN[unit]
                if n >= 2:
                    pe.wait_ge(tp_free, n - 1)
                m = parts[0].shape[0]
                for c, src in enumerate(parts):
                    ins = T.transpose(tp[n % 2][:, c * m:(c + 1) * m], src, ident[0:m, 0:m])
                ins.then_inc(tp_ready, 1)

            def quarter(rows, base=0):
                return [rows[:, base + c * P:base + (c + 1) * P] for c in range(4)]

            pe.wait_ge(ident_in, 16)
            for t in range(NT):
                pe.wait_ge(h_ready, t + 1)
                for c in range(2):
                    turns(("h", 2 * t + c), quarter(hbuf[0:rows_of(t), t % 2, :], c * 512))

            def project(unit):
                kind, t = unit
                u, n = UNIT[unit], rows_of(t)
                pe.wait_ge(w_loaded[W_ORDER.index(kind)], 16)
                pe.wait_ge(tp_free, 2 * (t + 1))
                free_wait(pe, u)
                for k in range(KD):
                    ins = T.matmul(acc[u % 2][0:n, 0:W], hT[:, k, t * P:t * P + n],
                                   wg[:, W_ORDER.index(kind) % 2, k, :], start=k == 0, stop=k == KD - 1)
                ins.then_inc(acc_ready, 1)

            def turn_qk(kind, t):
                pe.wait_ge(q_ready if kind == "q" else k_ready, t + 1)
                turns((kind, t), quarter(qn[:, t % 2] if kind == "q" else kn[:, t]))

            for kind in ("q", "k"):
                for t in range(NT):
                    project((kind, t))
                    if t >= 1:
                        turn_qk(kind, t - 1)
            for t in range(NT):
                project(("v", t))

            def scores(n):
                i, h = TASKS[n]
                if n == 0:
                    pe.wait_ge(tp_free, TURN[("k", 3)] + 1)
                if n >= 2:
                    pe.wait_ge(masked_s, n - 1)
                r = slice(64 * (h % 2), 64 * (h % 2) + 64)
                T.matmul(sbk[n % 2][:, 0:P * (i + 1)], qT[r, h // 2, i * P:(i + 1) * P],
                         kT[r, h // 2, 0:P * (i + 1)], start=True, stop=True).then_inc(s_ready, 1)

            def turn_p(n):
                pe.wait_ge(exp_done, n + 1)
                if n >= 1:
                    pe.wait_ge(pt_copied, n)
                for j in range(TASKS[n][0] + 1):
                    ins = T.transpose(ptb[:, j * P:(j + 1) * P], p_sb[:, n % 2, j * P:(j + 1) * P], ident[:, :])
                ins.then_inc(p_turned, 1)

            def pv(n):
                i, h = TASKS[n]
                pe.wait_ge(pt_copied, n + 1)
                if n == 0:
                    left(pe, ("v", NT - 1))
                if n >= 1:
                    pe.wait_ge(o_done, n)
                for j in range(i + 1):
                    ins = T.matmul(ovb[:, 0:HD], pt_sb[:, n % 2, j * P:(j + 1) * P],
                                   vv[:, j, h * HD:(h + 1) * HD], start=j == 0, stop=j == i)
                ins.then_inc(pv_done, 1)

            scores(0)
            scores(1)
            n = 0
            for s, unit in enumerate(SLOTS):
                project(unit)
                if s < NS:
                    u = UNIT[("bq", s)]
                    if s == 0:
                        pe.wait_ge(selb_in, 16)
                        pe.wait_ge(q_ready, NT)
                    free_wait(pe, u)
                    T.matmul(acc[u % 2][:, 0:W], selb[0:NS, s, :], qs[0:NS], start=True, stop=True).then_inc(acc_ready, 1)
                for _ in range(PER_SLOT[s]):
                    turn_p(n)
                    if n + 2 < len(TASKS):
                        scores(n + 2)
                    pv(n)
                    n += 1
            pe.wait_ge(sums, NS)
            pe.wait_ge(masked_s, len(TASKS))
            pe.wait_ge(self_s, 1)
            pe.wait_ge(consts_in, 128)
            R = NS * HEADS
            for p_ in range(NPAT):
                T.transpose(sbk[0][0:R, p_ * P:(p_ + 1) * P], sT[:, p_, :], ident[:, :])
            T.matmul(sbk[0][0:R, 384:392], bindT, stat[0:NS, 32:40], start=True, stop=True).then_inc(st_ready, 1)
            pe.wait_ge(wt_mask, 1)
            pe.wait_ge(va_ready, NT)
            for j in range(4):
                u = UNIT[("mix", j)]
                free_wait(pe, u)
                for g in range(2):
                    ins = T.matmul(acc[u % 2][:, g * 256:(g + 1) * 256], wt[:, 2 * j + g, :],
                                   vn[:, 0:4, (2 * j + g) * HD:(2 * j + g + 1) * HD], start=True, stop=True)
                ins.then_inc(acc_ready, 1)
            left(pe, ("mix", 3))
            for t in range(NT - 1):
                turns(("sgu", t), quarter(uu[:, t]))
            pe.wait_ge(o_done, len(TASKS))
            for t in range(NT - 1):
                turns(("att", t), quarter(attn[:, t]))
            pe.wait_ge(sgu_s_ready, 1)
            turns(("sgu", NT - 1), quarter(uu[0:NS, 4]))
            pe.wait_ge(sp_ready, 1)
            for p_ in range(NPAT):
                T.transpose(sbk[1][:, p_ * R:(p_ + 1) * R], sall[:, p_ * P:(p_ + 1) * P], ident[0:R, 0:R])
            T.matmul(sbk[1][0:NS, 192:200], bind, stat[0:R, 40:48], start=True, stop=True).then_inc(stb_ready, 1)
            pe.wait_ge(ptm_ready, 2)
            for b in range(NS):
                u = UNIT[("pv", b)]
                free_wait(pe, u)
                pe.wait_ge(v_in[b % 2], 48 * (b // 2 + 1))
                for p_ in range(NPAT):
                    ins = T.matmul(acc[u % 2][0:NS, 0:W], ptm[:, p_, b * HEADS:(b + 1) * HEADS], vr[:, b % 2, p_, :],
                                   start=p_ == 0, stop=p_ == NPAT - 1)
                ins.then_inc(acc_ready, 1)
            left(pe, ("pv", NS - 1))
            pe.wait_ge(ones_set, 1)
            for c in range(4):
                T.matmul(ovb[:, c * NS:(c + 1) * NS], vw[:, c * P:(c + 1) * P], ident[0:NS, 0:NS], start=True, stop=False)
                for b in range(NS):
                    ins = T.matmul(ovb[:, c * NS + b:c * NS + b + 1], masked[0:NS, b, c * P:(c + 1) * P],
                                   ones[0:NS, 0:1], start=False, stop=b == NS - 1)
            ins.then_inc(fin_ready, 1)

            def router(t):
                n = rows_of(t)
                pe.wait_ge(tp_free, TURN[("h2", 2 * t + 1)] + 1)
                for k in range(KD):
                    ins = T.matmul(ptb[0:n, t * 36:(t + 1) * 36], h2T[:, k, 0:n], wr[:, k, :],
                                   start=k == 0, stop=k == KD - 1)
                ins.then_inc(r_done, 1)

            def h2_turns(t):
                pe.wait_ge(h2_ready, t + 1)
                for c in range(2):
                    turns(("h2", 2 * t + c), quarter(h2n[0:rows_of(t), t % 2, :], c * 512))
                router(t)

            pe.wait_ge(tp_free, TURN[("sgu", NT - 1)] + 1)
            for t in range(NT):
                n = rows_of(t)
                for half in range(2):
                    u = UNIT[("out", 2 * t + half)]
                    free_wait(pe, u)
                    pe.wait_ge(w_loaded[5 + half], 16)
                    if t == NT - 1:
                        pe.wait_ge(fin_copied, 1)
                    for k in range(KD):
                        ins = T.matmul(acc[u % 2][0:n, :], hT[:, k, t * P:t * P + n], wg[:, (5 + half) % 2, k, :],
                                       start=k == 0, stop=k == KD - 1)
                    ins.then_inc(acc_ready, 1)
                if t >= 1:
                    h2_turns(t - 1)
            h2_turns(NT - 1)
            pe.wait_ge(picks, 1)
            left(pe, ("out", 2 * NT - 1))
            for t in range(NT):
                n = rows_of(t)
                out = acc[0][:, t * NE:(t + 1) * NE]
                for e in range(t):
                    T.matmul(out, ones[:, :], M[:, e, :], start=e == 0, stop=False)
                ins = T.matmul(out, ltri[0:n, :], M[0:n, t, :], start=t == 0, stop=True)
            for t in range(NT):
                n = rows_of(t)
                ins2 = T.matmul(acc[1][:, 256:256 + NE], ones[0:n, :], M[0:n, t, :], start=t == 0, stop=t == NT - 1)
            ins.then_inc(ranks, 1)
            ins2.then_inc(cnt_ready, 1)
            for part, (a, b) in enumerate(((0, PAIRS), (PAIRS, TOTAL))):
                m = b - a
                pe.wait_ge(onehots, part + 1)
                if part == 0:
                    pe.wait_ge(tp_free, len(TURNS))
                for kt in range(2 * NT):
                    n = rows_of(kt % NT)
                    ins = T.matmul(tp[part][:, 0:2 * m], onehot_p[0:n, kt, :], val_q[0:n, kt, :, a:b],
                                   start=kt == 0, stop=kt == 2 * NT - 1)
                ins.then_inc(tabs, 1)

            def turn_x(n, b):
                pe.wait_ge(x_landed[b], gathered(n, b))
                for k in range(KD):
                    ins = T.transpose(sbk[k // 4][:, (k % 4) * P:(k % 4 + 1) * P], xg[:, b, k * P:(k + 1) * P], ident[:, :])
                ins.then_inc(turned, 1)

            def gate_up(n, j, first=False):
                b = j % 2
                pe.wait_ge(e_in[j], weights(n, j))
                pe.wait_ge(xt_copied, n + 1)
                bank = (ptb, ovb)[b]
                for e in range(2):
                    for m in range(2):
                        out = bank[:, (2 * e + m) * CAP:(2 * e + m + 1) * CAP]
                        for k in range(KD):
                            ins = T.matmul(out, ew[:, j, m, e, k * P:(k + 1) * P],
                                           xgT[:, b, k * P + e * CAP:k * P + (e + 1) * CAP],
                                           start=k == 0, stop=k == KD - 1)
                ins.then_inc(gu_done, 1)

            def down(n, j, first=False):
                b = j % 2
                pe.wait_ge(hid_done, n + 1)
                if not first:
                    pe.wait_ge(y_half_d, n - 1)
                    pe.wait_ge(y_half_a, n - 1)
                for e in range(2):
                    for half in range(2):
                        ins = T.matmul((acc, tp)[b][half][e * CAP:(e + 1) * CAP, :], hid[:, b, e * CAP:(e + 1) * CAP],
                                       ew[:, j, 2, e, half * 512:(half + 1) * 512], start=True, stop=True)
                ins.then_inc(down_done, 1)

            def work(first, last):
                turn_x(first, 0)
                if first == 0:
                    for n in range(4):
                        gate_up(n, n)
                        turn_x(n + 1, (n + 1) % 2)
                        if n == 0:
                            pe.wait_ge(flag_ready, 1)
                            pe.wait_ge(tab_ready, 2)
                        down(n, n, n < 2)
                with pe.Fori(4 if first == 0 else first, last - 7, 4) as i:
                    for j in range(4):
                        gate_up(i + j, j)
                        turn_x(i + (j + 1), (j + 1) % 2)
                        down(i + j, j)
                for j in range(4):
                    gate_up(last - 4 + j, j)
                    if j < 3:
                        turn_x(last - 3 + j, (j + 1) % 2)
                    down(last - 4 + j, j)

            work(0, PAIRS)
            more = pe.value_load(flag[0:1, 0:1], min_val=0, max_val=1)
            with pe.If(more > 0):
                work(PAIRS, TOTAL)


def scattered(n, b):
    return (n - b) * 8


def gathered(n, b):
    return (n - b) * 8 + 16


def weights(n, j):
    return (n - j) * 12 + 48


def kernel(**inputs):
    import concourse.bacc as bacc
    from concourse.bass_utils import run_bass_kernel_spmd

    a = {k: np.asarray(v) for k, v in inputs.items()}
    sgu_w = a["sgu_w"][0]
    feeds = {
        "x_prompt": a["x_prompt"], "x_sample": a["x_sample"],
        "cache_win_k": a["cache_win_k"], "cache_win_v": a["cache_win_v"],
        "ln1_g": a["ln1_g"].reshape(-1), "w_in": a["w_in"],
        "sgu_norm_g": a["sgu_norm_g"].reshape(-1),
        "sgu_wt": sgu_w.transpose(2, 0, 1), "sgu_w00": sgu_w[:, 0, 0],
        "sgu_bt": a["sgu_b"][0].T, "sgu_b0": a["sgu_b"][0, :, 0],
        "w_out": a["w_out"], "ln2_g": a["ln2_g"].reshape(-1),
        "w_router": np.concatenate([a["w_router_group"][0], a["w_router_expert"][0]], 1).reshape(P, KD, NG + NE),
        "b_router": np.concatenate([a["b_router_group"][0], a["b_router_expert"][0]]),
        "w_gate": a["w_gate"], "w_up": a["w_up"], "w_down": a["w_down"], "lnf_g": a["lnf_g"],
        "const": constants(),
    }
    outs = [("y_prompt", (1, SEQ, D)), ("y_sample", (NS, 1, D)),
            ("k_prompt", (1, 1, SEQ, HEADS, HD)), ("v_prompt", (1, 1, SEQ, HEADS, HD)),
            ("k_sample", (1, NS, 1, HEADS, HD)), ("v_sample", (1, NS, 1, HEADS, HD)),
            ("sgu_v_sample", (1, NS, 1, HEADS, HD))]
    nc = bacc.Bacc("TRN2", target_bir_lowering=False, num_devices=1)
    arrays, args = {}, []
    for name, v in feeds.items():
        v = np.ascontiguousarray(v)
        arrays["in_" + name] = v
        args.append(nc.dram_tensor("in_" + name, v.shape, mybir.dt.from_np(v.dtype), kind="ExternalInput").ap())
    for name, shape in outs:
        args.append(nc.dram_tensor("out_" + name, shape, F32, kind="ExternalOutput").ap())
    build(nc, *args)
    r = run_bass_kernel_spmd(nc, [arrays], core_ids=[0])
    return tuple(r.results[0]["out_" + name] for name, _ in outs)
```

```python
from contextlib import ExitStack

import numpy as np

import concourse.bass as bass
from concourse import mybir

F32 = mybir.dt.float32
I32 = mybir.dt.int32
F16 = mybir.dt.float16
ALU = mybir.AluOpType
ACT = mybir.ActivationFunctionType
AX = mybir.AxisListType.X

P = 128
D = 1024
KD = D // P
SEQ = 512
NS = 8
NT = SEQ // P + 1
HEADS, HD = 8, 64
W = HEADS * HD
PAST = 2048
DILATIONS = (1, 4, 16)
NPAT = len(DILATIONS)
NG, EPG = 4, 8
NE = NG * EPG
FE = 128
CAP = 64
PAIRS = NE // 2
ROUNDS = -(-(SEQ + NS) // CAP)
TOTAL = ROUNDS * PAIRS
ROWS = SEQ + NS
EPS = 1e-6
SCALE = HD ** -0.5
NEG = -1e30
FAR = 1.0e6

C_IDENT = 0
C_MASK = C_IDENT + P
C_ROPE = C_MASK + 4 * P
C_LTRI = C_ROPE + 2 * NT * HD
C_IOTA = C_LTRI + P
C_M100 = C_IOTA + TOTAL
C_ECODE = C_M100 + EPG
C_VAL = C_ECODE + NE
C_HM = C_VAL + 4 * NT
C_BIND = C_HM + HEADS
C_BINDT = C_BIND + NS
C_VALID = C_BINDT + NS * HEADS
C_END = C_VALID + 1


def rows_of(t):
    return P if t < NT - 1 else NS


def constants():
    c = np.zeros((P, C_END), np.float32)
    r = np.arange(P)
    c[:, C_IDENT:C_IDENT + P] = np.eye(P)
    for j in range(4):
        delta = (3 - j) * P + r[:, None] - r[None, :]
        count = ((delta >= 0) & (delta <= P)).astype(int)
        for dil in DILATIONS[1:]:
            count += (delta >= 0) & (delta % dil == 0)
        c[:, C_MASK + j * P:C_MASK + (j + 1) * P] = np.where(
            count > 0, np.log(np.maximum(count, 1)) / SCALE, NEG)
    inv = (np.float32(10000.0) ** (-np.arange(HD // 2, dtype=np.float32) * np.float32(2.0) / np.float32(HD))).astype(np.float32)
    for t in range(NT):
        pos = (t * P + r if t < NT - 1 else np.full(P, PAST)).astype(np.float32)
        ang = (pos[:, None] * inv[None, :]).astype(np.float32).astype(np.float64)
        at = C_ROPE + t * HD
        c[:, at:at + HD] = np.concatenate([np.cos(ang), np.cos(ang)], 1)
        at += NT * HD
        c[:, at:at + HD] = np.concatenate([-np.sin(ang), np.sin(ang)], 1)
    c[:, C_LTRI:C_LTRI + P] = r[:, None] < r[None, :]
    c[:, C_IOTA:C_IOTA + TOTAL] = np.arange(TOTAL)
    c[:, C_M100:C_M100 + EPG] = np.arange(EPG) - 100
    c[:, C_ECODE:C_ECODE + NE] = 1024 * np.arange(NE)
    for k in range(2):
        for t in range(NT):
            at = C_VAL + 2 * (k * NT + t)
            c[:, at] = t * P + r + 1
            c[:, at + 1] = k * ROWS + t * P + r + 1
    bh = np.arange(NS * HEADS)
    c[bh, C_HM + bh % HEADS] = 1
    c[bh, C_BIND + bh // HEADS] = 1
    c[bh // HEADS, C_BINDT + bh] = 1
    c[:NS, C_VALID] = 1
    return c


TILES = range(NT)
UNITS = [(_kind, t) for _kind in ("q", "k", "va", "v", "u") for t in TILES]
UNITS += [("mix", j) for j in range(4)]
UNITS += [("out", 2 * t + h) for t in TILES for h in range(2)]
UNIT = {u: n for n, u in enumerate(UNITS)}
BY_SCALAR = ("v", "u")
GROUP_AT = {"u": 0, "va": W, "q": 2 * W, "k": 3 * W, "v": 4 * W}
W_ORDER = ["q", "k", "va", "v", "u"]


def evacuated(n):
    scalar = UNITS[n][0] in BY_SCALAR
    return scalar, sum((u[0] in BY_SCALAR) == scalar for u in UNITS[:n + 1])


TURNS = [("h", 2 * t + c) for t in range(NT) for c in range(2)]
TURNS += [("q", t) for t in range(NT - 1)] + [("k", t) for t in range(NT - 1)]
TURNS += [("att", t) for t in range(NT - 1)] + [("sgu", t) for t in range(NT)]
TURNS += [("h2", 2 * t + c) for t in range(NT) for c in range(2)]
TURN = {u: n for n, u in enumerate(TURNS)}

LAST_ORDER = [NT - 1] + list(range(NT - 1))
TASKS = [(i, h) for i in range(4) for h in range(HEADS)]
FILL = []
for _kind, _t in [("v", 1), ("v", 2), ("v", 3), ("v", 4), ("pv", 0), ("pv", 1), ("u", 0), ("pv", 2), ("pv", 3),
                  ("u", 1), ("pv", 4), ("pv", 5), ("u", 2), ("pv", 6), ("u", 3), ("pv", 7), ("u", 4)]:
    FILL += [(_kind, _t, part) for part in range(NPAT if _kind == "pv" else KD)]


def fill_of(n):
    return FILL[len(FILL) * n // len(TASKS):len(FILL) * (n + 1) // len(TASKS)]


def finished_in(n):
    return [(kind, t) for kind, t, part in fill_of(n) if kind != "pv" and part == KD - 1]


def build(nc, x_prompt, x_sample, cache_k, cache_v, ln1_g, w_in, sgu_g, sgu_wt, sgu_w, sgu_bt, sgu_b,
          w_out, ln2_g, w_router, b_router, w_gate, w_up, w_down, lnf_g, const,
          y_prompt, y_sample, k_prompt, v_prompt, k_sample, v_sample, sgu_v_sample):
    h2_dram = nc.dram_tensor("h2_rows", (ROWS, D), F32, kind="Internal").ap()
    q_dram = nc.dram_tensor("sample_q", (NS, W), F32, kind="Internal").ap()
    y2_dram = nc.dram_tensor("expert_rows", (2 * ROWS, D), F32, kind="Internal").ap()

    with ExitStack() as ctx:
        def sb(name, shape, dt=F32):
            return ctx.enter_context(nc.sbuf_tensor(name, shape, dt))

        def sem(name):
            return ctx.enter_context(nc.semaphore(name))

        x = sb("x", [P, NT, D])
        hT = sb("hT", [P, KD, SEQ + NS])
        wring = sb("wring", [P, 2, KD * W])
        att = sb("att", [P, 4096])
        vring = sb("vring", [P, 3072])
        h2T = sb("h2T", [P, KD, P])
        gain = sb("gain", [P, D])
        gv = sb("gv", [P, 512])
        big = sb("big", [P, 4 * 6144])
        ident = sb("ident", [P, P])
        ones = sb("ones", [P, P])
        ltri = sb("ltri", [P, P])
        iota = sb("iota", [P, TOTAL])
        small = sb("small", [P, EPG + NE + 4 * NT + HEADS + NS + NS * HEADS + 1])
        sT = sb("sT", [P, NPAT, NS * HEADS])
        wr = sb("wr", [P, KD, NG + NE])
        rbias = sb("rbias", [P, NG + NE])
        negm = sb("negm", [P, 32])
        den = sb("den", [P, 32])
        stat = sb("stat", [P, 72])
        epsc = sb("epsc", [P, 1])
        flag = sb("flag", [P, 1], I32)

        def cut(base, at, *shape):
            n = int(np.prod(shape))
            v = base[:, at:at + n]
            if len(shape) == 2:
                return v.rearrange("p (a b) -> p a b", a=shape[0])
            if len(shape) == 3:
                return v.rearrange("p (a b c) -> p a b c", a=shape[0], b=shape[1])
            return v

        m100 = small[:, 0:EPG]
        ecode = small[:, EPG:EPG + NE]
        o = EPG + NE
        val = small[:, o:o + 4 * NT].rearrange("p (a v) -> p a v", v=2)
        o += 4 * NT
        hm, bind = small[0:NS * HEADS, o:o + HEADS], small[0:NS * HEADS, o + HEADS:o + HEADS + NS]
        bindT = small[0:NS, o + HEADS + NS:o + HEADS + NS + NS * HEADS]
        in_samples = small[:, o + HEADS + NS + NS * HEADS:]

        qT = cut(big, 0, 4, SEQ)
        kT = cut(big, 2048, 4, SEQ)
        mask = cut(big, 4096, 512)
        qn = cut(big, 4608, 2, W)
        qs = cut(big, 5632, W)
        kn = cut(big, 6144, NT, W)
        vn = cut(big, 8704, NT, W)
        kring = cut(big, 11264, 2, NPAT, W)
        prod = cut(big, 14336, NPAT, W)
        ptm = cut(big, 11264, NPAT, NS, NS * HEADS)
        masked = cut(big, 12800, W)[0:NS * HEADS]
        diag = cut(big, 13312, NS * HEADS)[0:NS * HEADS]
        own = cut(big, 13376, NS * HEADS)[0:NS]
        attn = cut(big, 15872, 4, W)
        sqt = cut(big, 17920, W)
        hbuf = cut(big, 15872, 2, D)
        vv = cut(big, 18432, NT, W)
        uu = cut(big, 20992, NT, W)
        cos = cut(big, 23552, NT, HD)
        sin = cut(big, 23552 + NT * HD, NT, HD)
        bcol = cut(big, 24192, HEADS)
        w00 = cut(big, 24200, HEADS)[0:NS]
        b0 = cut(big, 24208, HEADS)[0:NS]
        ew = big[:, :].rearrange("p (s m e n) -> p s m e n", s=4, m=3, e=2)

        wg = wring[:, :, :].rearrange("p s (k n) -> p s k n", k=KD)
        wflat = wring[:, :, :].rearrange("p s n -> p (s n)")
        hflat = hT[:, :, :].rearrange("p k n -> p (k n)")
        once = wflat[:, 0:6144].rearrange("p (m e n) -> p m e n", m=3, e=2)
        places = [ew[:, slot] for slot in range(4)] + [once]
        yrow = cut(wflat, 6144, 2, D)
        xg = cut(hflat, 0, 2, D)
        xgT = cut(hflat, 2048, 2, KD * P)
        sg = cut(vring, 2048, 2, 2 * CAP)
        hid = cut(vring, 2304, 2, 2 * CAP)
        idxg = vring[:, 2560:2562].bitcast(I32)
        idxs = vring[:, 2562:2564].bitcast(I32)

        s_sb = cut(att, 0, 2, 512)
        p_sb = cut(att, 1024, 2, 512)
        pt_sb = cut(att, 2048, 2, 512)
        qb = cut(att, 3072, 2, 512)
        rtmp = cut(att, 0, W)
        vr = cut(vring, 0, 2, NPAT, W)
        h2n = cut(vring, 0, 2, D)
        wt = h2T
        gvb = gv[:, 0:W]
        sall = gv[0:NS * HEADS, 0:NPAT * P + 1]

        at = [0]

        def route(*shape):
            n = int(np.prod(shape))
            v = cut(att, at[0], *shape)
            at[0] += n
            return v

        onehot_p = route(NT * P).bitcast(F16).rearrange("p (a b) -> p a b", a=2 * NT)
        L = route(NT, NG + NE)
        gmax, gsum, gp = route(NT), route(NT), route(NT)
        ge = route(NT, NG)
        gpick = route(NT, NG)
        gidx = route(NT)
        lmul = route(NT, NE)
        sel = route(NT, EPG)
        sel2 = route(NT, EPG)
        pickt = route(NT, EPG)
        m12 = route(2, NT)
        i12 = route(2, NT)
        o12 = route(2 * NT, EPG)
        ex = route(NT)
        gates = route(2, NT)
        O = route(2, NT, NE)
        M = route(NT, NE)
        X = route(NT, NE)
        OX = route(2 * NT, NE)
        rk, rm, r1, r2, r3, r4, rk2, rk3 = [route(2 * NT) for _ in range(8)]
        table = route(2 * TOTAL)
        tabtmp = route(2 * PAIRS * (ROUNDS - 1))
        assert at[0] <= 4096
        tab = table.bitcast(I32)
        val_q = cut(vring[:, :].bitcast(F16), 0, 2 * NT, 2, TOTAL)

        banks = [ctx.enter_context(nc.psum_tensor(f"bank{i}", [P, 512], F32)) for i in range(8)]
        acc, tp, sbk, ptb, ovb = banks[0:2], banks[2:4], banks[4:6], banks[6], banks[7]

        x_in = [sem(f"x_in{t}") for t in range(NT)]
        gain_in = sem("gain_in")
        ident_in, rope_in, mask_in, consts_in, gv_in, wt_in, wt_mask = [
            sem(n) for n in ("ident_in", "rope_in", "mask_in", "consts_in", "gv_in", "wt_in", "wt_masked")]
        w_loaded = [sem(f"w_loaded{i}") for i in range(7)]
        kq_in = [sem(f"keys_and_q_in{i}") for i in range(2)]
        q_stored = sem("q_stored")
        v_in = [sem(f"v_in{i}") for i in range(2)]
        squares, h_ready = sem("squares"), sem("h_ready")
        tp_ready, tp_free = sem("tp_ready"), sem("tp_free")
        acc_ready, free_d, free_a = sem("acc_ready"), sem("acc_free_vector"), sem("acc_free_scalar")
        q_ready, k_ready = sem("q_ready"), sem("k_ready")
        s_ready, masked_s, exp_done, p_turned, pt_copied, pv_done, o_done = [
            sem(n) for n in ("s_ready", "masked_s", "exp_done", "p_turned", "pt_copied", "pv_done", "o_done")]
        ones_set, eps_set, rooted = sem("ones_set"), sem("eps_set"), sem("rooted")
        prods, sums = sem("prods"), sem("sums")
        self_s, st_ready, sall_ready, sexp, sp_ready, stb_ready, ptm_zeroed, ptm_ready, sample_pv, heads_masked, fin_ready, fin_copied = [
            sem(n) for n in ("self_s", "st_ready", "sall_ready", "sexp", "sp_ready", "stb_ready", "ptm_zeroed", "ptm_ready",
                             "sample_pv", "heads_masked", "fin_ready", "fin_copied")]
        va_ready, sgu_s_ready = sem("va_ready"), sem("sgu_s_ready")
        sq2, h2_ready, r_done = sem("sq2"), sem("h2_ready"), sem("router_done")
        h2w = [sem(f"h2_written{t}") for t in range(NT)]
        dv, dv_more = sem("vector_step"), sem("vector_step_more_rounds")
        gexp_in, gexp, eexp_in, eexp = sem("gexp_in"), sem("gexp"), sem("eexp_in"), sem("eexp")
        picks, ranks, onehots, tabs, tab_ready, flag_ready, cnt_ready = [
            sem(n) for n in ("picks", "ranks", "onehots", "tabs", "tab_ready", "flag_ready", "cnt_ready")]
        zeroed = sem("zeroed")
        gu_in = [sem(f"gate_up_in{i}") for i in range(5)]
        down_in = [sem(f"down_in{i}") for i in range(5)]
        gidx_copied, sidx_copied = sem("gidx_copied"), sem("sidx_copied")
        x_landed = [sem(f"x_landed{i}") for i in range(2)]
        y_landed = [sem(f"y_landed{i}") for i in range(2)]
        turned, xt_copied, gu_done, silu_done, hid_done, down_done, y_half_d, y_half_a = [
            sem(n) for n in ("turned", "xt_copied", "gate_up_done", "silu_done", "hid_done", "down_done", "y_half_d", "y_half_a")]
        rows_ready, out_k, out_v, out_s, y_out = sem("rows_ready"), sem("out_k"), sem("out_v"), sem("out_s"), sem("y_out")
        rows_in = [sem(f"rows_in{t}") for t in range(NT)]
        mixed, sq3, y_ready = sem("mixed"), sem("sq3"), sem("y_ready")

        xp = x_prompt.rearrange("a (t p) d -> (a t) p d", p=P)
        xs = x_sample.rearrange("b a d -> (b a) d")
        w_in_v = w_in.rearrange("a (k p) n -> (a p) k n", p=P)
        w_out_v = w_out.rearrange("a (k p) n -> (a p) k n", p=P)
        gate_v = [w[0].rearrange("e (p k) f -> p e (k f)", k=KD) for w in (w_gate, w_up)]
        down_v = w_down[0].rearrange("e p n -> p e n")
        yp = y_prompt.rearrange("a (t p) d -> (a t) p d", p=P)
        ys = y_sample.rearrange("b a d -> (b a) d")

        def free_wait(eng, n):
            if n >= 2:
                scalar, count = evacuated(n - 2)
                eng.wait_ge(free_a if scalar else free_d, count)

        def left(eng, unit):
            scalar, count = evacuated(UNIT[unit])
            eng.wait_ge(free_a if scalar else free_d, count)

        def bcast_rows(src, rows=P):
            return src.partition_broadcast(rows)

        def gate_up_loads(sp, slot, pair):
            for m in range(2):
                sp.dma_start(places[slot][:, m], gate_v[m][:, bass.ds(pair, 2), :]).then_inc(gu_in[slot], 16)

        def down_load(sp, slot, pair):
            sp.dma_start(places[slot][:, 2], down_v[:, bass.ds(pair, 2), :]).then_inc(down_in[slot], 16)

        block = ctx.enter_context(nc.Block())

        @block.sync
        def _(sp):
            sp.dma_start(x[:, 0, :], xp[0]).then_inc(x_in[0], 16)
            for t in range(1, NT - 1):
                sp.dma_start(x[:, t, :], xp[t]).then_inc(x_in[t], 16)
            sp.dma_start(x[0:NS, NT - 1, :], xs).then_inc(x_in[NT - 1], 16)

            def load_w(n):
                if 2 <= n:
                    sp.wait_ge(acc_ready, UNIT[(W_ORDER[n - 2], NT - 1)] + 1)
                dst = wg[:, n % 2]
                if n < 5:
                    at = GROUP_AT[W_ORDER[n]]
                    src = w_in_v[:, :, at:at + W]
                else:
                    src = w_out_v[:, :, (n - 5) * W:(n - 4) * W]
                sp.dma_start(dst, src).then_inc(w_loaded[n], 16)

            def load_k(b):
                if b >= 2:
                    sp.wait_ge(prods, b - 1)
                for p_, dil in enumerate(DILATIONS):
                    src = cache_k[0, b, PAST - P * dil:PAST:dil].rearrange("j h d -> j (h d)")
                    sp.dma_start(kring[:, b % 2, p_, :], src).then_inc(kq_in[b % 2], 16)

            def load_q(b):
                sp.dma_start(qb[:, b % 2, :], q_dram[b].partition_broadcast(P)).then_inc(kq_in[b % 2], 16)

            def load_v(b):
                if b >= 2:
                    sp.wait_ge(sample_pv, b - 1)
                for p_, dil in enumerate(DILATIONS):
                    src = cache_v[0, b, PAST - P * dil:PAST:dil].rearrange("j h d -> j (h d)")
                    sp.dma_start(vr[:, b % 2, p_, :], src).then_inc(v_in[b % 2], 16)

            load_w(0)
            sp.dma_start(cos[:, :, :], const[:, C_ROPE:C_ROPE + NT * HD].rearrange("p (t n) -> p t n", t=NT)).then_inc(rope_in, 16)
            sp.dma_start(sin[:, :, :], const[:, C_ROPE + NT * HD:C_LTRI].rearrange("p (t n) -> p t n", t=NT)).then_inc(rope_in, 16)
            load_w(1)
            load_k(0)
            load_k(1)
            sp.dma_start(gvb, sgu_g.partition_broadcast(P)).then_inc(gv_in, 16)
            sp.dma_start(mask, const[:, C_MASK:C_MASK + 4 * P]).then_inc(mask_in, 16)
            sp.dma_start(wt[:, :, :], sgu_wt).then_inc(wt_in, 16)
            sp.dma_start(ltri[:, :], const[:, C_LTRI:C_LTRI + P]).then_inc(consts_in, 16)
            sp.dma_start(iota[:, :], const[:, C_IOTA:C_IOTA + TOTAL]).then_inc(consts_in, 16)
            sp.dma_start(small[:, :], const[:, C_M100:C_END]).then_inc(consts_in, 16)
            sp.dma_start(wr[:, :, :], w_router).then_inc(consts_in, 16)
            sp.dma_start(rbias[:, :], b_router.partition_broadcast(P)).then_inc(consts_in, 16)
            sp.dma_start(bcol[:, :], sgu_bt).then_inc(consts_in, 16)
            sp.dma_start(w00[:, :], sgu_w.partition_broadcast(NS)).then_inc(consts_in, 16)
            sp.dma_start(b0[:, :], sgu_b.partition_broadcast(NS)).then_inc(consts_in, 16)
            load_w(2)
            sp.wait_ge(q_ready, NT)
            sp.dma_start(q_dram, qs[0:NS]).then_inc(q_stored, 16)
            sp.wait_ge(q_stored, 16)
            load_q(0)
            load_q(1)
            for b in range(2, NS):
                if b == 6:
                    load_w(3)
                load_k(b)
                load_q(b)
            load_v(0)
            load_v(1)
            load_w(4)
            load_w(5)
            for b in range(2, NS):
                load_v(b)
            load_w(6)
            sp.wait_ge(masked_s, len(TASKS))
            sp.wait_ge(s_ready, len(TASKS))
            sp.wait_ge(self_s, 1)
            sp.wait_ge(prods, NS)
            gate_up_loads(sp, 0, 0)
            down_load(sp, 0, 0)
            sp.wait_ge(sums, NS)
            sp.wait_ge(acc_ready, UNIT[("mix", 3)] + 1)
            sp.wait_ge(sgu_s_ready, 1)
            sp.wait_ge(tp_ready, TURN[("sgu", NT - 1)] + 1)
            sp.wait_ge(out_k, 32)
            sp.wait_ge(out_s, 16)
            sp.wait_ge(fin_ready, 1)
            gate_up_loads(sp, 1, 2)
            down_load(sp, 1, 2)
            gate_up_loads(sp, 2, 4)
            down_load(sp, 2, 4)
            sp.wait_ge(out_v, 32)
            gate_up_loads(sp, 3, 6)
            down_load(sp, 3, 6)
            sp.wait_ge(acc_ready, UNIT[("out", 2 * NT - 1)] + 1)
            gate_up_loads(sp, 4, 8)
            down_load(sp, 4, 8)
            for n in range(5, PAIRS):
                used = n - 4 if n < 9 else n - 3
                sp.wait_ge(gu_done, used)
                gate_up_loads(sp, (n - 1) % 4, 2 * n)
                sp.wait_ge(down_done, used)
                down_load(sp, (n - 1) % 4, 2 * n)
            sp.wait_ge(flag_ready, 1)
            more = sp.value_load(flag[0:1, 0:1], min_val=0, max_val=1)
            with sp.If(more > 0):
                with sp.Fori(PAIRS, TOTAL - PAIRS + 1, PAIRS) as r:
                    with sp.Fori(0, PAIRS - 3, 4) as i:
                        for j in range(4):
                            sp.wait_ge(gu_done, r + i + (j - 3))
                            gate_up_loads(sp, (j + 3) % 4, i * 2 + 2 * j)
                            sp.wait_ge(down_done, r + i + (j - 3))
                            down_load(sp, (j + 3) % 4, i * 2 + 2 * j)
            sp.wait_ge(rows_ready, 1)
            rows = big[:, 0:2 * NT * D].rearrange("p (t k n) -> p t k n", t=NT, k=2)
            for t in LAST_ORDER:
                n = rows_of(t)
                for k in range(2):
                    at = k * ROWS + t * P
                    sp.dma_start(rows[0:n, t, k], y2_dram[at:at + n, :]).then_inc(rows_in[t], 16)
            for i, t in enumerate(LAST_ORDER):
                sp.wait_ge(y_ready, i + 1)
                sp.dma_start(yp[t] if t < NT - 1 else ys, x[0:rows_of(t), t, :]).then_inc(y_out, 16)
            sp.wait_ge(y_out, 16 * NT)

        @block.gpsimd
        def _(pool):
            nc.gpsimd.memset(epsc[:], EPS).then_inc(eps_set, 1)
            nc.gpsimd.memset(ones[:], 1.0).then_inc(ones_set, 1)
            pool.wait_ge(wt_in, 16)
            nc.gpsimd.affine_select(out=wt[:, :, :], in_=wt[:, :, :], compare_op=ALU.is_ge, fill=0.0, base=0,
                                    pattern=[[0, HEADS], [1, P]], channel_multiplier=-1).then_inc(wt_mask, 1)
            kp = k_prompt.rearrange("a b (t p) h d -> (a b p) t (h d)", p=P)
            vp = v_prompt.rearrange("a b (t p) h d -> (a b p) t (h d)", p=P)
            for b in range(NS):
                if b == 3:
                    pool.wait_ge(k_ready, NT)
                    pool.dma_start(kp, kn[:, 0:4, :]).then_inc(out_k, 16)
                    pool.dma_start(k_sample.rearrange("a b t h d -> (a b t) (h d)"), kn[0:NS, 4, :]).then_inc(out_k, 16)
                pool.wait_ge(kq_in[b % 2], 64 * (b // 2 + 1))
                if b >= 1:
                    pool.wait_ge(sums, b)
                nc.gpsimd.tensor_tensor(
                    prod[:, :, :], kring[:, b % 2],
                    qb[:, b % 2, :].unsqueeze(1).to_broadcast([P, NPAT, W]), ALU.mult).then_inc(prods, 1)
            pool.wait_ge(prods, NS)
            nc.gpsimd.memset(ptm[:, :, :, :], 0.0).then_inc(ptm_zeroed, 1)
            pool.wait_ge(va_ready, NT)
            pool.dma_start(sgu_v_sample.rearrange("a b t h d -> (a b t) (h d)"), vn[0:NS, 4, :]).then_inc(out_s, 16)
            left(pool, ("v", NT - 1))
            pool.dma_start(vp, vv[:, 0:4, :]).then_inc(out_v, 16)
            pool.dma_start(v_sample.rearrange("a b t h d -> (a b t) (h d)"), vv[0:NS, 4, :]).then_inc(out_v, 16)
            for t in range(NT):
                pool.wait_ge(h2_ready, t + 1)
                pool.dma_start(h2_dram[t * P:t * P + rows_of(t), :], h2n[0:rows_of(t), t % 2, :]).then_inc(h2w[t], 16)
            pool.wait_ge(acc_ready, UNIT[("out", 2 * NT - 1)] + 1)
            nc.gpsimd.memset(xg[:, :, :], 0.0).then_inc(zeroed, 1)
            pool.wait_ge(zeroed, 1)
            for t in range(NT):
                pool.wait_ge(h2w[t], 16)
            pool.wait_ge(tab_ready, 1)

            def gather(n, b, first=False):
                if not first:
                    pool.wait_ge(turned, n - 1)
                nc.gpsimd.tensor_copy(idxg[:, b:b + 1], tab[:, bass.ds(n, 1)]).then_inc(gidx_copied, 1)
                pool.wait_ge(gidx_copied, n + 1)
                nc.gpsimd.indirect_dma_start(
                    out=xg[:, b, :], out_offset=None, in_=h2_dram,
                    in_offset=bass.IndirectOffsetOnAxis(ap=idxg[:, b:b + 1], axis=0),
                    bounds_check=n + (ROWS - 1), oob_is_err=False).then_inc(x_landed[b], 16)

            def scatter(n, b):
                pool.wait_ge(y_half_d, n + 1)
                pool.wait_ge(y_half_a, n + 1)
                nc.gpsimd.tensor_copy(idxs[:, b:b + 1], tab[:, bass.ds(n + TOTAL, 1)]).then_inc(sidx_copied, 1)
                pool.wait_ge(sidx_copied, n + 1)
                nc.gpsimd.indirect_dma_start(
                    out=y2_dram, out_offset=bass.IndirectOffsetOnAxis(ap=idxs[:, b:b + 1], axis=0),
                    in_=yrow[:, b, :], in_offset=None,
                    bounds_check=n + (2 * ROWS - 1), oob_is_err=False).then_inc(y_landed[b], 16)

            def work(first, last):
                gather(first, 0, first == 0)
                gather(first + 1, 1, first == 0)
                with pool.Fori(first, last - 7, 4) as i:
                    for j in range(4):
                        gather(i + (j + 2), j % 2)
                        scatter(i + j, j % 2)
                for n in range(last - 4, last):
                    if n + 2 < last:
                        gather(n + 2, n % 2)
                    scatter(n, n % 2)
                for b in range(2):
                    pool.wait_ge(y_landed[b], 8 * last)

            work(0, PAIRS)
            pool.wait_ge(flag_ready, 1)
            more = pool.value_load(flag[0:1, 0:1], min_val=0, max_val=1)
            with pool.If(more > 0):
                pool.wait_ge(tab_ready, 2)
                work(PAIRS, TOTAL)
            pool.drain().then_inc(rows_ready, 1)
            for s_, n_ in ((out_k, 32), (out_v, 32), (out_s, 16)):
                pool.wait_ge(s_, n_)

        @block.scalar
        def _(act):
            act.dma_start(gain[:, :], ln1_g.partition_broadcast(P)).then_inc(gain_in, 16)
            act.dma_start(ident[:, :], const[:, C_IDENT:C_IDENT + P]).then_inc(ident_in, 16)

            def turn(unit, dst):
                n = TURN[unit]
                m = dst.shape[-1]
                act.wait_ge(tp_ready, n + 1)
                src = tp[n % 2][:, 0:4 * m].rearrange("p (c m) -> p c m", c=4)
                nc.scalar.activation(dst, src, ACT.Copy).then_inc(tp_free, 1)

            def cols(t):
                return slice(t * P, t * P + rows_of(t))

            def root(sem_, count, v):
                act.wait_ge(sem_, count)
                nc.scalar.activation(v, v, ACT.Sqrt, bias=epsc[0:v.shape[0], :]).then_inc(rooted, 1)

            act.wait_ge(eps_set, 1)
            def square(t):
                act.wait_ge(x_in[t], 16)
                if t >= 2:
                    act.wait_ge(tp_ready, 2 * (t - 1))
                n = rows_of(t)
                nc.scalar.activation(hbuf[0:n, t % 2, :], x[0:n, t, :], ACT.Square, scale=D ** -0.5,
                                     accum_out=stat[0:n, t:t + 1]).then_inc(squares, 1)
                root(squares, t + 1, stat[0:n, t:t + 1])

            square(0)
            square(1)
            for t in range(NT):
                for c in range(2):
                    turn(("h", 2 * t + c), hT[:, 4 * c:4 * c + 4, cols(t)])
                if t + 2 < NT:
                    square(t + 2)
            for t in range(NT - 1):
                turn(("q", t), qT[:, :, cols(t)])

            def copy_unit(unit, dst):
                n = UNIT[unit]
                act.wait_ge(acc_ready, n + 1)
                nc.scalar.activation(dst, acc[n % 2][0:dst.shape[0], 0:W], ACT.Copy).then_inc(free_a, 1)

            for t in range(NT - 1):
                turn(("k", t), kT[:, :, cols(t)])
            def exps(n):
                width = P * (TASKS[n][0] + 1)
                act.wait_ge(masked_s, n + 1)
                if n >= 2:
                    act.wait_ge(p_turned, n - 1)
                nc.scalar.activation(p_sb[:, n % 2, 0:width], s_sb[:, n % 2, 0:width], ACT.Exp, scale=-1.0,
                                     bias=negm[:, n:n + 1], accum_out=den[:, n:n + 1]).then_inc(exp_done, 1)

            def copy_pt(n):
                width = P * (TASKS[n][0] + 1)
                act.wait_ge(p_turned, n + 1)
                if n >= 2:
                    act.wait_ge(pv_done, n - 1)
                nc.scalar.activation(pt_sb[:, n % 2, 0:width], ptb[:, 0:width], ACT.Copy).then_inc(pt_copied, 1)

            exps(0)
            copy_unit(("v", 0), vv[:, 0, :])
            for n in range(len(TASKS)):
                copy_pt(n)
                if n + 1 < len(TASKS):
                    exps(n + 1)
                for kind, t in finished_in(n):
                    copy_unit((kind, t), (vv if kind == "v" else uu)[0:rows_of(t), t, :])
                if n == 2:
                    act.wait_ge(sall_ready, 1)
                    nc.scalar.activation(sall, sall, ACT.Exp, bias=stat[0:64, 11:12],
                                         accum_out=stat[0:64, 12:13]).then_inc(sexp, 1)
            for t in range(NT - 1):
                turn(("att", t), hT[:, 4:8, cols(t)])
            for t in range(NT):
                turn(("sgu", t), hT[:, 0:4, cols(t)])
            act.wait_ge(fin_ready, 1)
            nc.scalar.activation(hT[:, 4:8, cols(NT - 1)], ovb[:, 0:4 * NS].rearrange("p (c b) -> p c b", c=4),
                                 ACT.Copy).then_inc(fin_copied, 1)
            act.wait_ge(h_ready, NT)
            act.dma_start(gain[:, :], ln2_g.partition_broadcast(P)).then_inc(gain_in, 16)

            def square2(t):
                n = rows_of(t)
                left(act, ("out", 2 * t + 1))
                act.wait_ge(sample_pv, NS)
                if t >= 2:
                    act.wait_ge(h2w[t - 2], 16)
                    act.wait_ge(tp_ready, TURN[("h2", 2 * (t - 2) + 1)] + 1)
                nc.scalar.activation(h2n[0:n, t % 2, :], x[0:n, t, :], ACT.Square, scale=D ** -0.5,
                                     accum_out=stat[0:n, 16 + t:17 + t]).then_inc(sq2, 1)
                root(sq2, t + 1, stat[0:n, 16 + t:17 + t])

            def turn_h2(t):
                if t >= 1:
                    act.wait_ge(r_done, t)
                else:
                    act.wait_ge(acc_ready, UNIT[("mix", 3)] + 1)
                for c in range(2):
                    turn(("h2", 2 * t + c), h2T[:, 4 * c:4 * c + 4, 0:rows_of(t)])

            for t in range(NT):
                square2(t)
                turn_h2(t)
            act.wait_ge(gexp_in, 1)
            nc.scalar.activation(ge, ge, ACT.Exp).then_inc(gexp, 1)
            act.wait_ge(eexp_in, 1)
            nc.scalar.activation(ex, ex, ACT.Exp).then_inc(eexp, 1)
            act.wait_ge(h2_ready, NT)
            act.dma_start(gain[:, :], lnf_g.partition_broadcast(P)).then_inc(gain_in, 16)

            def copy_xt(n, b):
                act.wait_ge(turned, n + 1)
                for c in range(2):
                    last = nc.scalar.activation(xgT[:, b, c * 512:(c + 1) * 512], sbk[c][:, :], ACT.Copy)
                last.then_inc(xt_copied, 1)

            def silu(n, b):
                act.wait_ge(gu_done, n + 1)
                bank = (ptb, ovb)[b]
                src = bank[:, 0:4 * CAP].rearrange("p (e m c) -> p e m c", e=2, m=2)[:, :, 0, :]
                nc.scalar.activation(sg[:, b].rearrange("p (e c) -> p e c", e=2), src, ACT.Silu).then_inc(silu_done, 1)

            def copy_y(n, b, first=False):
                act.wait_ge(down_done, n + 1)
                if not first:
                    act.wait_ge(y_landed[b], scattered(n, b))
                bank = (acc, tp)[b]
                nc.scalar.activation(yrow[:, b, 512:1024], bank[1][:, :], ACT.Copy).then_inc(y_half_a, 1)

            def work(first, last):
                copy_xt(first, 0)
                if first == 0:
                    for n in range(4):
                        silu(n, n % 2)
                        copy_xt(n + 1, (n + 1) % 2)
                        copy_y(n, n % 2, n < 2)
                with act.Fori(4 if first == 0 else first, last - 7, 4) as i:
                    for j in range(4):
                        silu(i + j, j % 2)
                        copy_xt(i + (j + 1), (j + 1) % 2)
                        copy_y(i + j, j % 2)
                for n in range(last - 4, last):
                    silu(n, n % 2)
                    if n + 1 < last:
                        copy_xt(n + 1, (n + 1) % 2)
                    copy_y(n, n % 2)

            work(0, PAIRS)
            act.wait_ge(flag_ready, 1)
            more = act.value_load(flag[0:1, 0:1], min_val=0, max_val=1)
            with act.If(more > 0):
                work(PAIRS, TOTAL)
            for i, t in enumerate(LAST_ORDER):
                n = rows_of(t)
                act.wait_ge(mixed, i + 1)
                nc.scalar.activation(hT[0:n, :, 0:P], x[0:n, t, :].rearrange("p (k n) -> p k n", k=KD), ACT.Square, scale=D ** -0.5,
                                     accum_out=stat[0:n, 24 + t:25 + t]).then_inc(sq3, 1)
                root(sq3, i + 1, stat[0:n, 24 + t:25 + t])

        @block.vector
        def _(dve):
            steps = {dv: 0, dv_more: 0}

            def step(ins, chain=dv):
                steps[chain] += 1
                ins.then_inc(chain, 1)
                dve.wait_ge(chain, steps[chain])

            V = nc.vector

            def rsqrt(y, v, w):
                step(V.tensor_scalar(w.bitcast(I32), v.bitcast(I32), 1, None, ALU.logical_shift_right))
                step(V.tensor_scalar(y.bitcast(I32), w.bitcast(I32), -1.0, float(0x5F3759DF), ALU.mult, ALU.add))
                for _ in range(3):
                    step(V.tensor_tensor(w, y, y, ALU.mult))
                    step(V.scalar_tensor_tensor(out=w, in0=w, scalar=-0.5, in1=v, op0=ALU.mult, op1=ALU.mult))
                    step(V.scalar_tensor_tensor(out=y, in0=w, scalar=1.5, in1=y, op0=ALU.add, op1=ALU.mult))

            dve.wait_ge(gain_in, 16)
            for t in range(NT):
                n = rows_of(t)
                dve.wait_ge(rooted, t + 1)
                step(V.reciprocal(stat[0:n, 5 + t:6 + t], stat[0:n, t:t + 1]))
                V.scalar_tensor_tensor(out=hbuf[0:n, t % 2, :], in0=x[0:n, t, :], scalar=stat[0:n, 5 + t:6 + t],
                                       in1=gain[0:n, :], op0=ALU.mult, op1=ALU.mult).then_inc(h_ready, 1)

            def rope(kind, t):
                u = UNIT[(kind, t)]
                n = rows_of(t)
                dst = kn[0:n, t] if kind == "k" else (qn[0:n, t % 2] if t < NT - 1 else qs[0:n])
                z = acc[u % 2][0:n, 0:W].rearrange("p (h n) -> p h n", h=HEADS)
                d3 = dst.rearrange("p (h n) -> p h n", h=HEADS)
                t3 = rtmp[0:n].rearrange("p (h n) -> p h n", h=HEADS)
                half = HD // 2

                def tb(table, a, b):
                    return table[0:n, t, a:b].unsqueeze(1).to_broadcast([n, HEADS, b - a])
                dve.wait_ge(acc_ready, u + 1)
                if kind == "q" and 2 <= t < NT - 1:
                    dve.wait_ge(tp_ready, TURN[("q", t - 2)] + 1)
                V.tensor_tensor(d3, z, tb(cos, 0, HD), ALU.mult)
                V.tensor_tensor(t3[:, :, 0:half], z[:, :, half:HD], tb(sin, 0, half), ALU.mult)
                V.tensor_tensor(t3[:, :, half:HD], z[:, :, 0:half], tb(sin, half, HD), ALU.mult).then_inc(free_d, 1)
                dve.wait_ge(free_d, evacuated(u)[1])
                V.tensor_tensor(dst, dst, rtmp[0:n], ALU.add).then_inc(q_ready if kind == "q" else k_ready, 1)
                dve.wait_ge(q_ready if kind == "q" else k_ready, t + 1)

            def sum_prod(b):
                dve.wait_ge(prods, b + 1)
                V.tensor_reduce(sT[:, :, b * HEADS:(b + 1) * HEADS],
                                prod[:, :, :].rearrange("p a (h n) -> p a h n", h=HEADS), AX, ALU.add).then_inc(sums, 1)

            dve.wait_ge(rope_in, 32)
            for t in range(NT):
                rope("q", t)
            for t in range(NT):
                rope("k", t)
                if t >= 2:
                    sum_prod(t - 2)
            pr = rtmp[0:NS]
            step(V.tensor_tensor(pr, qs[0:NS], kn[0:NS, 4], ALU.mult))
            V.tensor_reduce(stat[0:NS, 32:40], pr.rearrange("p (h n) -> p h n", h=HEADS), AX, ALU.add).then_inc(self_s, 1)

            def add_mask(n):
                i, h = TASKS[n]
                width = P * (i + 1)
                dve.wait_ge(s_ready, n + 1)
                if n >= 2:
                    dve.wait_ge(exp_done, n - 1)
                V.tensor_tensor_reduce(out=s_sb[:, n % 2, 0:width], in0=sbk[n % 2][:, 0:width],
                                       in1=mask[:, (3 - i) * P:4 * P], scale=-SCALE, scalar=3.0e38,
                                       op0=ALU.add, op1=ALU.min, accum_out=negm[:, n:n + 1]).then_inc(masked_s, 1)

            def scale_o(n):
                i, h = TASKS[n]
                dve.wait_ge(exp_done, n + 1)
                step(V.reciprocal(den[:, n:n + 1], den[:, n:n + 1]))
                dve.wait_ge(pv_done, n + 1)
                V.tensor_scalar(attn[:, i, h * HD:(h + 1) * HD], ovb[:, 0:HD], den[:, n:n + 1], None,
                                ALU.mult).then_inc(o_done, 1)

            def va(t):
                u = UNIT[("va", t)]
                n = rows_of(t)
                z = acc[u % 2][0:n, 0:W]
                dst = vn[0:n, t]
                g3 = dst.rearrange("p (h n) -> p h n", h=HEADS)
                r8 = stat[0:n, 48:56]
                dve.wait_ge(acc_ready, u + 1)
                V.tensor_copy(dst, z).then_inc(free_d, 1)
                dve.wait_ge(free_d, evacuated(u)[1])
                step(V.scalar_tensor_tensor(out=sqt[0:n], in0=dst, scalar=1.0 / HD, in1=dst, op0=ALU.mult, op1=ALU.mult))
                step(V.tensor_reduce(r8, sqt[0:n].rearrange("p (h n) -> p h n", h=HEADS), AX, ALU.add))
                step(V.tensor_scalar(r8, r8, EPS, None, ALU.add))
                y8 = stat[0:n, 56:64]
                rsqrt(y8, r8, stat[0:n, 64:72])
                step(V.tensor_tensor(g3, g3, y8.unsqueeze(2).to_broadcast([n, HEADS, HD]), ALU.mult))
                V.tensor_tensor(dst, dst, gvb[0:n], ALU.mult).then_inc(va_ready, 1)

            dve.wait_ge(mask_in, 16)
            dve.wait_ge(gv_in, 16)
            dve.wait_ge(self_s, 1)
            add_mask(0)
            add_mask(1)
            for t in range(NT):
                va(t)
                sum_prod(3 + t)

            def g8(v):
                return v.unsqueeze(2).to_broadcast([v.shape[0], HEADS, HD])

            def h8(v):
                return v.rearrange("p (h n) -> p h n", h=HEADS)

            R = NS * HEADS

            def sample_scores():
                dve.wait_ge(st_ready, 1)
                dve.wait_ge(va_ready, NT)
                step(V.tensor_scalar(sall[:, 0:NPAT * P], tp[0][0:R, 0:NPAT * P], SCALE, None, ALU.mult))
                step(V.tensor_tensor_reduce(out=stat[0:R, 40:48], in0=tp[0][0:R, 384:392], in1=hm, scale=SCALE,
                                            scalar=0.0, op0=ALU.mult, op1=ALU.add, accum_out=stat[0:R, 10:11]))
                step(V.tensor_scalar(sall[:, NPAT * P:], stat[0:R, 10:11], float(np.log(NPAT)), None, ALU.add))
                step(V.tensor_reduce(stat[0:R, 13:14], sall, AX, ALU.max))
                V.tensor_scalar(stat[0:R, 11:12], stat[0:R, 13:14], -1.0, None, ALU.mult).then_inc(sall_ready, 1)

            def sample_probs():
                dve.wait_ge(sexp, 1)
                step(V.reciprocal(stat[0:R, 14:15], stat[0:R, 12:13]))
                step(V.tensor_scalar(sall, sall, stat[0:R, 14:15], None, ALU.mult))
                dve.wait_ge(prods, NS)
                V.tensor_scalar(diag, ident[0:R, 0:R], sall[:, NPAT * P:], None, ALU.mult).then_inc(sp_ready, 1)

            def sample_columns():
                dve.wait_ge(stb_ready, 1)
                dve.wait_ge(ptm_zeroed, 1)
                for b in range(NS):
                    cols_ = slice(b * HEADS, (b + 1) * HEADS)
                    V.tensor_copy(ptm[:, :, b, cols_],
                                  tp[1][:, 0:NPAT * R].rearrange("p (a r) -> p a r", a=NPAT)[:, :, cols_])
                V.tensor_copy(own, tp[1][0:NS, NPAT * R:(NPAT + 1) * R]).then_inc(ptm_ready, 1)

            for n in range(len(TASKS)):
                if n + 2 < len(TASKS):
                    add_mask(n + 2)
                scale_o(n)
                if n == 2:
                    dve.wait_ge(consts_in, 128)
                    sample_scores()
                if n == 4:
                    sample_probs()
                if n == 6:
                    sample_columns()
            us, vs_ = uu[0:NS, 4], vn[0:NS, 4]
            tmp8 = sqt[0:NS]
            step(V.tensor_tensor(h8(tmp8), h8(vs_), g8(w00[:, :]), ALU.mult))
            step(V.tensor_tensor(h8(tmp8), h8(tmp8), g8(b0[:, :]), ALU.add))
            left(dve, ("u", NT - 1))
            V.tensor_tensor(us, us, tmp8, ALU.mult).then_inc(sgu_s_ready, 1)

            def mix(j):
                u = UNIT[("mix", j)]
                dve.wait_ge(acc_ready, u + 1)
                for g in range(2):
                    cols_ = slice((2 * j + g) * HD, (2 * j + g + 1) * HD)
                    src = acc[u % 2][:, g * 256:(g + 1) * 256].rearrange("p (t n) -> p t n", t=4)
                    last = V.scalar_tensor_tensor(out=uu[:, 0:4, cols_], in0=src,
                                                  scalar=bcol[:, 2 * j + g:2 * j + g + 1], in1=uu[:, 0:4, cols_],
                                                  op0=ALU.add, op1=ALU.mult)
                last.then_inc(free_d, 1)

            dve.wait_ge(sample_pv, NS + 1)
            V.tensor_tensor(h8(masked), h8(tp[0][0:R, :]), g8(hm), ALU.mult).then_inc(heads_masked, 1)
            for j in range(4):
                mix(j)
            for t in range(NT):
                n = rows_of(t)
                for half in range(2):
                    u = UNIT[("out", 2 * t + half)]
                    dve.wait_ge(acc_ready, u + 1)
                    xh = x[0:n, t, half * 512:(half + 1) * 512]
                    ins = V.tensor_tensor(xh, xh, acc[u % 2][0:n, :], ALU.add)
                    ins.then_inc(free_d, 1)
                dve.wait_ge(free_d, evacuated(u)[1])
                if t == 0:
                    dve.wait_ge(gain_in, 32)
                dve.wait_ge(rooted, NT + t + 1)
                step(V.reciprocal(stat[0:n, 16 + t:17 + t], stat[0:n, 16 + t:17 + t]))
                V.scalar_tensor_tensor(
                    out=h2n[0:n, t % 2, :].rearrange("p (k q) -> p k q", k=KD),
                    in0=x[0:n, t, :].rearrange("p (q k) -> p k q", k=KD), scalar=stat[0:n, 16 + t:17 + t],
                    in1=gain[0:n, :].rearrange("p (q k) -> p k q", k=KD),
                    op0=ALU.mult, op1=ALU.mult).then_inc(h2_ready, 1)

            def over_t(v, m):
                return v.unsqueeze(2).to_broadcast([P, v.shape[1], m])

            def over_r(v, t=NT):
                return v.unsqueeze(1).to_broadcast([P, t, v.shape[1]])
            dve.wait_ge(pv_done, len(TASKS))
            step(V.memset(L[:, NT - 1, :], 0.0))
            dve.wait_ge(r_done, NT)
            lg = ptb[:, 0:NT * (NG + NE)].rearrange("p (t n) -> p t n", t=NT)
            V.tensor_tensor(L[:, 0:NT - 1, :], lg[:, 0:NT - 1, :], over_r(rbias[:, :], NT - 1), ALU.add)
            step(V.tensor_tensor(L[0:NS, NT - 1, :], lg[0:NS, NT - 1, :], rbias[0:NS, :], ALU.add))
            L4 = L[:, :, 0:NG]
            step(V.tensor_reduce(gmax, L4, AX, ALU.max))
            V.tensor_tensor(ge, L4, over_t(gmax, NG), ALU.subtract).then_inc(gexp_in, 1)
            step(V.tensor_tensor(gpick, L4, over_t(gmax, NG), ALU.is_ge))
            step(V.tensor_tensor(gpick, gpick, over_r(m100[:, 0:NG]), ALU.mult))
            step(V.tensor_reduce(gidx, gpick, AX, ALU.min))
            step(V.tensor_tensor(gpick, over_r(m100[:, 0:NG]), over_t(gidx, NG), ALU.is_equal))
            og = gpick.unsqueeze(3).to_broadcast([P, NT, NG, EPG])
            le4 = L[:, :, NG:NG + NE].rearrange("p t (g e) -> p t g e", g=NG)
            lm4 = lmul.rearrange("p t (g e) -> p t g e", g=NG)
            step(V.tensor_tensor(lm4, le4, og, ALU.mult))
            step(V.tensor_reduce(sel, lmul.rearrange("p t (g e) -> p t e g", g=NG), AX, ALU.add))
            for k, s_ in enumerate((sel, sel2)):
                ok = o12[:, k * NT:(k + 1) * NT, :]
                step(V.tensor_reduce(m12[:, k, :], s_, AX, ALU.max))
                step(V.tensor_tensor(pickt, s_, over_t(m12[:, k, :], EPG), ALU.is_ge))
                step(V.tensor_tensor(pickt, pickt, over_r(m100), ALU.mult))
                step(V.tensor_reduce(i12[:, k, :], pickt, AX, ALU.min))
                step(V.tensor_tensor(ok, over_r(m100), over_t(i12[:, k, :], EPG), ALU.is_equal))
                if k == 0:
                    step(V.scalar_tensor_tensor(out=sel2, in0=ok, scalar=NEG, in1=sel, op0=ALU.mult, op1=ALU.add))
            V.tensor_tensor(ex, m12[:, 1, :], m12[:, 0, :], ALU.subtract).then_inc(eexp_in, 1)
            for k in range(2):
                ins = V.tensor_tensor(
                    O[:, k].rearrange("p t (g e) -> p t g e", g=NG), og,
                    o12[:, k * NT:(k + 1) * NT, :].unsqueeze(2).to_broadcast([P, NT, NG, EPG]), ALU.mult)
            step(ins)
            step(V.tensor_tensor(M, O[:, 0], O[:, 1], ALU.add))
            V.tensor_scalar(M[:, NT - 1, :], M[:, NT - 1, :], in_samples, None, ALU.mult).then_inc(picks, 1)
            dve.wait_ge(gexp, 1)
            step(V.tensor_reduce(gsum, ge, AX, ALU.add))
            dve.wait_ge(eexp, 1)
            step(V.tensor_scalar(gp, ex, 1.0, None, ALU.add))
            step(V.tensor_tensor(gp, gp, gsum, ALU.mult))
            step(V.reciprocal(gates[:, 0, :], gp))
            step(V.tensor_tensor(gates[:, 1, :], gates[:, 0, :], ex, ALU.mult))
            dve.wait_ge(ranks, 1)
            pre = acc[0][:, 0:NT * NE].rearrange("p (t n) -> p t n", t=NT)
            step(V.tensor_tensor(X, pre, over_r(ecode), ALU.add))
            for k in range(2):
                ins = V.tensor_tensor(OX[:, k * NT:(k + 1) * NT, :], O[:, k], X, ALU.mult)
            step(ins)
            step(V.tensor_reduce(rk, OX, AX, ALU.add))
            xi, lo, hi, rd, pr_ = [v.bitcast(I32) for v in (rm, r2, r3, rk2, rk3)]
            step(V.tensor_copy(xi, rk))
            V.tensor_scalar(lo, xi, CAP - 1, None, ALU.bitwise_and)
            V.tensor_scalar(hi, xi, 4, CAP, ALU.logical_shift_right, ALU.bitwise_and)
            V.tensor_scalar(rd, xi, 6, 15, ALU.logical_shift_right, ALU.bitwise_and)
            step(V.tensor_scalar(pr_, xi, 11, None, ALU.logical_shift_right))
            V.tensor_tensor(r1, lo, hi, ALU.add)
            step(V.scalar_tensor_tensor(out=r4, in0=rd, scalar=float(PAIRS), in1=pr_, op0=ALU.mult, op1=ALU.add))
            dve.wait_ge(h2w[NT - 1], 16)
            dve.wait_ge(h2w[NT - 2], 16)
            V.tensor_tensor(onehot_p, over_r(iota[:, 0:P], 2 * NT), over_t(r1, P), ALU.is_equal)

            def tables(part, a, b, bank, chain):
                m = b - a
                for v in range(2):
                    ins = V.tensor_tensor(val_q[:, :, v, a:b], over_r(iota[:, a:b], 2 * NT), over_t(r4, m), ALU.is_equal)
                step(ins, chain)
                for v in range(2):
                    ins = V.tensor_tensor(val_q[:, :, v, a:b], val_q[:, :, v, a:b],
                                          val[:, :, v:v + 1].to_broadcast([P, 2 * NT, m]), ALU.mult)
                ins.then_inc(onehots, 1)
                dve.wait_ge(tabs, part + 1)
                src = bank[:, 0:2 * m].rearrange("p (v n) -> p v n", v=2)
                tt = tabtmp[:, 0:2 * m].rearrange("p (v n) -> p v n", v=2)
                step(V.tensor_scalar(tt, src, 0.0, FAR, ALU.is_equal, ALU.mult), chain)
                dst = tab.rearrange("p (v n) -> p v n", v=2)[:, :, a:b]
                V.scalar_tensor_tensor(out=dst, in0=src, scalar=-1.0, in1=tt, op0=ALU.add, op1=ALU.add).then_inc(tab_ready, 1)

            tables(0, 0, PAIRS, tp[0], dv)
            dve.wait_ge(cnt_ready, 1)
            step(V.tensor_reduce(rk[:, 0:1], acc[1][:, 256:256 + NE], AX, ALU.max))
            V.tensor_scalar(flag[:, :], rk[:, 0:1], float(CAP), None, ALU.is_gt).then_inc(flag_ready, 1)

            def hidden(n, b):
                dve.wait_ge(silu_done, n + 1)
                bank = (ptb, ovb)[b]
                up = bank[:, 0:4 * CAP].rearrange("p (e m c) -> p e m c", e=2, m=2)[:, :, 1, :]
                V.tensor_tensor(hid[:, b].rearrange("p (e c) -> p e c", e=2),
                                sg[:, b].rearrange("p (e c) -> p e c", e=2), up, ALU.mult).then_inc(hid_done, 1)

            def copy_y(n, b, first=False):
                dve.wait_ge(down_done, n + 1)
                if not first:
                    dve.wait_ge(y_landed[b], scattered(n, b))
                V.tensor_copy(yrow[:, b, 0:512], (acc, tp)[b][0][:, :]).then_inc(y_half_d, 1)

            def work(first, last):
                if first == 0:
                    for n in range(4):
                        hidden(n, n % 2)
                        copy_y(n, n % 2, n < 2)
                with dve.Fori(4 if first == 0 else first, last - 3, 4) as i:
                    for j in range(4):
                        hidden(i + j, j % 2)
                        copy_y(i + j, j % 2)

            work(0, PAIRS)
            more = dve.value_load(flag[0:1, 0:1], min_val=0, max_val=1)
            with dve.If(more > 0):
                tables(1, PAIRS, TOTAL, tp[1], dv_more)
                work(PAIRS, TOTAL)
            rows = big[:, 0:2 * NT * D].rearrange("p (t k n) -> p t k n", t=NT, k=2)
            dve.wait_ge(gain_in, 48)

            def add_rows(t):
                n = rows_of(t)
                xt = x[0:n, t, :]
                dve.wait_ge(rows_in[t], 32)
                step(V.scalar_tensor_tensor(out=xt, in0=rows[0:n, t, 0], scalar=gates[0:n, 0, t:t + 1], in1=xt,
                                            op0=ALU.mult, op1=ALU.add))
                V.scalar_tensor_tensor(out=xt, in0=rows[0:n, t, 1], scalar=gates[0:n, 1, t:t + 1], in1=xt,
                                       op0=ALU.mult, op1=ALU.add).then_inc(mixed, 1)

            def final_norm(i, t):
                n = rows_of(t)
                xt = x[0:n, t, :]
                dve.wait_ge(mixed, i + 1)
                dve.wait_ge(rooted, 2 * NT + i + 1)
                step(V.reciprocal(stat[0:n, 24 + t:25 + t], stat[0:n, 24 + t:25 + t]))
                V.scalar_tensor_tensor(out=xt, in0=xt, scalar=stat[0:n, 24 + t:25 + t], in1=gain[0:n, :],
                                       op0=ALU.mult, op1=ALU.mult).then_inc(y_ready, 1)

            add_rows(LAST_ORDER[0])
            for i in range(1, NT):
                add_rows(LAST_ORDER[i])
                final_norm(i - 1, LAST_ORDER[i - 1])
            final_norm(NT - 1, LAST_ORDER[NT - 1])

        @block.tensor
        def _(pe):
            T = nc.tensor

            def turns(unit, parts):
                n = TURN[unit]
                if n >= 2:
                    pe.wait_ge(tp_free, n - 1)
                m = parts[0].shape[0]
                for c, src in enumerate(parts):
                    ins = T.transpose(tp[n % 2][:, c * m:(c + 1) * m], src, ident[0:m, 0:m])
                ins.then_inc(tp_ready, 1)

            def quarter(rows, base=0):
                return [rows[:, base + c * P:base + (c + 1) * P] for c in range(4)]

            pe.wait_ge(ident_in, 16)

            def turn_h(t):
                pe.wait_ge(h_ready, t + 1)
                for c in range(2):
                    turns(("h", 2 * t + c), quarter(hbuf[0:rows_of(t), t % 2, :], c * 512))

            def project(unit):
                kind, t = unit
                u, n = UNIT[unit], rows_of(t)
                pe.wait_ge(w_loaded[W_ORDER.index(kind)], 16)
                pe.wait_ge(tp_free, 2 * (t + 1))
                free_wait(pe, u)
                for k in range(KD):
                    part_of(unit, k)

            def part_of(unit, k):
                kind, t = unit
                u, n = UNIT[unit], rows_of(t)
                ins = T.matmul(acc[u % 2][0:n, 0:W], hT[:, k, t * P:t * P + n],
                               wg[:, W_ORDER.index(kind) % 2, k, :], start=k == 0, stop=k == KD - 1)
                if k == KD - 1:
                    ins.then_inc(acc_ready, 1)

            def turn_qk(kind, t):
                pe.wait_ge(q_ready if kind == "q" else k_ready, t + 1)
                turns((kind, t), quarter(qn[:, t % 2] if kind == "q" else kn[:, t]))

            turn_h(0)
            turn_h(1)
            for t in range(NT):
                project(("q", t))
                if t + 2 < NT:
                    turn_h(t + 2)
                if t >= 2:
                    turn_qk("q", t - 2)
            project(("k", 0))
            turn_qk("q", NT - 2)
            for t in range(1, NT):
                project(("k", t))
                turn_qk("k", t - 1)
            def scores(n):
                i, h = TASKS[n]
                if n == 0:
                    pe.wait_ge(tp_free, TURN[("k", 3)] + 1)
                if n >= 2:
                    pe.wait_ge(masked_s, n - 1)
                r = slice(64 * (h % 2), 64 * (h % 2) + 64)
                T.matmul(sbk[n % 2][:, 0:P * (i + 1)], qT[r, h // 2, i * P:(i + 1) * P],
                         kT[r, h // 2, 0:P * (i + 1)], start=True, stop=True).then_inc(s_ready, 1)

            def turn_p(n):
                pe.wait_ge(exp_done, n + 1)
                if n >= 1:
                    pe.wait_ge(pt_copied, n)
                for j in range(TASKS[n][0] + 1):
                    ins = T.transpose(ptb[:, j * P:(j + 1) * P], p_sb[:, n % 2, j * P:(j + 1) * P], ident[:, :])
                ins.then_inc(p_turned, 1)

            def pv(n):
                i, h = TASKS[n]
                pe.wait_ge(pt_copied, n + 1)
                if h == 0:
                    left(pe, ("v", i))
                if n >= 1:
                    pe.wait_ge(o_done, n)
                for j in range(i + 1):
                    ins = T.matmul(ovb[:, 0:HD], pt_sb[:, n % 2, j * P:(j + 1) * P],
                                   vv[:, j, h * HD:(h + 1) * HD], start=j == 0, stop=j == i)
                ins.then_inc(pv_done, 1)

            R = NS * HEADS

            def turn_scores():
                pe.wait_ge(sums, NS)
                pe.wait_ge(self_s, 1)
                pe.wait_ge(consts_in, 128)
                for p_ in range(NPAT):
                    T.transpose(tp[0][0:R, p_ * P:(p_ + 1) * P], sT[:, p_, :], ident[:, :])
                T.matmul(tp[0][0:R, 384:392], bindT, stat[0:NS, 32:40], start=True, stop=True).then_inc(st_ready, 1)

            def turn_probs():
                pe.wait_ge(sp_ready, 1)
                for p_ in range(NPAT):
                    T.transpose(tp[1][:, p_ * R:(p_ + 1) * R], sall[:, p_ * P:(p_ + 1) * P], ident[0:R, 0:R])
                T.matmul(tp[1][0:NS, NPAT * R:(NPAT + 1) * R], bind, diag, start=True, stop=True).then_inc(stb_ready, 1)

            def sample_values(b, p_):
                if p_ == 0:
                    pe.wait_ge(v_in[b % 2], 48 * (b // 2 + 1))
                    if b == 0:
                        pe.wait_ge(ptm_ready, 1)
                ins = T.matmul(tp[0][0:R, :], ptm[:, p_, b, :], vr[:, b % 2, p_, :], start=b + p_ == 0, stop=False)
                if p_ == NPAT - 1:
                    ins.then_inc(sample_pv, 1)

            def fill(kind, t, part):
                if kind == "pv":
                    sample_values(t, part)
                    return
                if part == 0:
                    free_wait(pe, UNIT[(kind, t)])
                    pe.wait_ge(w_loaded[W_ORDER.index(kind)], 16)
                part_of((kind, t), part)

            scores(0)
            scores(1)
            for t in range(NT):
                project(("va", t))
            project(("v", 0))
            for n in range(len(TASKS)):
                turn_p(n)
                if n + 2 < len(TASKS):
                    scores(n + 2)
                for piece in fill_of(n):
                    fill(*piece)
                pv(n)
                if n == 2:
                    turn_scores()
                if n == 5:
                    turn_probs()
            left(pe, ("v", NT - 1))
            T.matmul(tp[0][0:R, :], own, vv[0:NS, NT - 1, :], start=False, stop=True).then_inc(sample_pv, 1)

            def mix(j):
                u = UNIT[("mix", j)]
                free_wait(pe, u)
                for g in range(2):
                    ins = T.matmul(acc[u % 2][:, g * 256:(g + 1) * 256], wt[:, 2 * j + g, :],
                                   vn[:, 0:4, (2 * j + g) * HD:(2 * j + g + 1) * HD], start=True, stop=True)
                ins.then_inc(acc_ready, 1)

            pe.wait_ge(wt_mask, 1)
            pe.wait_ge(va_ready, NT)
            for j in range(4):
                mix(j)
            pe.wait_ge(heads_masked, 1)
            pe.wait_ge(o_done, len(TASKS))
            for c in range(4):
                ins = T.matmul(ovb[:, c * NS:(c + 1) * NS], masked[:, c * P:(c + 1) * P], bind, start=True, stop=True)
            ins.then_inc(fin_ready, 1)
            for t in range(NT - 1):
                turns(("att", t), quarter(attn[:, t]))
            left(pe, ("mix", 3))
            for t in range(NT - 1):
                turns(("sgu", t), quarter(uu[:, t]))
            pe.wait_ge(sgu_s_ready, 1)
            turns(("sgu", NT - 1), quarter(uu[0:NS, 4]))
            def router(t):
                n = rows_of(t)
                pe.wait_ge(tp_free, TURN[("h2", 2 * t + 1)] + 1)
                for k in range(KD):
                    ins = T.matmul(ptb[0:n, t * 36:(t + 1) * 36], h2T[:, k, 0:n], wr[:, k, :],
                                   start=k == 0, stop=k == KD - 1)
                ins.then_inc(r_done, 1)

            def h2_turns(t):
                pe.wait_ge(h2_ready, t + 1)
                for c in range(2):
                    turns(("h2", 2 * t + c), quarter(h2n[0:rows_of(t), t % 2, :], c * 512))

            pe.wait_ge(tp_free, TURN[("sgu", NT - 1)] + 1)
            for t in range(NT):
                n = rows_of(t)
                for half in range(2):
                    u = UNIT[("out", 2 * t + half)]
                    free_wait(pe, u)
                    pe.wait_ge(w_loaded[5 + half], 16)
                    if t == NT - 1:
                        pe.wait_ge(fin_copied, 1)
                    for k in range(KD):
                        ins = T.matmul(acc[u % 2][0:n, :], hT[:, k, t * P:t * P + n], wg[:, (5 + half) % 2, k, :],
                                       start=k == 0, stop=k == KD - 1)
                    ins.then_inc(acc_ready, 1)
                    if half == 0 and t >= 2:
                        router(t - 2)
                if t >= 1:
                    h2_turns(t - 1)
            router(NT - 2)
            h2_turns(NT - 1)
            router(NT - 1)
            pe.wait_ge(picks, 1)
            left(pe, ("out", 2 * NT - 1))
            ins = T.matmul(acc[0][:, 0:NT * NE], ltri[:, :], M[:, :, :], start=True, stop=False)
            for t in range(NT - 1):
                later = NT - 1 - t
                ins = T.matmul(acc[0][:, (t + 1) * NE:NT * NE], ones[:, :],
                               M[:, t:t + 1, :].to_broadcast([P, later, NE]), start=False, stop=t == NT - 2)
            ins.then_inc(ranks, 1)

            def table_sums(part, a, b):
                m = b - a
                pe.wait_ge(onehots, part + 1)
                for kt in range(2 * NT):
                    n = rows_of(kt % NT)
                    ins = T.matmul(tp[part][:, 0:2 * m], onehot_p[0:n, kt, :], val_q[0:n, kt, :, a:b],
                                   start=kt == 0, stop=kt == 2 * NT - 1)
                ins.then_inc(tabs, 1)

            for t in range(NT):
                ins = T.matmul(acc[1][:, 256:256 + NE], ones[:, :], M[:, t, :], start=t == 0, stop=t == NT - 1)
            ins.then_inc(cnt_ready, 1)
            pe.wait_ge(tp_free, len(TURNS))
            table_sums(0, 0, PAIRS)

            def turn_x(n, b):
                pe.wait_ge(x_landed[b], gathered(n, b))
                for k in range(KD):
                    ins = T.transpose(sbk[k // 4][:, (k % 4) * P:(k % 4 + 1) * P], xg[:, b, k * P:(k + 1) * P], ident[:, :])
                ins.then_inc(turned, 1)

            def gate_up(n, j, b):
                pe.wait_ge(gu_in[j], 2 * weights(n, j))
                pe.wait_ge(xt_copied, n + 1)
                bank = (ptb, ovb)[b]
                for e in range(2):
                    for m in range(2):
                        out = bank[:, (2 * e + m) * CAP:(2 * e + m + 1) * CAP]
                        for k in range(KD):
                            ins = T.matmul(out, places[j][:, m, e, k * P:(k + 1) * P],
                                           xgT[:, b, k * P + e * CAP:k * P + (e + 1) * CAP],
                                           start=k == 0, stop=k == KD - 1)
                ins.then_inc(gu_done, 1)

            def down(n, j, b, first=False):
                pe.wait_ge(hid_done, n + 1)
                pe.wait_ge(down_in[j], weights(n, j))
                if not first:
                    pe.wait_ge(y_half_d, n - 1)
                    pe.wait_ge(y_half_a, n - 1)
                for e in range(2):
                    for half in range(2):
                        ins = T.matmul((acc, tp)[b][half][e * CAP:(e + 1) * CAP, :], hid[:, b, e * CAP:(e + 1) * CAP],
                                       places[j][:, 2, e, half * 512:(half + 1) * 512], start=True, stop=True)
                ins.then_inc(down_done, 1)

            def work(first, last):
                turn_x(first, 0)
                start = first
                if first == 0:
                    start = 5
                    for n in range(start):
                        gate_up(n, n, n % 2)
                        turn_x(n + 1, (n + 1) % 2)
                        if n == 0:
                            pe.wait_ge(flag_ready, 1)
                            pe.wait_ge(tab_ready, 1)
                        down(n, n, n % 2, n < 2)
                rest = (last - start - 1) % 4 + 1
                with pe.Fori(start, last - rest - 3, 4) as i:
                    for j in range(4):
                        slot, b = (start + j - 1) % 4, (start + j) % 2
                        gate_up(i + j, slot, b)
                        turn_x(i + (j + 1), 1 - b)
                        down(i + j, slot, b)
                for n in range(last - rest, last):
                    slot, b = (n - 1) % 4, n % 2
                    gate_up(n, slot, b)
                    if n + 1 < last:
                        turn_x(n + 1, 1 - b)
                    down(n, slot, b)

            work(0, PAIRS)
            more = pe.value_load(flag[0:1, 0:1], min_val=0, max_val=1)
            with pe.If(more > 0):
                pe.wait_ge(y_half_d, PAIRS)
                pe.wait_ge(y_half_a, PAIRS)
                table_sums(1, PAIRS, TOTAL)
                pe.wait_ge(tab_ready, 2)
                work(PAIRS, TOTAL)


def scattered(n, b):
    return (n - b) * 8


def gathered(n, b):
    return (n - b) * 8 + 16


def weights(n, j):
    if isinstance(n, int) and n < 5:
        return 16
    return (n - (j + 1)) * 4 + 16


def kernel(**inputs):
    import concourse.bacc as bacc
    from concourse.bass_utils import run_bass_kernel_spmd

    a = {k: np.asarray(v) for k, v in inputs.items()}
    sgu_w = a["sgu_w"][0]
    feeds = {
        "x_prompt": a["x_prompt"], "x_sample": a["x_sample"],
        "cache_win_k": a["cache_win_k"], "cache_win_v": a["cache_win_v"],
        "ln1_g": a["ln1_g"].reshape(-1), "w_in": a["w_in"],
        "sgu_norm_g": a["sgu_norm_g"].reshape(-1),
        "sgu_wt": sgu_w.transpose(2, 0, 1), "sgu_w00": sgu_w[:, 0, 0],
        "sgu_bt": a["sgu_b"][0].T, "sgu_b0": a["sgu_b"][0, :, 0],
        "w_out": a["w_out"], "ln2_g": a["ln2_g"].reshape(-1),
        "w_router": np.concatenate([a["w_router_group"][0], a["w_router_expert"][0]], 1).reshape(P, KD, NG + NE),
        "b_router": np.concatenate([a["b_router_group"][0], a["b_router_expert"][0]]),
        "w_gate": a["w_gate"], "w_up": a["w_up"], "w_down": a["w_down"], "lnf_g": a["lnf_g"],
        "const": constants(),
    }
    outs = [("y_prompt", (1, SEQ, D)), ("y_sample", (NS, 1, D)),
            ("k_prompt", (1, 1, SEQ, HEADS, HD)), ("v_prompt", (1, 1, SEQ, HEADS, HD)),
            ("k_sample", (1, NS, 1, HEADS, HD)), ("v_sample", (1, NS, 1, HEADS, HD)),
            ("sgu_v_sample", (1, NS, 1, HEADS, HD))]
    nc = bacc.Bacc("TRN2", target_bir_lowering=False, num_devices=1)
    arrays, args = {}, []
    for name, v in feeds.items():
        v = np.ascontiguousarray(v)
        arrays["in_" + name] = v
        args.append(nc.dram_tensor("in_" + name, v.shape, mybir.dt.from_np(v.dtype), kind="ExternalInput").ap())
    for name, shape in outs:
        args.append(nc.dram_tensor("out_" + name, shape, F32, kind="ExternalOutput").ap())
    build(nc, *args)
    r = run_bass_kernel_spmd(nc, [arrays], core_ids=[0])
    return tuple(r.results[0]["out_" + name] for name, _ in outs)
```

```python
from contextlib import ExitStack

import numpy as np

import concourse.bass as bass
from concourse import mybir

F32 = mybir.dt.float32
I32 = mybir.dt.int32
F16 = mybir.dt.float16
ALU = mybir.AluOpType
ACT = mybir.ActivationFunctionType
AX = mybir.AxisListType.X

P = 128
D = 1024
KD = D // P
SEQ = 512
NS = 8
NT = SEQ // P + 1
HEADS, HD = 8, 64
W = HEADS * HD
PAST = 2048
DILATIONS = (1, 4, 16)
NPAT = len(DILATIONS)
NG, EPG = 4, 8
NE = NG * EPG
FE = 128
CAP = 64
PAIRS = NE // 2
ROUNDS = -(-(SEQ + NS) // CAP)
TOTAL = ROUNDS * PAIRS
ROWS = SEQ + NS
EPS = 1e-6
SCALE = HD ** -0.5
NEG = -1e30
H_UP, W_UP = 16.0, 64.0
UNDO = 1.0 / (H_UP * W_UP)
P_UP, V_UP = 4096.0, 64.0
UNDO_PV = 1.0 / (P_UP * V_UP)
PIECES = 4
FAR = 1.0e6

C_IDENT = 0
C_MASK = C_IDENT + P
C_ROPE = C_MASK + 4 * P
C_LTRI = C_ROPE + 2 * NT * HD
C_IOTA = C_LTRI + P
C_M100 = C_IOTA + TOTAL
C_ECODE = C_M100 + EPG
C_VAL = C_ECODE + NE
C_HM = C_VAL + 4 * NT
C_BIND = C_HM + HEADS
C_BINDT = C_BIND + NS
C_VALID = C_BINDT + NS * HEADS
C_END = C_VALID + 1


def rows_of(t):
    return P if t < NT - 1 else NS


def constants():
    c = np.zeros((P, C_END), np.float32)
    r = np.arange(P)
    c[:, C_IDENT:C_IDENT + P] = np.eye(P)
    for j in range(4):
        delta = (3 - j) * P + r[:, None] - r[None, :]
        count = ((delta >= 0) & (delta <= P)).astype(int)
        for dil in DILATIONS[1:]:
            count += (delta >= 0) & (delta % dil == 0)
        c[:, C_MASK + j * P:C_MASK + (j + 1) * P] = np.where(
            count > 0, np.log(np.maximum(count, 1)) / SCALE, NEG)
    inv = (np.float32(10000.0) ** (-np.arange(HD // 2, dtype=np.float32) * np.float32(2.0) / np.float32(HD))).astype(np.float32)
    for t in range(NT):
        pos = (t * P + r if t < NT - 1 else np.full(P, PAST)).astype(np.float32)
        ang = (pos[:, None] * inv[None, :]).astype(np.float32).astype(np.float64)
        at = C_ROPE + t * HD
        c[:, at:at + HD] = np.concatenate([np.cos(ang), np.cos(ang)], 1) * UNDO
        at += NT * HD
        c[:, at:at + HD] = np.concatenate([-np.sin(ang), np.sin(ang)], 1) * UNDO
    c[:, C_LTRI:C_LTRI + P] = r[:, None] < r[None, :]
    c[:, C_IOTA:C_IOTA + TOTAL] = np.arange(TOTAL)
    c[:, C_M100:C_M100 + EPG] = np.arange(EPG) - 100
    c[:, C_ECODE:C_ECODE + NE] = 1024 * np.arange(NE)
    for k in range(2):
        for t in range(NT):
            at = C_VAL + 2 * (k * NT + t)
            c[:, at] = t * P + r + 1
            c[:, at + 1] = k * ROWS + t * P + r + 1
    bh = np.arange(NS * HEADS)
    for part in range(2):
        c[part * NS * HEADS + bh, C_HM + bh % HEADS] = 1
        c[part * NS * HEADS + bh, C_BIND + bh // HEADS] = 1
    c[bh // HEADS, C_BINDT + bh] = 1
    c[:NS, C_VALID] = 1
    return c


TILES = range(NT)
UNITS = [(_kind, t) for _kind in ("q", "k", "va", "v") for t in TILES]
UNITS += [("u", t) for t in range(NT - 1)]
UNITS += [("mix", j) for j in range(4)]
UNITS += [("u", NT - 1)]
OUT_ORDER = [(0, 0), (1, 0), (0, 1), (1, 1)] + [(t, h) for t in range(2, NT) for h in range(2)]
UNITS += [("out", 2 * t + h) for t, h in OUT_ORDER]
UNIT = {u: n for n, u in enumerate(UNITS)}
BY_SCALAR = ("va", "v", "u")
GROUP_AT = {"u": 0, "va": W, "q": 2 * W, "k": 3 * W, "v": 4 * W}
W_ORDER = ["q", "k", "va", "v", "u"]


def evacuated(n):
    scalar = UNITS[n][0] in BY_SCALAR
    return scalar, sum((u[0] in BY_SCALAR) == scalar for u in UNITS[:n + 1])


TURNS = [("h", 2 * t + c) for t in range(NT) for c in range(2)]
TURNS += [("q", t) for t in range(NT - 1)] + [("k", t) for t in range(NT - 1)]
TURNS += [("att", 0), ("att", 1), ("sgu", 0), ("att", 2), ("sgu", 1), ("sgu", 2), ("sgu", 3), ("att", 3), ("sgu", 4)]
TURNS += [("h2", 2 * t + c) for t in range(NT) for c in range(2)]
TURN_BANK = [n % 2 for n in range(TURNS.index(("att", 0)))] + [1] * 8
TURN_BANK += [n % 2 for n in range(len(TURNS) - len(TURN_BANK))]
TURN = {u: n for n, u in enumerate(TURNS)}
SPLIT = ("h", "att", "sgu")


def turned_out(n):
    split = TURNS[n][0] in SPLIT
    return split, sum((u[0] in SPLIT) == split for u in TURNS[:n + 1])



LAST_ORDER = [NT - 1] + list(range(NT - 1))
TASKS = [(i, h) for i in range(4) for h in range(HEADS)]
FILL = []
for _t in range(1, NT):
    FILL += [("v", _t, part) for part in range(KD)]
for _b, _rest in enumerate(([("u", 0)], [("u", 1)], [("u", 2)], [("u", 3.0)], [("u", 3.5), ("mix", 0), ("mix", 1)],
                            [("mix", 2), ("mix", 3), ("u", 4.0)], [("u", 4.5)], [])):
    FILL += [("pv", _b, part) for part in range(NPAT)]
    for _kind, _t in _rest:
        FILL += [(_kind, int(_t), part) for part in range(1 if _kind == "mix" else KD)
                 if isinstance(_t, int) or part // 4 == 2 * (_t % 1)]


def fill_of(n):
    return FILL[len(FILL) * n // len(TASKS):len(FILL) * (n + 1) // len(TASKS)]


def finished_in(n):
    return [(kind, t) for kind, t, part in fill_of(n) if kind == "mix" or kind != "pv" and part == KD - 1]


SPLIT_AFTER = {at + i: (group, i) for group, at in ((4, 5), (5, 13)) for i in range(PIECES)}
VALUE_AFTER = {}
for _n in range(len(TASKS)):
    for _kind, _b, _part in fill_of(_n):
        if (_kind, _part) == ("pv", NPAT - 1) and _b + 1 < NS:
            VALUE_AFTER.setdefault(_n, []).append(_b + 1)
VALUE_AFTER.setdefault(8, []).append(0)
TURN_AFTER = {20: ("att", 0), 24: ("att", 1), 27: ("sgu", 0), 28: ("att", 2),
              29: ("sgu", 1), 30: ("sgu", 2), 31: ("sgu", 3)}


def build(nc, x_prompt, x_sample, cache_k, cache_v, ln1_g, w_in, sgu_g, sgu_wt, sgu_w, sgu_bt, sgu_b,
          w_out, ln2_g, w_router, b_router, w_gate, w_up, w_down, lnf_g, const,
          y_prompt, y_sample, k_prompt, v_prompt, k_sample, v_sample, sgu_v_sample):
    h2_dram = nc.dram_tensor("h2_rows", (ROWS, D), F32, kind="Internal").ap()
    q_dram = nc.dram_tensor("sample_q", (NS, W), F32, kind="Internal").ap()
    y2_dram = nc.dram_tensor("expert_rows", (2 * ROWS, D), F32, kind="Internal").ap()

    with ExitStack() as ctx:
        def sb(name, shape, dt=F32):
            return ctx.enter_context(nc.sbuf_tensor(name, shape, dt))

        def sem(name):
            return ctx.enter_context(nc.semaphore(name))

        x = sb("x", [P, NT, D])
        hflat = sb("tokens_split", [P, KD * (SEQ + NS)])
        wflat = sb("weights_split", [P, 2 * KD * W])
        att = sb("att", [P, 4096])
        vring = sb("vring", [P, 3072])
        h2T = sb("h2T", [P, KD, P])
        gain = sb("gain", [P, D])
        gv = sb("gv", [P, 512])
        big = sb("big", [P, 4 * 6144])
        ident = sb("ident", [P, P])
        ones = sb("ones", [P, P])
        ltri = sb("ltri", [P, P])
        iota = sb("iota", [P, TOTAL])
        small = sb("small", [P, EPG + NE + 4 * NT + HEADS + NS + NS * HEADS + 1])
        sT = sb("sT", [P, NPAT, NS * HEADS])
        wr = sb("wr", [P, KD, NG + NE])
        rbias = sb("rbias", [P, NG + NE])
        negm = sb("negm", [P, 32])
        den = sb("den", [P, 32])
        stat = sb("stat", [P, 72])
        epsc = sb("epsc", [P, 1])
        flag = sb("flag", [P, 1], I32)

        def cut(base, at, *shape):
            n = int(np.prod(shape))
            v = base[:, at:at + n]
            if len(shape) == 2:
                return v.rearrange("p (a b) -> p a b", a=shape[0])
            if len(shape) == 3:
                return v.rearrange("p (a b c) -> p a b c", a=shape[0], b=shape[1])
            return v

        m100 = small[:, 0:EPG]
        ecode = small[:, EPG:EPG + NE]
        o = EPG + NE
        val = small[:, o:o + 4 * NT].rearrange("p (a v) -> p a v", v=2)
        o += 4 * NT
        hm2, bind2 = small[:, o:o + HEADS], small[:, o + HEADS:o + HEADS + NS]
        hm, bind = hm2[0:NS * HEADS], bind2[0:NS * HEADS]
        bindT = small[0:NS, o + HEADS + NS:o + HEADS + NS + NS * HEADS]
        in_samples = small[:, o + HEADS + NS + NS * HEADS:]

        qT = cut(big, 0, 4, SEQ)
        kT = cut(big, 2048, 4, SEQ)
        mask = cut(big, 4096, 512)
        qn = cut(big, 4608, 2, W)
        qs = cut(big, 5632, W)
        kn = cut(big, 6144, NT, W)
        vn = cut(big, 8704, NT, W)
        kring = cut(big, 11264, 2, NPAT, W)
        prod = cut(big, 14336, NPAT, W)
        ptm = big[:, 11264:12800].bitcast(F16).rearrange("p (a b s r) -> p a b s r", a=NPAT, b=NS, s=2)
        masked = cut(big, 12800, W)
        diag = cut(big, 13312, NS * HEADS)[0:NS * HEADS]
        own = cut(big, 13376, NS * HEADS)[0:NS]
        vsplit = big[:, 13440:14976].bitcast(F16).rearrange("p (s a n) -> p s a n", s=2, a=NPAT)
        attn = cut(big, 15872, 4, W)
        sqt = cut(big, 17920, W)
        hbuf = cut(big, 15872, 2, D)
        vv = cut(big, 18432, NT, W)
        uu = cut(big, 20992, NT, W)
        cos = cut(big, 23552, NT, HD)
        sin = cut(big, 23552 + NT * HD, NT, HD)
        bcol = cut(big, 24192, HEADS)
        w00 = cut(big, 24200, HEADS)[0:NS]
        b0 = cut(big, 24208, HEADS)[0:NS]
        ew = big[:, :].rearrange("p (s m e n) -> p s m e n", s=4, m=3, e=2)

        hT = hflat[:, :].bitcast(F16).rearrange("p (a k n) -> p a k n", a=2, k=KD)
        wg = wflat[:, :].bitcast(F16).rearrange("p (s a k n) -> p s a k n", s=2, a=2, k=KD)
        pieces_a = [cut(vring, 1024 * i, 2, W) for i in range(3)] + [cut(h2T[:, :, :].rearrange("p k n -> p (k n)"), 0, 2, W)]
        pieces_b = [cut(big, 4608 + 1024 * i, 2, W) for i in range(PIECES)]

        def pieces(n):
            return pieces_a if n < 4 else pieces_b

        once = wflat[:, 0:6144].rearrange("p (m e n) -> p m e n", m=3, e=2)
        places = [ew[:, slot] for slot in range(4)] + [once]
        yrow = cut(wflat, 6144, 2, D)
        xg = cut(hflat, 0, 2, D)
        xsplit = hflat[:, 2048:4096].bitcast(F16).rearrange("p (b k a c) -> p b k a c", b=2, k=KD, a=2)
        sg = cut(vring, 2048, 2, 2 * CAP)
        hid = cut(vring, 2304, 2, 2 * CAP)
        idxg = vring[:, 2560:2562].bitcast(I32)
        idxs = vring[:, 2562:2564].bitcast(I32)

        s_sb = cut(att, 0, 2, 512)
        p_sb = cut(att, 1024, 2, 512)
        pt_sb = cut(att, 2048, 2, 512)
        qb = cut(att, 3072, 2, 512)
        rtmp = cut(att, 0, W)
        vr = cut(vring, 0, 2, NPAT, W)
        h2n = cut(vring, 0, 2, D)
        wt = h2T
        gvb = gv[:, 0:W]
        sall = gv[0:NS * HEADS, 0:NPAT * P + 1]

        at = [0]

        def route(*shape):
            n = int(np.prod(shape))
            v = cut(att, at[0], *shape)
            at[0] += n
            return v

        onehot_p = route(NT * P).bitcast(F16).rearrange("p (a b) -> p a b", a=2 * NT)
        L = route(NT, NG + NE)
        gmax, gsum, gp = route(NT), route(NT), route(NT)
        ge = route(NT, NG)
        gpick = route(NT, NG)
        gidx = route(NT)
        lmul = route(NT, NE)
        sel = route(NT, EPG)
        sel2 = route(NT, EPG)
        pickt = route(NT, EPG)
        m12 = route(2, NT)
        i12 = route(2, NT)
        o12 = route(2 * NT, EPG)
        ex = route(NT)
        gates = route(2, NT)
        O = route(2, NT, NE)
        M = route(NT, NE)
        X = route(NT, NE)
        OX = route(2 * NT, NE)
        rk, rm, r1, r2, r3, r4, rk2, rk3 = [route(2 * NT) for _ in range(8)]
        table = route(2 * TOTAL)
        tabtmp = route(2 * PAIRS * (ROUNDS - 1))
        assert at[0] <= 3072
        esplit = [v.bitcast(F16).rearrange("p (a k f) -> p a k f", a=2, k=KD) for v in (
            att[:, 3072:4096], h2T[:, :, :].rearrange("p k n -> p (k n)"), vring[:, 0:1024], vring[:, 1024:2048])]
        tab = table.bitcast(I32)
        val_q = [cut(vring[:, 2564:3072].bitcast(F16), 0, 2 * NT, 2, PAIRS),
                 cut(vring[:, :].bitcast(F16), 0, 2 * NT, 2, TOTAL - PAIRS)]

        banks = [ctx.enter_context(nc.psum_tensor(f"bank{i}", [P, 512], F32)) for i in range(8)]
        acc, tp, sbk, ptb, ovb = banks[0:2], banks[2:4], banks[4:6], banks[6], banks[7]

        x_in = [sem(f"x_in{t}") for t in range(NT)]
        gain_in = sem("gain_in")
        ident_in, rope_in, mask_in, consts_in, gv_in, wt_in, wt_mask = [
            sem(n) for n in ("ident_in", "rope_in", "mask_in", "consts_in", "gv_in", "wt_in", "wt_masked")]
        w_loaded = [[sem(f"w{n}_piece{i}_in") for i in range(PIECES)] for n in range(7)]
        kq_in = [sem(f"keys_and_q_in{i}") for i in range(2)]
        q_stored = sem("q_stored")
        v_in = [sem(f"v_in{i}") for i in range(2)]
        squares, h_ready = sem("squares"), sem("h_ready")
        tp_ready, tp_free_a, tp_free_d = sem("tp_ready"), sem("tp_free_scalar"), sem("tp_free_vector")
        turn_high, w_high, w_split, fin_high = sem("turn_high"), sem("w_high"), sem("w_split"), sem("fin_high")
        va_sum, va_root = sem("va_sum"), sem("va_root")
        acc_ready, free_d, free_a = sem("acc_ready"), sem("acc_free_vector"), sem("acc_free_scalar")
        q_ready, k_ready = sem("q_ready"), sem("k_ready")
        s_ready, masked_s, exp_done, p_turned, pt_copied, pv_done, o_done = [
            sem(n) for n in ("s_ready", "masked_s", "exp_done", "p_turned", "pt_copied", "pv_done", "o_done")]
        ones_set, eps_set, rooted = sem("ones_set"), sem("eps_set"), sem("rooted")
        prods, sums = sem("prods"), sem("sums")
        self_s, st_ready, sall_ready, sexp, sp_ready, stb_ready, ptm_zeroed, ptm_ready, sample_pv, heads_masked, fin_ready, fin_copied, v_high, v_split = [
            sem(n) for n in ("self_s", "st_ready", "sall_ready", "sexp", "sp_ready", "stb_ready", "ptm_zeroed", "ptm_ready",
                             "sample_pv", "heads_masked", "fin_ready", "fin_copied", "v_high", "v_split")]
        va_ready, sgu_s_ready = sem("va_ready"), sem("sgu_s_ready")
        sq2, h2_ready, r_done = sem("sq2"), sem("h2_ready"), sem("router_done")
        h2w = [sem(f"h2_written{t}") for t in range(NT)]
        dv, dv_more = sem("vector_step"), sem("vector_step_more_rounds")
        gexp_in, gexp, eexp_in, eexp = sem("gexp_in"), sem("gexp"), sem("eexp_in"), sem("eexp")
        picks, ranks, onehots, tabs, tab_ready, flag_ready, cnt_ready = [
            sem(n) for n in ("picks", "ranks", "onehots", "tabs", "tab_ready", "flag_ready", "cnt_ready")]
        zeroed = sem("zeroed")
        gu_in = [[sem(f"{m}_in{i}") for i in range(5)] for m in ("gate", "up")]
        down_in = [sem(f"down_in{i}") for i in range(5)]
        gidx_copied, sidx_copied = sem("gidx_copied"), sem("sidx_copied")
        x_landed = [sem(f"x_landed{i}") for i in range(2)]
        y_landed = [sem(f"y_landed{i}") for i in range(2)]
        e_high, e_split, x_high = sem("expert_high"), sem("expert_split"), sem("x_high")
        turned, x_split, gu_parts, silu_done, hid_done, down_done, y_copied = [
            sem(n) for n in ("turned", "x_split", "gate_up_parts", "silu_done", "hid_done", "down_done", "y_copied")]
        rows_ready, out_k, out_v, out_s, y_out = sem("rows_ready"), sem("out_k"), sem("out_v"), sem("out_s"), sem("y_out")
        rows_in = [sem(f"rows_in{t}") for t in range(NT)]
        mixed, sq3, y_ready = sem("mixed"), sem("sq3"), sem("y_ready")

        xp = x_prompt.rearrange("a (t p) d -> (a t) p d", p=P)
        xs = x_sample.rearrange("b a d -> (b a) d")
        w_in_v = w_in.rearrange("a (k p) n -> (a p) k n", p=P)
        w_out_v = w_out.rearrange("a (k p) n -> (a p) k n", p=P)
        gate_v = [w[0].rearrange("e (p k) f -> p e (k f)", k=KD) for w in (w_gate, w_up)]
        down_v = w_down[0].rearrange("e p n -> p e n")
        yp = y_prompt.rearrange("a (t p) d -> (a t) p d", p=P)
        ys = y_sample.rearrange("b a d -> (b a) d")

        def free_wait(eng, n):
            if n >= 2:
                scalar, count = evacuated(n - 2)
                eng.wait_ge(free_a if scalar else free_d, count)

        def left(eng, unit):
            scalar, count = evacuated(UNIT[unit])
            eng.wait_ge(free_a if scalar else free_d, count)

        def wait_turned_out(eng, unit):
            split, count = turned_out(TURN[unit])
            eng.wait_ge(tp_free_d if split else tp_free_a, count)

        def gate_up_loads(sp, slot, pair):
            for m in range(2):
                sp.dma_start(places[slot][:, m], gate_v[m][:, bass.ds(pair, 2), :]).then_inc(gu_in[m][slot], 16)

        def down_load(sp, slot, pair):
            sp.dma_start(places[slot][:, 2], down_v[:, bass.ds(pair, 2), :]).then_inc(down_in[slot], 16)

        block = ctx.enter_context(nc.Block())

        @block.sync
        def _(sp):
            sp.dma_start(x[:, 0, :], xp[0]).then_inc(x_in[0], 16)
            sp.dma_start(x[:, 1, :], xp[1]).then_inc(x_in[1], 16)

            def load_w(n):
                if n == 4:
                    sp.wait_ge(self_s, 1)
                    sp.wait_ge(tp_ready, TURN[("k", NT - 2)] + 1)
                    sp.wait_ge(out_k, 32)
                elif n >= 1:
                    sp.wait_ge(w_split, PIECES * n)
                if n < 5:
                    at = GROUP_AT[W_ORDER[n]]
                    src = w_in_v[:, :, at:at + W]
                else:
                    src = w_out_v[:, :, (n - 5) * W:(n - 4) * W]
                for i, dst in enumerate(pieces(n)):
                    sp.dma_start(dst, src[:, 2 * i:2 * i + 2, :]).then_inc(w_loaded[n][i], 16)

            def load_k(b):
                if b >= 2:
                    sp.wait_ge(prods, b - 1)
                for p_, dil in enumerate(DILATIONS):
                    src = cache_k[0, b, PAST - P * dil:PAST:dil].rearrange("j h d -> j (h d)")
                    sp.dma_start(kring[:, b % 2, p_, :], src).then_inc(kq_in[b % 2], 16)

            def load_q(b):
                sp.dma_start(qb[:, b % 2, :], q_dram[b].partition_broadcast(P)).then_inc(kq_in[b % 2], 16)

            def load_v(b):
                if b >= 2:
                    sp.wait_ge(v_split, b - 1)
                for p_, dil in enumerate(DILATIONS):
                    src = cache_v[0, b, PAST - P * dil:PAST:dil].rearrange("j h d -> j (h d)")
                    sp.dma_start(vr[:, b % 2, p_, :], src).then_inc(v_in[b % 2], 16)

            load_w(0)
            for t in range(2, NT - 1):
                sp.dma_start(x[:, t, :], xp[t]).then_inc(x_in[t], 16)
            sp.dma_start(x[0:NS, NT - 1, :], xs).then_inc(x_in[NT - 1], 16)
            sp.dma_start(cos[:, :, :], const[:, C_ROPE:C_ROPE + NT * HD].rearrange("p (t n) -> p t n", t=NT)).then_inc(rope_in, 16)
            sp.dma_start(sin[:, :, :], const[:, C_ROPE + NT * HD:C_LTRI].rearrange("p (t n) -> p t n", t=NT)).then_inc(rope_in, 16)
            load_k(0)
            load_w(1)
            load_k(1)
            sp.dma_start(gvb, sgu_g.partition_broadcast(P)).then_inc(gv_in, 16)
            sp.dma_start(mask, const[:, C_MASK:C_MASK + 4 * P]).then_inc(mask_in, 16)
            sp.dma_start(ltri[:, :], const[:, C_LTRI:C_LTRI + P]).then_inc(consts_in, 16)
            sp.dma_start(iota[:, :], const[:, C_IOTA:C_IOTA + TOTAL]).then_inc(consts_in, 16)
            sp.dma_start(small[:, :], const[:, C_M100:C_END]).then_inc(consts_in, 16)
            sp.dma_start(wr[:, :, :], w_router).then_inc(consts_in, 16)
            sp.dma_start(rbias[:, :], b_router.partition_broadcast(P)).then_inc(consts_in, 16)
            sp.dma_start(bcol[:, :], sgu_bt).then_inc(consts_in, 16)
            sp.dma_start(w00[:, :], sgu_w.partition_broadcast(NS)).then_inc(consts_in, 16)
            sp.dma_start(b0[:, :], sgu_b.partition_broadcast(NS)).then_inc(consts_in, 16)
            load_w(2)
            sp.wait_ge(q_ready, NT)
            sp.dma_start(q_dram, qs[0:NS]).then_inc(q_stored, 16)
            sp.wait_ge(q_stored, 16)
            load_q(0)
            load_q(1)
            for b in range(2, NS):
                if b == 4:
                    load_w(3)
                load_k(b)
                load_q(b)
            load_w(4)
            sp.wait_ge(w_split, 4 * PIECES)
            sp.dma_start(wt[:, :, :], sgu_wt).then_inc(wt_in, 16)
            load_v(0)
            load_v(1)
            load_w(5)
            for b in range(2, 6):
                load_v(b)
            load_w(6)
            for b in range(6, NS):
                load_v(b)
            sp.wait_ge(masked_s, len(TASKS))
            sp.wait_ge(s_ready, len(TASKS))
            sp.wait_ge(self_s, 1)
            sp.wait_ge(prods, NS)
            sp.wait_ge(w_split, 7 * PIECES)
            gate_up_loads(sp, 0, 0)
            down_load(sp, 0, 0)
            sp.wait_ge(sums, NS)
            sp.wait_ge(acc_ready, UNIT[("mix", 3)] + 1)
            sp.wait_ge(sgu_s_ready, 1)
            sp.wait_ge(tp_ready, TURN[("sgu", NT - 1)] + 1)
            sp.wait_ge(out_k, 32)
            sp.wait_ge(out_s, 16)
            sp.wait_ge(fin_ready, 1)
            sp.wait_ge(h2w[0], 16)
            gate_up_loads(sp, 1, 2)
            down_load(sp, 1, 2)
            sp.wait_ge(h2w[1], 16)
            gate_up_loads(sp, 2, 4)
            down_load(sp, 2, 4)
            sp.wait_ge(out_v, 32)
            sp.wait_ge(h2w[2], 16)
            gate_up_loads(sp, 3, 6)
            down_load(sp, 3, 6)
            sp.wait_ge(acc_ready, UNIT[("out", 2 * NT - 1)] + 1)
            gate_up_loads(sp, 4, 8)
            down_load(sp, 4, 8)
            for n in range(5, PAIRS):
                used = n - 4 if n < 9 else n - 3
                before = (n - 2) % 4
                if n > 5:
                    sp.wait_ge(gu_in[1][before], weights(n - 1, before))
                sp.wait_ge(e_split, 4 * used)
                gate_up_loads(sp, (n - 1) % 4, 2 * n)
                if n > 5:
                    sp.wait_ge(down_in[before], weights(n - 1, before))
                sp.wait_ge(down_done, used)
                down_load(sp, (n - 1) % 4, 2 * n)
            sp.wait_ge(flag_ready, 1)
            more = sp.value_load(flag[0:1, 0:1], min_val=0, max_val=1)
            with sp.If(more > 0):
                with sp.Fori(PAIRS, TOTAL - PAIRS + 1, PAIRS) as r:
                    with sp.Fori(0, PAIRS - 3, 4) as i:
                        for j in range(4):
                            sp.wait_ge(e_split, (r + i + (j - 3)) * 4)
                            gate_up_loads(sp, (j + 3) % 4, i * 2 + 2 * j)
                            sp.wait_ge(down_done, r + i + (j - 3))
                            down_load(sp, (j + 3) % 4, i * 2 + 2 * j)
            sp.wait_ge(rows_ready, 1)
            rows = big[:, 0:2 * NT * D].rearrange("p (t k n) -> p t k n", t=NT, k=2)
            for t in LAST_ORDER:
                n = rows_of(t)
                for k in range(2):
                    at = k * ROWS + t * P
                    sp.dma_start(rows[0:n, t, k], y2_dram[at:at + n, :]).then_inc(rows_in[t], 16)
            for i, t in enumerate(LAST_ORDER):
                sp.wait_ge(y_ready, i + 1)
                sp.dma_start(yp[t] if t < NT - 1 else ys, x[0:rows_of(t), t, :]).then_inc(y_out, 16)
            sp.wait_ge(y_out, 16 * NT)

        @block.gpsimd
        def _(pool):
            nc.gpsimd.memset(epsc[:], EPS).then_inc(eps_set, 1)
            nc.gpsimd.memset(ones[:], 1.0).then_inc(ones_set, 1)
            kp = k_prompt.rearrange("a b (t p) h d -> (a b p) t (h d)", p=P)
            vp = v_prompt.rearrange("a b (t p) h d -> (a b p) t (h d)", p=P)
            for b in range(NS):
                if b == 3:
                    pool.wait_ge(k_ready, NT)
                    pool.dma_start(kp, kn[:, 0:4, :]).then_inc(out_k, 16)
                    pool.dma_start(k_sample.rearrange("a b t h d -> (a b t) (h d)"), kn[0:NS, 4, :]).then_inc(out_k, 16)
                pool.wait_ge(kq_in[b % 2], 64 * (b // 2 + 1))
                if b >= 1:
                    pool.wait_ge(sums, b)
                nc.gpsimd.tensor_tensor(
                    prod[:, :, :], kring[:, b % 2],
                    qb[:, b % 2, :].unsqueeze(1).to_broadcast([P, NPAT, W]), ALU.mult).then_inc(prods, 1)
            pool.wait_ge(prods, NS)
            nc.gpsimd.memset(big[:, 11264:12800], 0.0).then_inc(ptm_zeroed, 1)
            pool.wait_ge(wt_in, 16)
            nc.gpsimd.affine_select(out=wt[:, :, :], in_=wt[:, :, :], compare_op=ALU.is_ge, fill=0.0, base=0,
                                    pattern=[[0, HEADS], [1, P]], channel_multiplier=-1).then_inc(wt_mask, 1)
            pool.wait_ge(va_ready, NT)
            pool.dma_start(sgu_v_sample.rearrange("a b t h d -> (a b t) (h d)"), vn[0:NS, 4, :]).then_inc(out_s, 16)
            left(pool, ("v", NT - 1))
            pool.dma_start(vp, vv[:, 0:4, :]).then_inc(out_v, 16)
            pool.dma_start(v_sample.rearrange("a b t h d -> (a b t) (h d)"), vv[0:NS, 4, :]).then_inc(out_v, 16)
            for t in range(NT):
                pool.wait_ge(h2_ready, t + 1)
                pool.dma_start(h2_dram[t * P:t * P + rows_of(t), :], h2n[0:rows_of(t), t % 2, :]).then_inc(h2w[t], 16)
            pool.wait_ge(acc_ready, UNIT[("out", 2 * NT - 1)] + 1)
            nc.gpsimd.memset(xg[:, :, :], 0.0).then_inc(zeroed, 1)
            pool.wait_ge(zeroed, 1)
            for t in range(NT):
                pool.wait_ge(h2w[t], 16)
            pool.wait_ge(tab_ready, 1)

            def gather(n, b, first=False):
                if not first:
                    pool.wait_ge(turned, n - 1)
                nc.gpsimd.tensor_copy(idxg[:, b:b + 1], tab[:, bass.ds(n, 1)]).then_inc(gidx_copied, 1)
                pool.wait_ge(gidx_copied, n + 1)
                nc.gpsimd.indirect_dma_start(
                    out=xg[:, b, :], out_offset=None, in_=h2_dram,
                    in_offset=bass.IndirectOffsetOnAxis(ap=idxg[:, b:b + 1], axis=0),
                    bounds_check=n + (ROWS - 1), oob_is_err=False).then_inc(x_landed[b], 16)

            def scatter(n, b):
                pool.wait_ge(y_copied, n + 1)
                nc.gpsimd.tensor_copy(idxs[:, b:b + 1], tab[:, bass.ds(n + TOTAL, 1)]).then_inc(sidx_copied, 1)
                pool.wait_ge(sidx_copied, n + 1)
                nc.gpsimd.indirect_dma_start(
                    out=y2_dram, out_offset=bass.IndirectOffsetOnAxis(ap=idxs[:, b:b + 1], axis=0),
                    in_=yrow[:, b, :], in_offset=None,
                    bounds_check=n + (2 * ROWS - 1), oob_is_err=False).then_inc(y_landed[b], 16)

            def work(first, last):
                gather(first, 0, first == 0)
                gather(first + 1, 1, first == 0)
                gather(first + 2, 0)
                with pool.Fori(first, last - 7, 4) as i:
                    for j in range(4):
                        gather(i + (j + 3), (j + 1) % 2)
                        scatter(i + j, j % 2)
                for n in range(last - 4, last):
                    if n + 3 < last:
                        gather(n + 3, (n + 1) % 2)
                    scatter(n, n % 2)
                for b in range(2):
                    pool.wait_ge(y_landed[b], 8 * last)

            work(0, PAIRS)
            pool.wait_ge(flag_ready, 1)
            more = pool.value_load(flag[0:1, 0:1], min_val=0, max_val=1)
            with pool.If(more > 0):
                pool.wait_ge(tab_ready, 2)
                work(PAIRS, TOTAL)
            pool.drain().then_inc(rows_ready, 1)
            for s_, n_ in ((out_k, 32), (out_v, 32), (out_s, 16)):
                pool.wait_ge(s_, n_)

        @block.scalar
        def _(act):
            act.dma_start(gain[:, :], ln1_g.partition_broadcast(P)).then_inc(gain_in, 16)
            act.dma_start(ident[:, :], const[:, C_IDENT:C_IDENT + P]).then_inc(ident_in, 16)

            def turn(unit, dst):
                n = TURN[unit]
                m = dst.shape[-1]
                act.wait_ge(tp_ready, n + 1)
                src = tp[TURN_BANK[n]][:, 0:4 * m].rearrange("p (c m) -> p c m", c=4)
                nc.scalar.activation(dst, src, ACT.Copy).then_inc(tp_free_a, 1)

            def turn_split(unit, dst):
                n = TURN[unit]
                m = dst.shape[-1]
                act.wait_ge(tp_ready, n + 1)
                src = tp[TURN_BANK[n]][:, 0:4 * m].rearrange("p (c m) -> p c m", c=4)
                nc.scalar.activation(dst, src, ACT.Copy, scale=H_UP).then_inc(turn_high, 1)

            def split_high(n, i):
                act.wait_ge(w_loaded[n][i], 16)
                if n >= 2 and i == 0:
                    act.wait_ge(acc_ready, UNIT[(W_ORDER[n - 2], NT - 1)] + 1)
                nc.scalar.activation(wg[:, n % 2, 0, 2 * i:2 * i + 2, :], pieces(n)[i], ACT.Copy,
                                     scale=W_UP).then_inc(w_high, 1)

            def cols(t):
                return slice(t * P, t * P + rows_of(t))

            def root(sem_, count, v):
                act.wait_ge(sem_, count)
                nc.scalar.activation(v, v, ACT.Sqrt, bias=epsc[0:v.shape[0], :]).then_inc(rooted, 1)

            act.wait_ge(eps_set, 1)
            def square(t):
                act.wait_ge(x_in[t], 16)
                if t >= 2:
                    act.wait_ge(tp_ready, 2 * (t - 1))
                n = rows_of(t)
                nc.scalar.activation(hbuf[0:n, t % 2, :], x[0:n, t, :], ACT.Square, scale=D ** -0.5,
                                     accum_out=stat[0:n, t:t + 1]).then_inc(squares, 1)
                root(squares, t + 1, stat[0:n, t:t + 1])

            def turn_h(t):
                for c in range(2):
                    turn_split(("h", 2 * t + c), hT[:, 0, 4 * c:4 * c + 4, cols(t)])

            square(0)
            square(1)
            turn_h(0)
            split_high(0, 0)
            turn_h(1)
            for i in range(1, PIECES):
                split_high(0, i)
            square(2)
            square(3)
            turn_h(2)
            square(4)
            turn_h(3)
            turn_h(4)
            for i in range(PIECES):
                split_high(1, i)
            for t in range(NT - 1):
                turn(("q", t), qT[:, :, cols(t)])

            def copy_unit(unit, dst):
                n = UNIT[unit]
                act.wait_ge(acc_ready, n + 1)
                nc.scalar.activation(dst, acc[n % 2][0:dst.shape[0], 0:W], ACT.Copy, scale=UNDO).then_inc(free_a, 1)

            for t in range(NT - 1):
                turn(("k", t), kT[:, :, cols(t)])
                split_high(2, t)

            def va(t):
                n, rows = UNIT[("va", t)], rows_of(t)
                act.wait_ge(acc_ready, n + 1)
                if t >= 1:
                    act.wait_ge(va_sum, t)
                z = acc[n % 2][0:rows, 0:W]
                nc.scalar.activation(vn[0:rows, t], z, ACT.Copy, scale=UNDO)
                nc.scalar.activation(sqt[0:rows], z, ACT.Square, scale=UNDO * HD ** -0.5).then_inc(free_a, 1)
                act.wait_ge(va_sum, t + 1)
                r8 = stat[0:rows, 48:56]
                nc.scalar.activation(r8, r8, ACT.Sqrt, bias=epsc[0:rows, :]).then_inc(va_root, 1)

            for t in range(NT):
                va(t)
                if t < PIECES:
                    split_high(3, t)

            def exps(n):
                width = P * (TASKS[n][0] + 1)
                act.wait_ge(masked_s, n + 1)
                if n >= 2:
                    act.wait_ge(p_turned, n - 1)
                nc.scalar.activation(p_sb[:, n % 2, 0:width], s_sb[:, n % 2, 0:width], ACT.Exp, scale=-1.0,
                                     bias=negm[:, n:n + 1], accum_out=den[:, n:n + 1]).then_inc(exp_done, 1)

            def copy_pt(n):
                width = P * (TASKS[n][0] + 1)
                act.wait_ge(p_turned, n + 1)
                if n >= 2:
                    act.wait_ge(pv_done, n - 1)
                nc.scalar.activation(pt_sb[:, n % 2, 0:width], ptb[:, 0:width], ACT.Copy).then_inc(pt_copied, 1)

            def high_v(b):
                act.wait_ge(v_in[b % 2], 48 * (b // 2 + 1))
                if b == 0:
                    act.wait_ge(sums, NS)
                if b >= 1:
                    act.wait_ge(sample_pv, b)
                nc.scalar.activation(vsplit[:, 0], vr[:, b % 2], ACT.Copy, scale=V_UP).then_inc(v_high, 1)

            def turn_head(kind, t):
                act.wait_ge(acc_ready, UNIT[("u", t)] + 1)
                chunks = slice(4, 8) if kind == "att" else slice(0, 4)
                turn_split((kind, t), hT[:, 0, chunks, cols(t)])

            exps(0)
            copy_unit(("v", 0), vv[:, 0, :])
            for n in range(len(TASKS)):
                copy_pt(n)
                if n + 1 < len(TASKS):
                    exps(n + 1)
                for kind, t in finished_in(n):
                    if kind != "mix":
                        copy_unit((kind, t), (vv if kind == "v" else uu)[0:rows_of(t), t, :])
                if n in SPLIT_AFTER:
                    split_high(*SPLIT_AFTER[n])
                for b in VALUE_AFTER.get(n, []):
                    high_v(b)
                if n in TURN_AFTER:
                    turn_head(*TURN_AFTER[n])
                if n == 5:
                    act.wait_ge(sall_ready, 1)
                    nc.scalar.activation(sall, sall, ACT.Exp, bias=stat[0:64, 11:12],
                                         accum_out=stat[0:64, 12:13]).then_inc(sexp, 1)
            turn_head("att", NT - 2)
            act.wait_ge(fin_ready, 1)
            nc.scalar.activation(hT[:, 0, 4:8, cols(NT - 1)], ovb[:, 0:4 * NS].rearrange("p (c b) -> p c b", c=4),
                                 ACT.Copy, scale=H_UP * UNDO_PV).then_inc(fin_high, 1)
            turn_head("sgu", NT - 1)
            for i in range(PIECES):
                split_high(6, i)
            act.wait_ge(h_ready, NT)
            act.dma_start(gain[:, :], ln2_g.partition_broadcast(P)).then_inc(gain_in, 16)

            def square2(t):
                n = rows_of(t)
                left(act, ("out", 2 * t + 1))
                act.wait_ge(sample_pv, NS)
                if t >= 2:
                    act.wait_ge(h2w[t - 2], 16)
                    act.wait_ge(tp_ready, TURN[("h2", 2 * (t - 2) + 1)] + 1)
                nc.scalar.activation(h2n[0:n, t % 2, :], x[0:n, t, :], ACT.Square, scale=D ** -0.5,
                                     accum_out=stat[0:n, 16 + t:17 + t]).then_inc(sq2, 1)
                root(sq2, t + 1, stat[0:n, 16 + t:17 + t])

            def turn_h2(t):
                if t >= 1:
                    act.wait_ge(r_done, t)
                else:
                    act.wait_ge(acc_ready, UNIT[("mix", 3)] + 1)
                for c in range(2):
                    turn(("h2", 2 * t + c), h2T[:, 4 * c:4 * c + 4, 0:rows_of(t)])

            for t in range(NT):
                square2(t)
                turn_h2(t)
            act.wait_ge(gexp_in, 1)
            nc.scalar.activation(ge, ge, ACT.Exp).then_inc(gexp, 1)
            act.wait_ge(eexp_in, 1)
            nc.scalar.activation(ex, ex, ACT.Exp).then_inc(eexp, 1)
            def high_e(n, slot, q):
                act.wait_ge(gu_in[q // 2][slot], weights(n, slot))
                if not isinstance(n, int) or n > 0:
                    act.wait_ge(gu_parts, n * 4 + (q - 3))
                nc.scalar.activation(esplit[q][:, 0], places[slot][:, q // 2, q % 2, :].rearrange("p (k f) -> p k f", k=KD),
                                     ACT.Copy, scale=W_UP).then_inc(e_high, 1)

            act.wait_ge(prods, NS)
            high_e(0, 0, 0)
            act.wait_ge(r_done, NT)
            high_e(0, 0, 1)
            for t in range(NT):
                act.wait_ge(h2w[t], 16)
            high_e(0, 0, 2)
            high_e(0, 0, 3)
            act.wait_ge(h2_ready, NT)
            act.dma_start(gain[:, :], lnf_g.partition_broadcast(P)).then_inc(gain_in, 16)

            def high_x(n, b):
                act.wait_ge(turned, n + 1)
                for c in range(2):
                    last = nc.scalar.activation(xsplit[:, b, 4 * c:4 * c + 4, 0, :], sbk[c][:, :].rearrange("p (k c) -> p k c", k=4),
                                                ACT.Copy, scale=H_UP)
                last.then_inc(x_high, 1)

            def silu(n, b):
                act.wait_ge(gu_parts, n * 4 + 2)
                nc.scalar.activation(sg[:, b], ptb[:, 0:2 * CAP], ACT.Silu, scale=UNDO).then_inc(silu_done, 1)

            def copy_y(n, b, first=False):
                act.wait_ge(down_done, n + 1)
                if not first:
                    act.wait_ge(y_landed[b], scattered(n, b))
                for half in range(2):
                    last = nc.scalar.activation(yrow[:, b, half * 512:(half + 1) * 512], (acc, tp)[b][half][:, :], ACT.Copy)
                last.then_inc(y_copied, 1)

            def middle(n, b, slot, first=False):
                high_e(n + 1, slot, 0)
                silu(n, b)
                high_x(n + 1, 1 - b)
                high_e(n + 1, slot, 1)
                copy_y(n, b, first)
                high_e(n + 1, slot, 2)
                high_e(n + 1, slot, 3)

            def work(first, last):
                if first > 0:
                    act.wait_ge(tabs, 2)
                    for q in range(4):
                        high_e(first, (first - 1) % 4, q)
                high_x(first, 0)
                if first == 0:
                    for n in range(4):
                        middle(n, n % 2, n + 1, n < 2)
                with act.Fori(4 if first == 0 else first, last - 7, 4) as i:
                    for j in range(4):
                        middle(i + j, j % 2, j)
                for n in range(last - 4, last - 1):
                    middle(n, n % 2, n % 4)
                silu(last - 1, 1)
                copy_y(last - 1, 1)

            work(0, PAIRS)
            act.wait_ge(flag_ready, 1)
            more = act.value_load(flag[0:1, 0:1], min_val=0, max_val=1)
            with act.If(more > 0):
                work(PAIRS, TOTAL)
            for i, t in enumerate(LAST_ORDER):
                n = rows_of(t)
                act.wait_ge(mixed, i + 1)
                nc.scalar.activation(hflat[0:n, 0:D], x[0:n, t, :], ACT.Square, scale=D ** -0.5,
                                     accum_out=stat[0:n, 24 + t:25 + t]).then_inc(sq3, 1)
                root(sq3, i + 1, stat[0:n, 24 + t:25 + t])

        @block.vector
        def _(dve):
            steps = {dv: 0, dv_more: 0}

            def step(ins, chain=dv):
                steps[chain] += 1
                ins.then_inc(chain, 1)
                dve.wait_ge(chain, steps[chain])

            V = nc.vector

            def low(unit, dst):
                n = TURN[unit]
                m = dst.shape[-1]
                dve.wait_ge(turn_high, turned_out(n)[1])
                src = tp[TURN_BANK[n]][:, 0:4 * m].rearrange("p (c m) -> p c m", c=4)
                V.scalar_tensor_tensor(out=dst[:, 1], in0=src, scalar=H_UP, in1=dst[:, 0],
                                       op0=ALU.mult, op1=ALU.subtract).then_inc(tp_free_d, 1)

            def cols(t):
                return slice(t * P, t * P + rows_of(t))

            def low_h(t):
                for c in range(2):
                    low(("h", 2 * t + c), hT[:, :, 4 * c:4 * c + 4, cols(t)])

            def split_low(n, i):
                dve.wait_ge(w_high, PIECES * n + i + 1)
                V.scalar_tensor_tensor(out=wg[:, n % 2, 1, 2 * i:2 * i + 2, :], in0=pieces(n)[i], scalar=W_UP,
                                       in1=wg[:, n % 2, 0, 2 * i:2 * i + 2, :],
                                       op0=ALU.mult, op1=ALU.subtract).then_inc(w_split, 1)

            dve.wait_ge(gain_in, 16)

            def norm(t):
                n = rows_of(t)
                dve.wait_ge(rooted, t + 1)
                step(V.reciprocal(stat[0:n, 5 + t:6 + t], stat[0:n, t:t + 1]))
                V.scalar_tensor_tensor(out=hbuf[0:n, t % 2, :], in0=x[0:n, t, :], scalar=stat[0:n, 5 + t:6 + t],
                                       in1=gain[0:n, :], op0=ALU.mult, op1=ALU.mult).then_inc(h_ready, 1)

            def rope(kind, t):
                u = UNIT[(kind, t)]
                n = rows_of(t)
                dst = kn[0:n, t] if kind == "k" else (qn[0:n, t % 2] if t < NT - 1 else qs[0:n])
                z = acc[u % 2][0:n, 0:W].rearrange("p (h n) -> p h n", h=HEADS)
                d3 = dst.rearrange("p (h n) -> p h n", h=HEADS)
                t3 = rtmp[0:n].rearrange("p (h n) -> p h n", h=HEADS)
                half = HD // 2

                def tb(table, a, b):
                    return table[0:n, t, a:b].unsqueeze(1).to_broadcast([n, HEADS, b - a])
                dve.wait_ge(acc_ready, u + 1)
                if kind == "q" and 2 <= t < NT - 1:
                    dve.wait_ge(tp_ready, TURN[("q", t - 2)] + 1)
                V.tensor_tensor(d3, z, tb(cos, 0, HD), ALU.mult)
                V.tensor_tensor(t3[:, :, 0:half], z[:, :, half:HD], tb(sin, 0, half), ALU.mult)
                V.tensor_tensor(t3[:, :, half:HD], z[:, :, 0:half], tb(sin, half, HD), ALU.mult).then_inc(free_d, 1)
                dve.wait_ge(free_d, evacuated(u)[1])
                V.tensor_tensor(dst, dst, rtmp[0:n], ALU.add).then_inc(q_ready if kind == "q" else k_ready, 1)
                dve.wait_ge(q_ready if kind == "q" else k_ready, t + 1)

            def sum_prod(b):
                dve.wait_ge(prods, b + 1)
                V.tensor_reduce(sT[:, :, b * HEADS:(b + 1) * HEADS],
                                prod[:, :, :].rearrange("p a (h n) -> p a h n", h=HEADS), AX, ALU.add).then_inc(sums, 1)

            norm(0)
            norm(1)
            low_h(0)
            split_low(0, 0)
            low_h(1)
            for i in range(1, PIECES):
                split_low(0, i)
            norm(2)
            norm(3)
            dve.wait_ge(rope_in, 32)
            rope("q", 0)
            low_h(2)
            norm(4)
            rope("q", 1)
            low_h(3)
            low_h(4)
            rope("q", 2)
            for i in range(PIECES):
                split_low(1, i)
            rope("q", 3)
            rope("q", 4)
            for t in range(NT):
                rope("k", t)
                if t < PIECES:
                    split_low(2, t)
                if t >= 2:
                    sum_prod(t - 2)
            pr = rtmp[0:NS]
            step(V.tensor_tensor(pr, qs[0:NS], kn[0:NS, 4], ALU.mult))
            V.tensor_reduce(stat[0:NS, 32:40], pr.rearrange("p (h n) -> p h n", h=HEADS), AX, ALU.add).then_inc(self_s, 1)

            def add_mask(n):
                i, h = TASKS[n]
                width = P * (i + 1)
                dve.wait_ge(s_ready, n + 1)
                if n >= 2:
                    dve.wait_ge(exp_done, n - 1)
                V.tensor_tensor_reduce(out=s_sb[:, n % 2, 0:width], in0=sbk[n % 2][:, 0:width],
                                       in1=mask[:, (3 - i) * P:4 * P], scale=-SCALE, scalar=3.0e38,
                                       op0=ALU.add, op1=ALU.min, accum_out=negm[:, n:n + 1]).then_inc(masked_s, 1)

            def scale_o(n):
                i, h = TASKS[n]
                dve.wait_ge(exp_done, n + 1)
                step(V.reciprocal(den[:, n:n + 1], den[:, n:n + 1]))
                dve.wait_ge(pv_done, n + 1)
                V.tensor_scalar(attn[:, i, h * HD:(h + 1) * HD], ovb[:, 0:HD], den[:, n:n + 1], None,
                                ALU.mult).then_inc(o_done, 1)

            def va(t):
                n = rows_of(t)
                dst = vn[0:n, t]
                g3 = dst.rearrange("p (h n) -> p h n", h=HEADS)
                r8, y8 = stat[0:n, 48:56], stat[0:n, 56:64]
                left(dve, ("va", t))
                V.tensor_reduce(r8, sqt[0:n].rearrange("p (h n) -> p h n", h=HEADS), AX, ALU.add).then_inc(va_sum, 1)
                dve.wait_ge(va_root, t + 1)
                step(V.reciprocal(y8, r8))
                step(V.tensor_tensor(g3, g3, y8.unsqueeze(2).to_broadcast([n, HEADS, HD]), ALU.mult))
                V.tensor_tensor(dst, dst, gvb[0:n], ALU.mult).then_inc(va_ready, 1)

            dve.wait_ge(mask_in, 16)
            dve.wait_ge(gv_in, 16)
            dve.wait_ge(self_s, 1)
            add_mask(0)
            add_mask(1)
            for t in range(NT):
                va(t)
                if t < PIECES:
                    split_low(3, t)
                if t in (0, 1, 3):
                    sum_prod(3 + t - t // 3)

            def g8(v):
                return v.unsqueeze(2).to_broadcast([v.shape[0], HEADS, HD])

            def h8(v):
                return v.rearrange("p (h n) -> p h n", h=HEADS)

            R = NS * HEADS

            def sample_scores():
                dve.wait_ge(st_ready, 1)
                dve.wait_ge(va_ready, NT)
                step(V.tensor_scalar(sall[:, 0:NPAT * P], tp[0][0:R, 0:NPAT * P], SCALE, None, ALU.mult))
                step(V.tensor_tensor_reduce(out=stat[0:R, 40:48], in0=tp[0][0:R, 384:392], in1=hm, scale=SCALE,
                                            scalar=0.0, op0=ALU.mult, op1=ALU.add, accum_out=stat[0:R, 10:11]))
                step(V.tensor_scalar(sall[:, NPAT * P:], stat[0:R, 10:11], float(np.log(NPAT)), None, ALU.add))
                step(V.tensor_reduce(stat[0:R, 13:14], sall, AX, ALU.max))
                V.tensor_scalar(stat[0:R, 11:12], stat[0:R, 13:14], -1.0, None, ALU.mult).then_inc(sall_ready, 1)

            def sample_probs():
                dve.wait_ge(sexp, 1)
                step(V.reciprocal(stat[0:R, 14:15], stat[0:R, 12:13]))
                step(V.tensor_scalar(sall, sall, stat[0:R, 14:15], None, ALU.mult))
                dve.wait_ge(prods, NS)
                V.tensor_scalar(diag, ident[0:R, 0:R], sall[:, NPAT * P:], None, ALU.mult).then_inc(sp_ready, 1)

            def sample_columns():
                dve.wait_ge(stb_ready, 1)
                dve.wait_ge(ptm_zeroed, 1)
                src = tp[1][:, 0:NPAT * R].rearrange("p (a r) -> p a r", a=NPAT)
                diagonal = [(b, slice(b * HEADS, (b + 1) * HEADS)) for b in range(NS)]
                for b, cols_ in diagonal:
                    ins = V.tensor_scalar(ptm[:, :, b, 0, cols_], src[:, :, cols_], P_UP, None, ALU.mult)
                step(ins)
                for b, cols_ in diagonal:
                    V.scalar_tensor_tensor(out=ptm[:, :, b, 1, cols_], in0=src[:, :, cols_], scalar=P_UP,
                                           in1=ptm[:, :, b, 0, cols_], op0=ALU.mult, op1=ALU.subtract)
                V.tensor_scalar(own, tp[1][0:NS, NPAT * R:(NPAT + 1) * R], P_UP * V_UP, None, ALU.mult).then_inc(ptm_ready, 1)

            def mix(j):
                u = UNIT[("mix", j)]
                dve.wait_ge(acc_ready, u + 1)
                for g in range(2):
                    cols_ = slice((2 * j + g) * HD, (2 * j + g + 1) * HD)
                    src = acc[u % 2][:, g * 256:(g + 1) * 256].rearrange("p (t n) -> p t n", t=4)
                    last = V.scalar_tensor_tensor(out=uu[:, 0:4, cols_], in0=src,
                                                  scalar=bcol[:, 2 * j + g:2 * j + g + 1], in1=uu[:, 0:4, cols_],
                                                  op0=ALU.add, op1=ALU.mult)
                last.then_inc(free_d, 1)

            def low_head(kind, t):
                chunks = slice(4, 8) if kind == "att" else slice(0, 4)
                low((kind, t), hT[:, :, chunks, cols(t)])

            us, vs_ = uu[0:NS, 4], vn[0:NS, 4]
            tmp8 = sqt[0:NS]
            for n in range(len(TASKS)):
                if n + 2 < len(TASKS):
                    add_mask(n + 2)
                for kind, t in finished_in(n):
                    if kind == "mix":
                        if t == 0:
                            left(dve, ("u", NT - 2))
                        mix(t)
                scale_o(n)
                if n in SPLIT_AFTER:
                    split_low(*SPLIT_AFTER[n])
                for b in VALUE_AFTER.get(n, []):
                    dve.wait_ge(v_high, b + 1)
                    V.scalar_tensor_tensor(out=vsplit[:, 1], in0=vr[:, b % 2], scalar=V_UP, in1=vsplit[:, 0],
                                           op0=ALU.mult, op1=ALU.subtract).then_inc(v_split, 1)
                if n in TURN_AFTER:
                    low_head(*TURN_AFTER[n])
                if n in (1, 3):
                    sum_prod(NS - 2 + n // 2)
                if n == 5:
                    dve.wait_ge(consts_in, 128)
                    sample_scores()
                if n == 7:
                    sample_probs()
                if n == 9:
                    sample_columns()
                if n == 10:
                    step(V.tensor_tensor(h8(tmp8), h8(vs_), g8(w00[:, :]), ALU.mult))
                    step(V.tensor_tensor(h8(tmp8), h8(tmp8), g8(b0[:, :]), ALU.add))
            left(dve, ("u", NT - 1))
            V.tensor_tensor(us, us, tmp8, ALU.mult).then_inc(sgu_s_ready, 1)

            dve.wait_ge(sample_pv, NS)
            V.tensor_tensor(h8(masked), h8(tp[0][:, :]), g8(hm2), ALU.mult).then_inc(heads_masked, 1)
            low_head("att", NT - 2)
            dve.wait_ge(fin_high, 1)
            V.scalar_tensor_tensor(out=hT[:, 1, 4:8, cols(NT - 1)], in0=ovb[:, 0:4 * NS].rearrange("p (c b) -> p c b", c=4),
                                   scalar=H_UP * UNDO_PV, in1=hT[:, 0, 4:8, cols(NT - 1)],
                                   op0=ALU.mult, op1=ALU.subtract).then_inc(fin_copied, 1)
            low_head("sgu", NT - 1)
            for i in range(PIECES):
                split_low(6, i)

            def add_out(t, half):
                n, u = rows_of(t), UNIT[("out", 2 * t + half)]
                dve.wait_ge(acc_ready, u + 1)
                xh = x[0:n, t, half * 512:(half + 1) * 512]
                V.scalar_tensor_tensor(out=xh, in0=acc[u % 2][0:n, :], scalar=UNDO, in1=xh,
                                       op0=ALU.mult, op1=ALU.add).then_inc(free_d, 1)

            add_out(0, 0)
            add_out(1, 0)
            for t in range(NT):
                n = rows_of(t)
                if t >= 2:
                    add_out(t, 0)
                add_out(t, 1)
                left(dve, ("out", 2 * t + 1))
                if t == 0:
                    dve.wait_ge(gain_in, 32)
                dve.wait_ge(rooted, NT + t + 1)
                step(V.reciprocal(stat[0:n, 16 + t:17 + t], stat[0:n, 16 + t:17 + t]))
                V.scalar_tensor_tensor(
                    out=h2n[0:n, t % 2, :].rearrange("p (k q) -> p k q", k=KD),
                    in0=x[0:n, t, :].rearrange("p (q k) -> p k q", k=KD), scalar=stat[0:n, 16 + t:17 + t],
                    in1=gain[0:n, :].rearrange("p (q k) -> p k q", k=KD),
                    op0=ALU.mult, op1=ALU.mult).then_inc(h2_ready, 1)

            def over_t(v, m):
                return v.unsqueeze(2).to_broadcast([P, v.shape[1], m])

            def over_r(v, t=NT):
                return v.unsqueeze(1).to_broadcast([P, t, v.shape[1]])
            dve.wait_ge(pv_done, len(TASKS))
            step(V.memset(L[:, NT - 1, :], 0.0))
            dve.wait_ge(r_done, NT)
            lg = ptb[:, 0:NT * (NG + NE)].rearrange("p (t n) -> p t n", t=NT)
            V.tensor_tensor(L[:, 0:NT - 1, :], lg[:, 0:NT - 1, :], over_r(rbias[:, :], NT - 1), ALU.add)
            step(V.tensor_tensor(L[0:NS, NT - 1, :], lg[0:NS, NT - 1, :], rbias[0:NS, :], ALU.add))
            L4 = L[:, :, 0:NG]
            step(V.tensor_reduce(gmax, L4, AX, ALU.max))
            V.tensor_tensor(ge, L4, over_t(gmax, NG), ALU.subtract).then_inc(gexp_in, 1)
            step(V.tensor_tensor(gpick, L4, over_t(gmax, NG), ALU.is_ge))
            step(V.tensor_tensor(gpick, gpick, over_r(m100[:, 0:NG]), ALU.mult))
            step(V.tensor_reduce(gidx, gpick, AX, ALU.min))
            step(V.tensor_tensor(gpick, over_r(m100[:, 0:NG]), over_t(gidx, NG), ALU.is_equal))
            og = gpick.unsqueeze(3).to_broadcast([P, NT, NG, EPG])
            le4 = L[:, :, NG:NG + NE].rearrange("p t (g e) -> p t g e", g=NG)
            lm4 = lmul.rearrange("p t (g e) -> p t g e", g=NG)
            step(V.tensor_tensor(lm4, le4, og, ALU.mult))
            step(V.tensor_reduce(sel, lmul.rearrange("p t (g e) -> p t e g", g=NG), AX, ALU.add))
            for k, s_ in enumerate((sel, sel2)):
                ok = o12[:, k * NT:(k + 1) * NT, :]
                step(V.tensor_reduce(m12[:, k, :], s_, AX, ALU.max))
                step(V.tensor_tensor(pickt, s_, over_t(m12[:, k, :], EPG), ALU.is_ge))
                step(V.tensor_tensor(pickt, pickt, over_r(m100), ALU.mult))
                step(V.tensor_reduce(i12[:, k, :], pickt, AX, ALU.min))
                step(V.tensor_tensor(ok, over_r(m100), over_t(i12[:, k, :], EPG), ALU.is_equal))
                if k == 0:
                    step(V.scalar_tensor_tensor(out=sel2, in0=ok, scalar=NEG, in1=sel, op0=ALU.mult, op1=ALU.add))
            V.tensor_tensor(ex, m12[:, 1, :], m12[:, 0, :], ALU.subtract).then_inc(eexp_in, 1)
            for k in range(2):
                ins = V.tensor_tensor(
                    O[:, k].rearrange("p t (g e) -> p t g e", g=NG), og,
                    o12[:, k * NT:(k + 1) * NT, :].unsqueeze(2).to_broadcast([P, NT, NG, EPG]), ALU.mult)
            step(ins)
            step(V.tensor_tensor(M, O[:, 0], O[:, 1], ALU.add))
            V.tensor_scalar(M[:, NT - 1, :], M[:, NT - 1, :], in_samples, None, ALU.mult).then_inc(picks, 1)
            dve.wait_ge(gexp, 1)
            step(V.tensor_reduce(gsum, ge, AX, ALU.add))
            dve.wait_ge(eexp, 1)
            step(V.tensor_scalar(gp, ex, 1.0, None, ALU.add))
            step(V.tensor_tensor(gp, gp, gsum, ALU.mult))
            step(V.reciprocal(gates[:, 0, :], gp))
            step(V.tensor_tensor(gates[:, 1, :], gates[:, 0, :], ex, ALU.mult))
            dve.wait_ge(ranks, 1)
            pre = acc[0][:, 0:NT * NE].rearrange("p (t n) -> p t n", t=NT)
            step(V.tensor_tensor(X, pre, over_r(ecode), ALU.add))
            for k in range(2):
                ins = V.tensor_tensor(OX[:, k * NT:(k + 1) * NT, :], O[:, k], X, ALU.mult)
            step(ins)
            step(V.tensor_reduce(rk, OX, AX, ALU.add))
            xi, lo, hi, rd, pr_ = [v.bitcast(I32) for v in (rm, r2, r3, rk2, rk3)]
            step(V.tensor_copy(xi, rk))
            V.tensor_scalar(lo, xi, CAP - 1, None, ALU.bitwise_and)
            V.tensor_scalar(hi, xi, 4, CAP, ALU.logical_shift_right, ALU.bitwise_and)
            V.tensor_scalar(rd, xi, 6, 15, ALU.logical_shift_right, ALU.bitwise_and)
            step(V.tensor_scalar(pr_, xi, 11, None, ALU.logical_shift_right))
            V.tensor_tensor(r1, lo, hi, ALU.add)
            step(V.scalar_tensor_tensor(out=r4, in0=rd, scalar=float(PAIRS), in1=pr_, op0=ALU.mult, op1=ALU.add))
            dve.wait_ge(h2w[NT - 1], 16)
            dve.wait_ge(h2w[NT - 2], 16)
            V.tensor_tensor(onehot_p, over_r(iota[:, 0:P], 2 * NT), over_t(r1, P), ALU.is_equal)

            def tables(part, a, b, bank, chain):
                m = b - a
                vq = val_q[part]
                for v in range(2):
                    ins = V.tensor_tensor(vq[:, :, v, :], over_r(iota[:, a:b], 2 * NT), over_t(r4, m), ALU.is_equal)
                step(ins, chain)
                for v in range(2):
                    ins = V.tensor_tensor(vq[:, :, v, :], vq[:, :, v, :],
                                          val[:, :, v:v + 1].to_broadcast([P, 2 * NT, m]), ALU.mult)
                ins.then_inc(onehots, 1)
                dve.wait_ge(tabs, part + 1)
                src = bank[:, 0:2 * m].rearrange("p (v n) -> p v n", v=2)
                tt = tabtmp[:, 0:2 * m].rearrange("p (v n) -> p v n", v=2)
                step(V.tensor_scalar(tt, src, 0.0, FAR, ALU.is_equal, ALU.mult), chain)
                dst = tab.rearrange("p (v n) -> p v n", v=2)[:, :, a:b]
                V.scalar_tensor_tensor(out=dst, in0=src, scalar=-1.0, in1=tt, op0=ALU.add, op1=ALU.add).then_inc(tab_ready, 1)

            tables(0, 0, PAIRS, tp[0], dv)
            dve.wait_ge(cnt_ready, 1)
            step(V.tensor_reduce(rk[:, 0:1], acc[1][:, 256:256 + NE], AX, ALU.max))
            V.tensor_scalar(flag[:, :], rk[:, 0:1], float(CAP), None, ALU.is_gt).then_inc(flag_ready, 1)

            def low_e(n, slot, q):
                dve.wait_ge(e_high, n * 4 + (q + 1))
                V.scalar_tensor_tensor(out=esplit[q][:, 1], in0=places[slot][:, q // 2, q % 2, :].rearrange("p (k f) -> p k f", k=KD),
                                       scalar=W_UP, in1=esplit[q][:, 0], op0=ALU.mult, op1=ALU.subtract).then_inc(e_split, 1)

            def low_x(n, b):
                dve.wait_ge(x_high, n + 1)
                for c in range(2):
                    last = V.scalar_tensor_tensor(out=xsplit[:, b, 4 * c:4 * c + 4, 1, :],
                                                  in0=sbk[c][:, :].rearrange("p (k c) -> p k c", k=4), scalar=H_UP,
                                                  in1=xsplit[:, b, 4 * c:4 * c + 4, 0, :], op0=ALU.mult, op1=ALU.subtract)
                last.then_inc(x_split, 1)

            def hidden(n, b):
                dve.wait_ge(gu_parts, n * 4 + 4)
                dve.wait_ge(silu_done, n + 1)
                V.scalar_tensor_tensor(out=hid[:, b], in0=ovb[:, 0:2 * CAP], scalar=UNDO, in1=sg[:, b],
                                       op0=ALU.mult, op1=ALU.mult).then_inc(hid_done, 1)

            def middle(n, b, slot):
                low_e(n + 1, slot, 0)
                hidden(n, b)
                low_x(n + 1, 1 - b)
                for q in range(1, 4):
                    low_e(n + 1, slot, q)

            def work(first, last):
                for q in range(4):
                    low_e(first, 0 if first == 0 else (first - 1) % 4, q)
                low_x(first, 0)
                if first == 0:
                    for n in range(4):
                        middle(n, n % 2, n + 1)
                with dve.Fori(4 if first == 0 else first, last - 7, 4) as i:
                    for j in range(4):
                        middle(i + j, j % 2, j)
                for n in range(last - 4, last - 1):
                    middle(n, n % 2, n % 4)
                hidden(last - 1, 1)

            work(0, PAIRS)
            more = dve.value_load(flag[0:1, 0:1], min_val=0, max_val=1)
            with dve.If(more > 0):
                dve.wait_ge(gu_parts, 4 * PAIRS)
                tables(1, PAIRS, TOTAL, tp[1], dv_more)
                work(PAIRS, TOTAL)
            rows = big[:, 0:2 * NT * D].rearrange("p (t k n) -> p t k n", t=NT, k=2)
            dve.wait_ge(gain_in, 48)

            def add_rows(t):
                n = rows_of(t)
                xt = x[0:n, t, :]
                dve.wait_ge(rows_in[t], 32)
                step(V.scalar_tensor_tensor(out=xt, in0=rows[0:n, t, 0], scalar=gates[0:n, 0, t:t + 1], in1=xt,
                                            op0=ALU.mult, op1=ALU.add))
                V.scalar_tensor_tensor(out=xt, in0=rows[0:n, t, 1], scalar=gates[0:n, 1, t:t + 1], in1=xt,
                                       op0=ALU.mult, op1=ALU.add).then_inc(mixed, 1)

            def final_norm(i, t):
                n = rows_of(t)
                xt = x[0:n, t, :]
                dve.wait_ge(mixed, i + 1)
                dve.wait_ge(rooted, 2 * NT + i + 1)
                step(V.reciprocal(stat[0:n, 24 + t:25 + t], stat[0:n, 24 + t:25 + t]))
                V.scalar_tensor_tensor(out=xt, in0=xt, scalar=stat[0:n, 24 + t:25 + t], in1=gain[0:n, :],
                                       op0=ALU.mult, op1=ALU.mult).then_inc(y_ready, 1)

            add_rows(LAST_ORDER[0])
            for i in range(1, NT):
                add_rows(LAST_ORDER[i])
                final_norm(i - 1, LAST_ORDER[i - 1])
            final_norm(NT - 1, LAST_ORDER[NT - 1])

        @block.tensor
        def _(pe):
            T = nc.tensor

            def turns(unit, parts):
                n = TURN[unit]
                bank = TURN_BANK[n]
                if bank in TURN_BANK[:n]:
                    before = n - 1 - TURN_BANK[:n][::-1].index(bank)
                    wait_turned_out(pe, TURNS[before])
                m = parts[0].shape[0]
                for c, src in enumerate(parts):
                    ins = T.transpose(tp[bank][:, c * m:(c + 1) * m], src, ident[0:m, 0:m])
                ins.then_inc(tp_ready, 1)

            def quarter(rows, base=0):
                return [rows[:, base + c * P:base + (c + 1) * P] for c in range(4)]

            pe.wait_ge(ident_in, 16)

            def turn_h(t):
                pe.wait_ge(h_ready, t + 1)
                for c in range(2):
                    turns(("h", 2 * t + c), quarter(hbuf[0:rows_of(t), t % 2, :], c * 512))

            def project(unit):
                kind, t = unit
                wait_turned_out(pe, ("h", 2 * t + 1))
                free_wait(pe, UNIT[unit])
                for k in range(KD):
                    if k % 2 == 0:
                        pe.wait_ge(w_split, PIECES * W_ORDER.index(kind) + k // 2 + 1)
                    part_of(unit, k)

            def three_passes(out, tokens, k, place, columns):
                for high_low, part in ((0, 0), (0, 1), (1, 0)):
                    ins = T.matmul(out, hT[:, high_low, k, tokens], wg[:, place, part, k, columns],
                                   start=k == 0 and high_low + part == 0, stop=k == KD - 1 and high_low == 1)
                return ins

            def part_of(unit, k):
                kind, t = unit
                u, n = UNIT[unit], rows_of(t)
                ins = three_passes(acc[u % 2][0:n, 0:W], slice(t * P, t * P + n), k, W_ORDER.index(kind) % 2, slice(0, W))
                if k == KD - 1:
                    ins.then_inc(acc_ready, 1)

            def turn_qk(kind, t):
                pe.wait_ge(q_ready if kind == "q" else k_ready, t + 1)
                turns((kind, t), quarter(qn[:, t % 2] if kind == "q" else kn[:, t]))

            turn_h(0)
            turn_h(1)
            for t in range(NT):
                project(("q", t))
                if t + 2 < NT:
                    turn_h(t + 2)
                if t >= 2:
                    turn_qk("q", t - 2)
            project(("k", 0))
            turn_qk("q", NT - 2)
            for t in range(1, NT):
                project(("k", t))
                turn_qk("k", t - 1)
            def scores(n):
                i, h = TASKS[n]
                if n == 0:
                    wait_turned_out(pe, ("k", NT - 2))
                if n >= 2:
                    pe.wait_ge(masked_s, n - 1)
                r = slice(64 * (h % 2), 64 * (h % 2) + 64)
                T.matmul(sbk[n % 2][:, 0:P * (i + 1)], qT[r, h // 2, i * P:(i + 1) * P],
                         kT[r, h // 2, 0:P * (i + 1)], start=True, stop=True).then_inc(s_ready, 1)

            def turn_p(n):
                pe.wait_ge(exp_done, n + 1)
                if n >= 1:
                    pe.wait_ge(pt_copied, n)
                for j in range(TASKS[n][0] + 1):
                    ins = T.transpose(ptb[:, j * P:(j + 1) * P], p_sb[:, n % 2, j * P:(j + 1) * P], ident[:, :])
                ins.then_inc(p_turned, 1)

            def pv(n):
                i, h = TASKS[n]
                pe.wait_ge(pt_copied, n + 1)
                if h == 0:
                    left(pe, ("v", i))
                if n >= 1:
                    pe.wait_ge(o_done, n)
                for j in range(i + 1):
                    ins = T.matmul(ovb[:, 0:HD], pt_sb[:, n % 2, j * P:(j + 1) * P],
                                   vv[:, j, h * HD:(h + 1) * HD], start=j == 0, stop=j == i)
                ins.then_inc(pv_done, 1)

            R = NS * HEADS

            def turn_scores():
                pe.wait_ge(sums, NS)
                pe.wait_ge(self_s, 1)
                pe.wait_ge(consts_in, 128)
                for p_ in range(NPAT):
                    T.transpose(tp[0][0:R, p_ * P:(p_ + 1) * P], sT[:, p_, :], ident[:, :])
                T.matmul(tp[0][0:R, 384:392], bindT, stat[0:NS, 32:40], start=True, stop=True).then_inc(st_ready, 1)

            def turn_probs():
                pe.wait_ge(sp_ready, 1)
                for p_ in range(NPAT):
                    T.transpose(tp[1][:, p_ * R:(p_ + 1) * R], sall[:, p_ * P:(p_ + 1) * P], ident[0:R, 0:R])
                T.matmul(tp[1][0:NS, NPAT * R:(NPAT + 1) * R], bind, diag, start=True, stop=True).then_inc(stb_ready, 1)

            def sample_values(b, p_):
                if p_ == 0:
                    pe.wait_ge(v_split, b + 1)
                    if b == 0:
                        pe.wait_ge(ptm_ready, 1)
                        left(pe, ("v", NT - 1))
                first, last = b + p_ == 0, b == NS - 1 and p_ == NPAT - 1
                if not last:
                    T.matmul(tp[0][:, :], ptm[:, p_, b, :, :], vsplit[:, 0, p_, :], start=first, stop=False)
                ins = T.matmul(tp[0][0:R, :], ptm[:, p_, b, 0, :], vsplit[:, 1, p_, :], start=False, stop=False)
                if last:
                    T.matmul(tp[0][0:R, :], own, vv[0:NS, NT - 1, :], start=False, stop=False)
                    ins = T.matmul(tp[0][:, :], ptm[:, p_, b, :, :], vsplit[:, 0, p_, :], start=False, stop=True)
                if p_ == NPAT - 1:
                    ins.then_inc(sample_pv, 1)

            def mix(j):
                u = UNIT[("mix", j)]
                free_wait(pe, u)
                if j == 0:
                    pe.wait_ge(wt_mask, 1)
                    pe.wait_ge(va_ready, NT)
                for g in range(2):
                    ins = T.matmul(acc[u % 2][:, g * 256:(g + 1) * 256], wt[:, 2 * j + g, :],
                                   vn[:, 0:4, (2 * j + g) * HD:(2 * j + g + 1) * HD], start=True, stop=True)
                ins.then_inc(acc_ready, 1)

            def fill(kind, t, part):
                if kind == "pv":
                    sample_values(t, part)
                    return
                if kind == "mix":
                    mix(t)
                    return
                if part == 0:
                    free_wait(pe, UNIT[(kind, t)])
                    pe.wait_ge(w_split, PIECES * (W_ORDER.index(kind) + 1))
                part_of((kind, t), part)

            def turn_head(kind, t):
                if kind == "att":
                    pe.wait_ge(o_done, HEADS * (t + 1))
                else:
                    left(pe, ("mix", 3))
                turns((kind, t), quarter((attn if kind == "att" else uu)[:, t]))

            scores(0)
            scores(1)
            for t in range(NT):
                project(("va", t))
            project(("v", 0))
            for n in range(len(TASKS)):
                turn_p(n)
                if n + 2 < len(TASKS):
                    scores(n + 2)
                for piece in fill_of(n):
                    fill(*piece)
                pv(n)
                if n in TURN_AFTER:
                    turn_head(*TURN_AFTER[n])
                if n == 5:
                    turn_scores()
                if n == 8:
                    turn_probs()
            def router(t):
                n = rows_of(t)
                wait_turned_out(pe, ("h2", 2 * t + 1))
                for k in range(KD):
                    ins = T.matmul(ptb[0:n, t * 36:(t + 1) * 36], h2T[:, k, 0:n], wr[:, k, :],
                                   start=k == 0, stop=k == KD - 1)
                ins.then_inc(r_done, 1)

            def h2_turns(t):
                pe.wait_ge(h2_ready, t + 1)
                for c in range(2):
                    turns(("h2", 2 * t + c), quarter(h2n[0:rows_of(t), t % 2, :], c * 512))


            def project_out(t, half):
                n = rows_of(t)
                u = UNIT[("out", 2 * t + half)]
                free_wait(pe, u)
                pe.wait_ge(w_split, PIECES * (6 + half))
                wait_turned_out(pe, ("sgu", t))
                if t == NT - 1:
                    pe.wait_ge(fin_copied, 1)
                else:
                    wait_turned_out(pe, ("att", t))
                for k in range(KD):
                    ins = three_passes(acc[u % 2][0:n, :], slice(t * P, t * P + n), k, (5 + half) % 2, slice(0, 512))
                ins.then_inc(acc_ready, 1)

            project_out(0, 0)
            turn_head("att", NT - 2)
            pe.wait_ge(heads_masked, 1)
            for c in range(4):
                ins = T.matmul(ovb[:, c * NS:(c + 1) * NS], masked[:, c * P:(c + 1) * P], bind2, start=True, stop=True)
            ins.then_inc(fin_ready, 1)
            pe.wait_ge(sgu_s_ready, 1)
            turns(("sgu", NT - 1), quarter(uu[0:NS, 4]))
            project_out(1, 0)
            project_out(0, 1)
            project_out(1, 1)
            h2_turns(0)
            for t in range(2, NT):
                project_out(t, 0)
                router(t - 2)
                project_out(t, 1)
                h2_turns(t - 1)
            router(NT - 2)
            h2_turns(NT - 1)
            router(NT - 1)
            pe.wait_ge(picks, 1)
            left(pe, ("out", 2 * NT - 1))
            ins = T.matmul(acc[0][:, 0:NT * NE], ltri[:, :], M[:, :, :], start=True, stop=False)
            for t in range(NT - 1):
                later = NT - 1 - t
                ins = T.matmul(acc[0][:, (t + 1) * NE:NT * NE], ones[:, :],
                               M[:, t:t + 1, :].to_broadcast([P, later, NE]), start=False, stop=t == NT - 2)
            ins.then_inc(ranks, 1)

            def table_sums(part, a, b):
                m = b - a
                pe.wait_ge(onehots, part + 1)
                for kt in range(2 * NT):
                    n = rows_of(kt % NT)
                    ins = T.matmul(tp[part][:, 0:2 * m], onehot_p[0:n, kt, :], val_q[part][0:n, kt, :, :],
                                   start=kt == 0, stop=kt == 2 * NT - 1)
                ins.then_inc(tabs, 1)

            for t in range(NT):
                ins = T.matmul(acc[1][:, 256:256 + NE], ones[:, :], M[:, t, :], start=t == 0, stop=t == NT - 1)
            ins.then_inc(cnt_ready, 1)
            wait_turned_out(pe, ("h2", 2 * NT - 1))
            table_sums(0, 0, PAIRS)

            def turn_x(n, b):
                pe.wait_ge(x_landed[b], gathered(n, b))
                for k in range(KD):
                    ins = T.transpose(sbk[k // 4][:, (k % 4) * P:(k % 4 + 1) * P], xg[:, b, k * P:(k + 1) * P], ident[:, :])
                ins.then_inc(turned, 1)

            def gate_up(n, b):
                pe.wait_ge(x_split, n + 1)
                for q in range(4):
                    pe.wait_ge(e_split, n * 4 + (q + 1))
                    e = q % 2
                    for k in range(KD):
                        for part, high_low in ((0, 0), (0, 1), (1, 0)):
                            ins = T.matmul((ptb, ovb)[q // 2][:, e * CAP:(e + 1) * CAP], esplit[q][:, part, k, :],
                                           xsplit[:, b, k, high_low, e * CAP:(e + 1) * CAP],
                                           start=k + part + high_low == 0, stop=k == KD - 1 and part == 1)
                    ins.then_inc(gu_parts, 1)

            def down(n, j, b, first=False):
                pe.wait_ge(hid_done, n + 1)
                pe.wait_ge(down_in[j], weights(n, j))
                if not first:
                    pe.wait_ge(y_copied, n - 1)
                for e in range(2):
                    for half in range(2):
                        ins = T.matmul((acc, tp)[b][half][e * CAP:(e + 1) * CAP, :], hid[:, b, e * CAP:(e + 1) * CAP],
                                       places[j][:, 2, e, half * 512:(half + 1) * 512], start=True, stop=True)
                ins.then_inc(down_done, 1)

            def work(first, last):
                turn_x(first, 0)
                start = first
                if first == 0:
                    start = 5
                    for n in range(start):
                        gate_up(n, n % 2)
                        turn_x(n + 1, (n + 1) % 2)
                        if n == 0:
                            pe.wait_ge(flag_ready, 1)
                            pe.wait_ge(tab_ready, 1)
                        down(n, n, n % 2, n < 2)
                rest = (last - start - 1) % 4 + 1
                with pe.Fori(start, last - rest - 3, 4) as i:
                    for j in range(4):
                        slot, b = (start + j - 1) % 4, (start + j) % 2
                        gate_up(i + j, b)
                        turn_x(i + (j + 1), 1 - b)
                        down(i + j, slot, b)
                for n in range(last - rest, last):
                    slot, b = (n - 1) % 4, n % 2
                    gate_up(n, b)
                    if n + 1 < last:
                        turn_x(n + 1, 1 - b)
                    down(n, slot, b)

            work(0, PAIRS)
            more = pe.value_load(flag[0:1, 0:1], min_val=0, max_val=1)
            with pe.If(more > 0):
                pe.wait_ge(y_copied, PAIRS)
                table_sums(1, PAIRS, TOTAL)
                pe.wait_ge(tab_ready, 2)
                work(PAIRS, TOTAL)


def scattered(n, b):
    return (n - b) * 8


def gathered(n, b):
    return (n - b) * 8 + 16


def weights(n, j):
    if isinstance(n, int) and n < 5:
        return 16
    return (n - (j + 1)) * 4 + 16


def kernel(**inputs):
    import concourse.bacc as bacc
    from concourse.bass_utils import run_bass_kernel_spmd

    a = {k: np.asarray(v) for k, v in inputs.items()}
    sgu_w = a["sgu_w"][0]
    feeds = {
        "x_prompt": a["x_prompt"], "x_sample": a["x_sample"],
        "cache_win_k": a["cache_win_k"], "cache_win_v": a["cache_win_v"],
        "ln1_g": a["ln1_g"].reshape(-1), "w_in": a["w_in"],
        "sgu_norm_g": a["sgu_norm_g"].reshape(-1),
        "sgu_wt": sgu_w.transpose(2, 0, 1), "sgu_w00": sgu_w[:, 0, 0],
        "sgu_bt": a["sgu_b"][0].T, "sgu_b0": a["sgu_b"][0, :, 0],
        "w_out": a["w_out"], "ln2_g": a["ln2_g"].reshape(-1),
        "w_router": np.concatenate([a["w_router_group"][0], a["w_router_expert"][0]], 1).reshape(P, KD, NG + NE),
        "b_router": np.concatenate([a["b_router_group"][0], a["b_router_expert"][0]]),
        "w_gate": a["w_gate"], "w_up": a["w_up"], "w_down": a["w_down"], "lnf_g": a["lnf_g"],
        "const": constants(),
    }
    outs = [("y_prompt", (1, SEQ, D)), ("y_sample", (NS, 1, D)),
            ("k_prompt", (1, 1, SEQ, HEADS, HD)), ("v_prompt", (1, 1, SEQ, HEADS, HD)),
            ("k_sample", (1, NS, 1, HEADS, HD)), ("v_sample", (1, NS, 1, HEADS, HD)),
            ("sgu_v_sample", (1, NS, 1, HEADS, HD))]
    nc = bacc.Bacc("TRN2", target_bir_lowering=False, num_devices=1)
    arrays, args = {}, []
    for name, v in feeds.items():
        v = np.ascontiguousarray(v)
        arrays["in_" + name] = v
        args.append(nc.dram_tensor("in_" + name, v.shape, mybir.dt.from_np(v.dtype), kind="ExternalInput").ap())
    for name, shape in outs:
        args.append(nc.dram_tensor("out_" + name, shape, F32, kind="ExternalOutput").ap())
    build(nc, *args)
    r = run_bass_kernel_spmd(nc, [arrays], core_ids=[0])
    return tuple(r.results[0]["out_" + name] for name, _ in outs)
```
